# Optimizing a Trainium2 kernel written in Bass

```python
import math
import jax, jax.numpy as jnp
from jax import lax
import numpy as np

D_MODEL = 1024
BATCH = 1
SEQ = 128
DEPTH = 1
DEC_BATCH = 1
DEC_SEQ = 1024
PAST_LEN = 128

GRID_W = 64
FOURIER_GROUPS = 4
FOURIER_WIDTH = D_MODEL // 4
FOURIER_GROUP_DIM = FOURIER_WIDTH // FOURIER_GROUPS
POOL_WINDOWS = (2, 4, 8, 16)
POOL_WIDTH = D_MODEL // 4
POOL_GROUP_DIM = POOL_WIDTH // len(POOL_WINDOWS)
MLSTM_HEADS = 4
MLSTM_WIDTH = D_MODEL // 2
MLSTM_HEAD_DIM = MLSTM_WIDTH // MLSTM_HEADS
MLSTM_CHUNK = 64
N_DIR = 2
N_BRANCH = 3
N_GATE_COLS = N_DIR * 2 * MLSTM_HEADS
D_FF = -(-8 * D_MODEL // (3 * 256)) * 256
IN_WIDTHS = (FOURIER_WIDTH, POOL_WIDTH, MLSTM_WIDTH, MLSTM_WIDTH, MLSTM_WIDTH, MLSTM_WIDTH, N_GATE_COLS, N_BRANCH * D_MODEL)
IN_SPLITS = tuple(sum(IN_WIDTHS[:i + 1]) for i in range(len(IN_WIDTHS) - 1))
D_IN = sum(IN_WIDTHS)
RMS_EPS = 1e-6
POS_BASE = 10000.0

kernel_name = 'hybrid_fourier_pool_mlstm_flow_step'

def rms_norm(x, g):
    xf = x.astype(jnp.float32)
    y = xf * lax.rsqrt(jnp.mean(xf * xf, axis=-1, keepdims=True) + RMS_EPS)
    return (y * g.astype(jnp.float32)).astype(x.dtype)

def grid_pos_embed(rows, dtype):
    quarter = D_MODEL // 4
    omega = 1.0 / (POS_BASE ** (jnp.arange(quarter, dtype=jnp.float32) / quarter))
    t = jnp.arange(rows * GRID_W)
    r = (t // GRID_W).astype(jnp.float32)
    col = (t % GRID_W).astype(jnp.float32)
    ar = r[:, None] * omega[None, :]
    ac = col[:, None] * omega[None, :]
    return jnp.concatenate([jnp.sin(ar), jnp.cos(ar), jnp.sin(ac), jnp.cos(ac)], axis=-1).astype(dtype)

def fourier_mix(u):
    B, L, _ = u.shape
    ug = u.astype(jnp.float32).reshape(B, L, FOURIER_GROUPS, FOURIER_GROUP_DIM)
    y = jnp.fft.fftn(ug, axes=(1, 3), norm='ortho').real
    return y.reshape(B, L, FOURIER_WIDTH).astype(u.dtype)

def pool_mix(u, rows, w_pool_l, pool_scale_l):
    B, L, _ = u.shape
    W = L // rows
    ur = u.astype(jnp.float32).reshape(B, rows, W, len(POOL_WINDOWS), POOL_GROUP_DIM)
    cs = jnp.concatenate([jnp.zeros_like(ur[:, :, :1]), jnp.cumsum(ur, axis=2)], axis=2)
    pos = jnp.arange(W)
    outs = []
    for g, w in enumerate(POOL_WINDOWS):
        left = w // 2
        right = w - 1 - left
        lo = jnp.clip(pos - left, 0, W - 1)
        hi = jnp.clip(pos + right, 0, W - 1)
        cnt = (hi - lo + 1).astype(jnp.float32)
        csg = cs[:, :, :, g]
        s = jnp.take(csg, hi + 1, axis=2) - jnp.take(csg, lo, axis=2)
        outs.append(s / cnt[:, None] - ur[:, :, :, g])
    p = jnp.stack(outs, axis=3).astype(u.dtype)
    p = jnp.einsum('brwgc,gcd->brwgd', p, w_pool_l)
    return p.reshape(B, L, POOL_WIDTH) * pool_scale_l

def mlstm_dir(q, k, v, ig, lf, C0, n0, m0):
    B, H, L, D = q.shape
    nc = L // MLSTM_CHUNK

    def to_chunks(a):
        a = a.reshape((B, H, nc, MLSTM_CHUNK) + a.shape[3:])
        return jnp.moveaxis(a, 2, 0)

    lower = jnp.tril(jnp.ones((MLSTM_CHUNK, MLSTM_CHUNK), dtype=bool))

    def step(carry, xs):
        C, n, m = carry
        qc, kc, vc, ic, fc = xs
        b = jnp.cumsum(fc, axis=-1)
        state_log = b + m[..., None]
        log_d = jnp.where(lower, b[..., :, None] - b[..., None, :] + ic[..., None, :], -jnp.inf)
        m_t = jnp.maximum(state_log, jnp.max(log_d, axis=-1))
        d = jnp.exp(log_d - m_t[..., None])
        sdec = jnp.exp(state_log - m_t)
        s = jnp.einsum('bhtd,bhsd->bhts', qc, kc) * d
        num = sdec[..., None] * jnp.einsum('bhtd,bhde->bhte', qc, C) + jnp.einsum('bhts,bhse->bhte', s, vc)
        den = sdec * jnp.einsum('bhtd,bhd->bht', qc, n) + jnp.sum(s, axis=-1)
        h = num / jnp.maximum(jnp.abs(den), jnp.exp(-m_t))[..., None]
        b_last = b[..., -1]
        w_log = b_last[..., None] - b + ic
        m_new = jnp.maximum(b_last + m, jnp.max(w_log, axis=-1))
        w = jnp.exp(w_log - m_new[..., None])
        carry_dec = jnp.exp(b_last + m - m_new)
        C_new = carry_dec[..., None, None] * C + jnp.einsum('bhs,bhsd,bhse->bhde', w, kc, vc)
        n_new = carry_dec[..., None] * n + jnp.einsum('bhs,bhsd->bhd', w, kc)
        return (C_new, n_new, m_new), h

    xs = (to_chunks(q), to_chunks(k), to_chunks(v), to_chunks(ig), to_chunks(lf))
    init = (C0.astype(jnp.float32), n0.astype(jnp.float32), m0.astype(jnp.float32))
    (C, n, m), h = lax.scan(step, init, xs)
    h = jnp.moveaxis(h, 0, 2).reshape(B, H, L, D)
    return h, C, n, m

def parallel_mixer(h, rows, C0, n0, m0, w_in_l, b_gate_l, w_proj_f_l, w_pool_l, pool_scale_l, w_proj_p_l, w_proj_m_l, w_out_l):
    B, L, _ = h.shape
    z = h @ w_in_l
    u_f, u_p, q, k, v, o, g_pre, merge = jnp.split(z, IN_SPLITS, axis=-1)
    y_f = fourier_mix(u_f) @ w_proj_f_l
    y_p = pool_mix(u_p, rows, w_pool_l, pool_scale_l) @ w_proj_p_l
    def heads(a):
        return a.astype(jnp.float32).reshape(B, L, MLSTM_HEADS, MLSTM_HEAD_DIM).transpose(0, 2, 1, 3)
    qh = heads(q)
    kh = heads(k) * (MLSTM_HEAD_DIM ** -0.5)
    vh = heads(v)
    gp = (g_pre.astype(jnp.float32).reshape(B, L, N_DIR, 2, MLSTM_HEADS) + b_gate_l.astype(jnp.float32)).transpose(2, 3, 0, 4, 1)
    ig = gp[:, 0]
    lf = jax.nn.log_sigmoid(gp[:, 1])
    hf, Cf, nf, mf = mlstm_dir(qh, kh, vh, ig[0], lf[0], C0[:, 0], n0[:, 0], m0[:, 0])
    def rev(a):
        return jnp.flip(a, axis=2)
    hb, Cb, nb, mb = mlstm_dir(rev(qh), rev(kh), rev(vh), rev(ig[1]), rev(lf[1]), C0[:, 1], n0[:, 1], m0[:, 1])
    hm = (hf + rev(hb)).transpose(0, 2, 1, 3).reshape(B, L, MLSTM_WIDTH).astype(h.dtype)
    y_m = (jax.nn.sigmoid(o) * hm) @ w_proj_m_l
    g_f, g_p, g_m = jnp.split(jax.nn.sigmoid(merge), N_BRANCH, axis=-1)
    y = (g_f * y_f + g_p * y_p + g_m * y_m) @ w_out_l
    C_out = jnp.stack([Cf, Cb], axis=1).astype(h.dtype)
    n_out = jnp.stack([nf, nb], axis=1).astype(h.dtype)
    m_out = jnp.stack([mf, mb], axis=1).astype(h.dtype)
    return y, C_out, n_out, m_out

def block(x, mod, rows, C0, n0, m0, norm_g_l, w_in_l, b_gate_l, w_proj_f_l, w_pool_l, pool_scale_l, w_proj_p_l, w_proj_m_l, w_out_l, w_ffn_in_l, w_ffn_out_l):
    shift1, scale1, gate1, shift2, scale2, gate2 = jnp.split(mod, 6, axis=-1)
    h = rms_norm(x, norm_g_l[0]) * (1 + scale1) + shift1
    y, C_out, n_out, m_out = parallel_mixer(h, rows, C0, n0, m0, w_in_l, b_gate_l, w_proj_f_l, w_pool_l, pool_scale_l, w_proj_p_l, w_proj_m_l, w_out_l)
    x = x + gate1 * rms_norm(y, norm_g_l[1])
    h = rms_norm(x, norm_g_l[2]) * (1 + scale2) + shift2
    a, b = jnp.split(h @ w_ffn_in_l, 2, axis=-1)
    x = x + gate2 * rms_norm((jax.nn.silu(a) * b) @ w_ffn_out_l, norm_g_l[3])
    return x, C_out, n_out, m_out

def setup_inputs(seed: int = 0) -> dict:
    key = jax.random.key(seed)
    ks = jax.random.split(key, 20)
    H, DH = MLSTM_HEADS, MLSTM_HEAD_DIM
    nrm = jax.random.normal
    gate_base = jnp.stack([jnp.zeros((H,), jnp.float32), jnp.linspace(3.0, 6.0, H, dtype=jnp.float32)])
    return {
        'x_prompt': nrm(ks[0], (BATCH, SEQ, D_MODEL), jnp.float32),
        'x_sample': nrm(ks[1], (DEC_BATCH, DEC_SEQ, D_MODEL), jnp.float32),
        'state_C': 0.3 * nrm(ks[2], (DEC_BATCH, DEPTH, N_DIR, H, DH, DH), jnp.float32),
        'state_n': 0.3 * nrm(ks[3], (DEC_BATCH, DEPTH, N_DIR, H, DH), jnp.float32),
        'state_m': nrm(ks[4], (DEC_BATCH, DEPTH, N_DIR, H), jnp.float32),
        'c': nrm(ks[5], (DEC_BATCH, D_MODEL), jnp.float32),
        'c_ctx': nrm(ks[6], (D_MODEL,), jnp.float32),
        'w_ada': 0.5 * D_MODEL ** -0.5 * nrm(ks[7], (DEPTH, D_MODEL, 6 * D_MODEL), jnp.float32),
        'b_ada': 0.02 * nrm(ks[8], (DEPTH, 6 * D_MODEL), jnp.float32),
        'norm_g': 1.0 + 0.05 * nrm(ks[9], (DEPTH, 4, D_MODEL), jnp.float32),
        'w_in': D_MODEL ** -0.5 * nrm(ks[10], (DEPTH, D_MODEL, D_IN), jnp.float32),
        'b_gate': gate_base[None, None] + 0.1 * nrm(ks[11], (DEPTH, N_DIR, 2, H), jnp.float32),
        'w_proj_f': FOURIER_WIDTH ** -0.5 * nrm(ks[12], (DEPTH, FOURIER_WIDTH, D_MODEL), jnp.float32),
        'w_pool': POOL_GROUP_DIM ** -0.5 * nrm(ks[13], (DEPTH, len(POOL_WINDOWS), POOL_GROUP_DIM, POOL_GROUP_DIM), jnp.float32),
        'pool_scale': 1.0 + 0.1 * nrm(ks[14], (DEPTH, POOL_WIDTH), jnp.float32),
        'w_proj_p': POOL_WIDTH ** -0.5 * nrm(ks[15], (DEPTH, POOL_WIDTH, D_MODEL), jnp.float32),
        'w_proj_m': MLSTM_WIDTH ** -0.5 * nrm(ks[16], (DEPTH, MLSTM_WIDTH, D_MODEL), jnp.float32),
        'w_out': D_MODEL ** -0.5 * nrm(ks[17], (DEPTH, D_MODEL, D_MODEL), jnp.float32),
        'w_ffn_in': D_MODEL ** -0.5 * nrm(ks[18], (DEPTH, D_MODEL, 2 * D_FF), jnp.float32),
        'w_ffn_out': D_FF ** -0.5 * nrm(ks[19], (DEPTH, D_FF, D_MODEL), jnp.float32),
    }

def reference(x_prompt, x_sample, state_C, state_n, state_m, c, c_ctx, w_ada, b_ada, norm_g, w_in, b_gate, w_proj_f, w_pool, pool_scale, w_proj_p, w_proj_m, w_out, w_ffn_in, w_ffn_out):
    def layer_params(i):
        return (norm_g[i], w_in[i], b_gate[i], w_proj_f[i], w_pool[i], pool_scale[i], w_proj_p[i], w_proj_m[i], w_out[i], w_ffn_in[i], w_ffn_out[i])

    Bp = x_prompt.shape[0]
    H, DH = MLSTM_HEADS, MLSTM_HEAD_DIM
    C_zero = jnp.zeros((Bp, N_DIR, H, DH, DH), jnp.float32)
    n_zero = jnp.zeros((Bp, N_DIR, H, DH), jnp.float32)
    m_zero = jnp.zeros((Bp, N_DIR, H), jnp.float32)
    xp = x_prompt
    Cs, ns, ms = [], [], []
    for i in range(DEPTH):
        mod_ctx = (jax.nn.silu(c_ctx) @ w_ada[i] + b_ada[i])[None, None, :]
        xp, C_i, n_i, m_i = block(xp, mod_ctx, 1, C_zero, n_zero, m_zero, *layer_params(i))
        Cs.append(C_i)
        ns.append(n_i)
        ms.append(m_i)
    new_state_C = jnp.stack(Cs, axis=1)
    new_state_n = jnp.stack(ns, axis=1)
    new_state_m = jnp.stack(ms, axis=1)

    rows = x_sample.shape[1] // GRID_W
    xs = x_sample + grid_pos_embed(rows, x_sample.dtype)[None]
    for i in range(DEPTH):
        mod_lat = (jax.nn.silu(c) @ w_ada[i] + b_ada[i])[:, None, :]
        xs, _, _, _ = block(xs, mod_lat, rows, state_C[:, i], state_n[:, i], state_m[:, i], *layer_params(i))

    return (xp, xs, new_state_C, new_state_n, new_state_m)


_drawn_inputs = setup_inputs


def setup_inputs(seed=0):
    import zlib

    import numpy as np

    out = dict(_drawn_inputs(seed))
    spreads = {}
    factors = {'pool_scale': 4.319, 'state_C': 2.851, 'state_m': 2.821}
    for name, (base, spread) in spreads.items():
        noise = np.random.default_rng([zlib.crc32(name.encode()), seed]).standard_normal(out[name].shape)
        drawn = base * np.exp(spread * noise) if base else spread * noise
        out[name] = __import__('jax').numpy.asarray(drawn.astype(out[name].dtype))
    for name, factor in factors.items():
        out[name] = (out[name] * factor).astype(out[name].dtype)
    return out
```

```python
from contextlib import ExitStack

import concourse.bass as bass
import numpy as np
from concourse import mybir

F32 = mybir.dt.float32
F32R = mybir.dt.float32r
ACT = mybir.ActivationFunctionType
ALU = mybir.AluOpType
AX = mybir.AxisListType

P = 128
D = 1024
KT = D // P
LAT, CTX = 1024, 128
T = LAT + CTX
NT = T // P
GW = 384
NG = T // GW
GRID_W = 64
FW = 256
GD = 64
MW = 512
H, DH = 4, 128
NGC = 16
DFF = 2816
FT = DFF // P
WINDOWS = (2, 4, 8, 16)
EPS = 1e-6
RAW, SPL = 4, 4
NEG = -1e30
NJ = NT * H
C1 = DH + 1

Z1_UNITS = (2 * FW + 3 * MW) // P
O_COL = 2 * FW + 3 * MW
GATE_COL = O_COL + MW
MERGE_COL = GATE_COL + NGC
Z2_UNITS = (MW + 3 * D) // P
U_Z1, U_ZG, U_Z2 = 0, Z1_UNITS, Z1_UNITS + 1
U_F = U_Z2 + Z2_UNITS
F_UNITS = 2 * (LAT // P) + 1
U_E = U_F + F_UNITS
E_UNITS = 2 * KT
U_FF = U_E + NG * E_UNITS
FO_K = (8, 7, 7)
FF_UNITS = 2 * FT + len(FO_K) * KT
U_END = U_FF + NG * FF_UNITS

V_C, V_CTX, V_BADA, V_NORM, V_PSC, V_ROWS = 0, 8, 16, 64, 96, 98

CB = {}
_at = 0
for _name, _w in (("rev", P), ("tri_f", P), ("tri_b", P), ("last", P), ("first", P), ("mask_f", P),
                  ("mask_b", P), ("pool", 8 * P), ("pos_r", 4 * 16), ("pos_c", 4 * 64), ("cb", 2 * P)):
    CB[_name] = slice(_at, _at + _w)
    _at += _w
CB_W = _at


def shape_constants():
    c = np.zeros((P, CB_W), np.float32)
    s, t = np.arange(P)[:, None], np.arange(P)[None, :]
    c[:, CB["rev"]] = (s + t == P - 1)
    c[:, CB["tri_f"]] = (s <= t)
    c[:, CB["tri_b"]] = (s >= t)
    c[P - 1, CB["last"]] = 1
    c[0, CB["first"]] = 1
    c[:, CB["mask_f"]] = np.where(s <= t, 0, NEG)
    c[:, CB["mask_b"]] = np.where(s >= t, 0, NEG)
    for kind, width in enumerate((GRID_W, CTX)):
        for g, w in enumerate(WINDOWS):
            m = np.zeros((P, P), np.float64)
            for x in range(P):
                row, pos = x // width * width, x % width
                lo, hi = max(pos - w // 2, 0), min(pos + w - 1 - w // 2, width - 1)
                m[row + lo:row + hi + 1, x] = 1.0 / (hi - lo + 1)
                m[x, x] -= 1.0
            c[:, CB["pool"].start + (kind * 4 + g) * P:][:, :P] = m
    quarter = D // 4
    omega = (np.float32(1.0) / np.float32(10000.0) ** (np.arange(quarter, dtype=np.float32) / np.float32(quarter)))
    for name, n in (("pos_r", 16), ("pos_c", 64)):
        arg = omega.astype(np.float32)[:, None] * np.arange(n, dtype=np.float32)[None, :]
        table = np.concatenate([np.sin(arg), np.cos(arg)]).astype(np.float32)
        c[:, CB[name]] = table.reshape(4, P, n).transpose(1, 0, 2).reshape(P, 4 * n)
    k = np.arange(GD)
    ang = 2 * np.pi * (k[:, None] * k[None, :] % GD) / GD
    for i, m in enumerate((np.cos(ang), -np.sin(ang))):
        for b in range(2):
            at = CB["cb"].start + i * P + b * GD
            c[b * GD:(b + 1) * GD, at:at + GD] = m
    dft = np.zeros((F_UNITS, P, D), np.float32)
    for n in (LAT, CTX):
        k = np.arange(n)
        ang = 2 * np.pi * (k[:, None] * k[None, :] % n) / n
        cs = np.stack([np.cos(ang), np.sin(ang)]) / np.sqrt(float(n) * GD)
        if n == LAT:
            dft[:-1] = cs.reshape(2 * LAT // P, P, LAT)
        else:
            dft[-1, :, :2 * CTX] = np.concatenate([cs[0], cs[1]], axis=1)
    base = np.concatenate([np.eye(P), np.ones((P, P))], axis=1).astype(np.float32)
    return base, c, dft


GD_ABS, GD_LF, GD_AL, GD_SCAN, GD_MCOPY, GD_MTOK = 3, 5, 9, 13, 15, 16
GD_G = GD_MTOK + 1 + 3 + 4 * (NT - 1) + 2 + 2 + 2
GD_LOGS = GD_G + 6
GD_END = GD_LOGS + 1


def build(nc, x_prompt, x_sample, state_C, state_n, state_m, vectors, w_ada, w_stream, b_gate, w_pool,
          k_base, k_cst, k_dft, y_prompt, y_sample, new_C, new_n, new_m):
    z_dram = nc.dram_tensor("z_scratch", (Z1_UNITS + Z2_UNITS, P, T), F32).ap()
    mix_dram = nc.dram_tensor("mix_scratch", (KT, P, T), F32).ap()
    kv_dram = nc.dram_tensor("kv_scratch", (NT, P, 2 * MW), F32).ap()
    g_dram = nc.dram_tensor("g_scratch", (2 * NT, H * P), F32).ap()
    h_dram = nc.dram_tensor("h_scratch", (2 * NT, P, MW), F32).ap()

    with ExitStack() as top:
        def sb(stack, name, shape, dt=F32):
            return stack.enter_context(nc.sbuf_tensor(name, shape, dt))

        def sem(name):
            return top.enter_context(nc.semaphore(name))

        bank = [top.enter_context(nc.psum_tensor(f"bank{i}", [P, 512], F32)) for i in range(8)]

        raw = sb(top, "raw", [P, RAW, D])
        w_hi = sb(top, "w_hi", [P, SPL, D], F32R)
        w_lo = sb(top, "w_lo", [P, SPL, D], F32R)
        xT = sb(top, "xT", [P, KT, T])
        base = sb(top, "base", [P, 2 * P])
        ident, ones = base[:, 0:P], base[:, P:2 * P]
        vec = sb(top, "vec", [P, V_ROWS])
        silu_c = sb(top, "silu_c", [P, KT, 2])
        mod = sb(top, "mod", [P, 48, 2])
        A1 = sb(top, "A1", [P, KT, 2])
        A2 = sb(top, "A2", [P, KT, 2])
        G1 = sb(top, "G1", [P, KT, 2])
        G2 = sb(top, "G2", [P, KT, 2])
        eps = sb(top, "eps", [P, 1])
        acc = sb(top, "acc", [P, GW])
        rstd = sb(top, "rstd", [P, GW])

        s1 = ExitStack()
        cst = sb(s1, "cst", [P, CB_W])
        K = {n: cst[:, s] for n, s in CB.items()}
        gz = sb(s1, "gz", [P, T])
        s1h = ExitStack()
        h_hi = sb(s1h, "h_hi", [P, KT, T], F32R)
        h_lo = sb(s1h, "h_lo", [P, KT, T], F32R)
        s1a = ExitStack()
        ada = sb(s1a, "ada", [P, 2, D])
        tmp1 = sb(s1a, "tmp1", [P, 4, GW])
        x_in = sb(s1a, "x_in", [P, 2, D])
        rows = sb(s1a, "rows", [V_ROWS, P])
        s1a.close()
        z_st = sb(s1h, "z_st", [P, 2, T])
        s1h.close()

        s2 = ExitStack()
        zt = sb(s2, "zt", [P, 2, 12, P])
        uf_hi = sb(s2, "uf_hi", [P, NT, FW], F32R)
        uf_lo = sb(s2, "uf_lo", [P, NT, FW], F32R)
        up = sb(s2, "up", [P, NT, FW])
        s2a = ExitStack()
        kv_st = sb(s2a, "kv_st", [P, 2, 2 * MW])
        s2a.close()
        ab_hi = sb(s2, "ab_hi", [P, 2, 2, T], F32R)
        ab_lo = sb(s2, "ab_lo", [P, 2, 2, T], F32R)
        cb_hi = sb(s2, "cb_hi", [P, 2, P], F32R)
        cb_lo = sb(s2, "cb_lo", [P, 2, P], F32R)
        m_st = sb(s2, "m_st", [P, 2, GW])
        pT = sb(s2, "pT", [P, 2, GW])
        wp = sb(s2, "wp", [P, 2, P])
        s2.close()
        s2 = ExitStack()
        q_sb = sb(s2, "q_sb", [P, 2, H, P])
        k_sb = sb(s2, "k_sb", [P, 2, H, P])
        kt_sb = sb(s2, "kt_sb", [P, 2, MW])
        v_sb = sb(s2, "v_sb", [P, 2, H, C1])
        g_sb = sb(s2, "g_sb", [P, 2, H, P])
        lw = sb(s2, "lw", [P, 2, H, P])
        ew = sb(s2, "ew", [P, 2, H, P])
        inter = sb(s2, "inter", [P, 2, H, C1])
        wv = sb(s2, "wv", [P, 2, H, C1])
        num = sb(s2, "num", [P, 2, H, C1])
        den = sb(s2, "den", [P, 2, H])
        sdec_now = sb(s2, "sdec_now", [P, 2, H])
        h_out = sb(s2, "h_out", [P, 2, H, DH])
        st_lat = sb(s2, "st_lat", [P, 2, H, C1])
        st_ctx = sb(s2, "st_ctx", [P, 2, H, C1])
        bg = sb(s2, "bg", [P, NGC])
        sm = sb(s2, "sm", [P, 2, H])
        gts = sb(s2, "gts", [P, NT, NGC])

        def gate(name):
            return sb(s2, name, [P, 2, NT, H])

        lf, absf, lse, cum, al, mtok, mprev, mnew, gneg, em, sdec, wst, carry, blast, mlast = (
            gate(n) for n in ("lf", "absf", "lse", "cum", "al", "mtok", "mprev", "mnew", "gneg", "em", "sdec",
                              "wst", "carry", "blast", "mlast"))
        mrev = sb(s2, "mrev", [P, NJ])
        rows_a = sb(s2, "rows_a", [NJ, 2, P])
        rows_m = sb(s2, "rows_m", [NJ, 2, P])
        g_rows = sb(s2, "g_rows", [2 * NJ, P])
        hf_sb = sb(s2, "hf_sb", [P, 2, 2, MW])
        o_sb = sb(s2, "o_sb", [P, 2, H, P])
        hs = sb(s2, "hs", [P, 2, MW])
        ho = sb(s2, "ho", [P, 2, H, P])
        s2.close()
        s1.close()

        s3 = ExitStack()
        y2 = sb(s3, "y2", [P, KT, GW])
        h2_hi = sb(s3, "h2_hi", [P, KT, GW], F32R)
        h2_lo = sb(s3, "h2_lo", [P, KT, GW], F32R)
        tmp3 = sb(s3, "tmp3", [P, 4, GW])
        s3a = ExitStack()
        mg = sb(s3a, "mg", [P, 2, 3, GW])
        mx_hi = sb(s3a, "mx_hi", [P, KT, GW], F32R)
        mx_lo = sb(s3a, "mx_lo", [P, KT, GW], F32R)
        mx_in = sb(s3a, "mx_in", [P, 2, GW])
        ya = sb(s3a, "ya", [P, 2, 3, GW])
        yy_hi = sb(s3a, "yy_hi", [P, KT, GW], F32R)
        yy_lo = sb(s3a, "yy_lo", [P, KT, GW], F32R)
        s3a.close()
        o_st = sb(s3, "o_st", [P, 2, 512])
        sa = sb(s3, "sa", [P, 2, GW])
        ff = sb(s3, "ff", [P, 2, GW])
        f_hi = sb(s3, "f_hi", [P, FT, GW], F32R)
        f_lo = sb(s3, "f_lo", [P, FT, GW], F32R)
        s3.close()

        s_raw = [sem(f"raw_landed{i}") for i in range(RAW)]
        s_whi, s_wlo, s_unit = sem("w_hi_ready"), sem("w_lo_ready"), sem("unit_multiplied")
        s_const, s_rows, s_vec, s_vecc, s_silu = (sem(n) for n in ("const_landed", "rows_landed", "vec_transposed",
                                                                   "vec_ready", "silu_ready"))
        s_set = sem("memsets_done")
        s_xin = [sem(f"x_landed{i}") for i in range(2)]
        s_xt, s_xev = sem("x_transposed"), sem("xT_ready")
        s_ada = [sem(f"ada_landed{i}") for i in range(2)]
        s_adam, s_modc, s_mod = sem("ada_multiplied"), sem("mod_chain"), sem("mod_ready")
        s_sq, s_accs, s_st, s_sd, s_rs = (sem(n) for n in ("square_ready", "square_summed", "mean_ready",
                                                           "root_ready", "rstd_ready"))
        s_nx, s_nf, s_nh, s_nl, s_app, s_xs = (
            sem(n) for n in ("norm_scaled", "norm_full", "norm_high", "norm_low", "residual_ready", "x_step"))
        s_zmm, s_zev = sem("z_multiplied"), sem("z_evacuated")
        s_zst = [sem(f"z_stored{i}") for i in range(2)]
        s_zt = [sem(f"zt_landed{i}") for i in range(2)]
        s_tmm, s_tact, s_tdve = sem("t_transposed"), sem("t_act"), sem("t_dve")
        s_kvst = [sem(f"kv_stored{i}") for i in range(2)]
        s_fmm, s_fhi, s_flo, s_cbh, s_cbl = (sem(n) for n in ("dft_multiplied", "dft_high", "dft_low", "cb_high",
                                                              "cb_low"))
        s_cmm, s_mev = sem("mix_multiplied"), sem("mix_evacuated")
        s_mst = [sem(f"mix_stored{i}") for i in range(2)]
        s_pmm, s_pa, s_pd, s_wp = sem("pooled"), sem("pool_act"), sem("pool_dve"), sem("w_pool_landed")
        s_wp0 = sem("w_pool_zeroed")
        s_gl, s_gp, s_gd, s_ga, s_gst = (sem(n) for n in ("gate_inputs_landed", "gate_pe", "gate_dve", "gate_act",
                                                          "g_rows_stored"))
        s_ld = [sem(f"chunk_landed{i}") for i in range(2)]
        s_st0 = sem("state_landed")
        s_qk, s_int, s_iev, s_t, s_e, s_p, s_wv, s_intra, s_kvm, s_num, s_den, s_hd, s_cup = (
            sem(n) for n in ("scores_ready", "inter_ready", "inter_evacuated", "logw_ready", "expw_ready",
                             "probs_ready", "wv_ready", "intra_ready", "kv_ready", "num_ready", "den_chain",
                             "h_ready", "state_updated"))
        s_sn = sem("decays_ready")
        s_hst = [sem(f"h_stored{i}") for i in range(2)]
        s_hl = [sem(f"h_landed{i}") for i in range(2)]
        s_hs, s_ht, s_ho = sem("h_summed"), sem("h_transposed"), sem("h_gated")
        s_host = [sem(f"hm_stored{i}") for i in range(2)]
        s_new = sem("new_state_stored")
        s_mx = [sem(f"mx_landed{i}") for i in range(2)]
        s_mxh, s_mxl = sem("mx_high"), sem("mx_low")
        s_mg = [sem(f"merge_landed{i}") for i in range(2)]
        s_ym, s_ya, s_yh, s_yl = (sem(n) for n in ("branches_gated", "y_summed", "y_high", "y_low"))
        s_e2e = sem("out_evacuated")
        s_sa, s_ff, s_fh, s_fl = (sem(n) for n in ("silu_a_ready", "f_ready", "f_high", "f_low"))
        s_foe = sem("ffn_out_evacuated")
        s_ot, s_oe = sem("out_transposed"), sem("out_staged")
        s_ost = [sem(f"out_stored{i}") for i in range(2)]

        ORDER = [("SQ", "h0"), ("ST", "h0"), ("HN", "h0"), ("SQ", "h1"), ("ST", "h1"), ("HN", "h1"), ("SQ", "h2"),
                 ("ST", "h2"), ("HN", "h2"), ("MIX", None),
                 ("MX", 0), ("E1", 0), ("MX", 1), ("E2", 0), ("SQ", "y0"), ("E1", 1), ("ST", "y0"), ("X", "y0"),
                 ("MX", 2), ("SQ", "x0"), ("E2", 1), ("ST", "x0"), ("HN", "x0"), ("SQ", "y1"), ("E1", 2),
                 ("ST", "y1"), ("X", "y1"), ("E2", 2), ("SQ", "y2"), ("FI", 0), ("ST", "y2"), ("X", "y2"),
                 ("SQ", "x1"), ("ST", "x1"), ("FO", 0), ("HN", "x1"), ("SQ", "o0"), ("FI", 1), ("ST", "o0"),
                 ("X", "o0"), ("OT", 0), ("SQ", "x2"), ("ST", "x2"), ("FO", 1), ("HN", "x2"), ("SQ", "o1"),
                 ("FI", 2), ("ST", "o1"), ("X", "o1"), ("OT", 1), ("FO", 2), ("SQ", "o2"), ("ST", "o2"),
                 ("X", "o2"), ("OT", 2)]
        number = {}
        tmp_at, uses = {}, 0
        for stage, which in ORDER:
            if stage in ("SQ", "ST", "HN", "X"):
                number[stage, which] = sum(1 for k in number if k[0] == stage)
                if stage in ("SQ", "HN"):
                    tmp_at[stage, which] = uses
                    uses += KT
        apply_order = [(s, w) for s, w in ORDER if s in ("HN", "X")]

        def wait_applied(eng, n):
            s, w = apply_order[n - 1]
            if s == "HN":
                eng.wait_ge(s_nl, KT * (number[s, w] + 1))
            else:
                eng.wait_ge(s_app, number[s, w] + 1)

        def wait_x(eng, which):
            eng.wait_ge(s_app, number["X", which] + 1)

        def wait_tmp(eng, m):
            for (stage, w), at in tmp_at.items():
                if at <= m - 4 < at + KT:
                    n = KT * number[stage, w] + m - 4 - at + 1
                    eng.wait_ge(s_accs if stage == "SQ" else s_nl, n)

        def halves(g):
            return [(0, GW, 0)] if g < NG - 1 else [(0, LAT - g * GW, 0), (LAT - g * GW, GW, 1)]

        def source(which):
            g = int(which[1])
            return y2[:, :, :] if which[0] in "yo" else xT[:, :, g * GW:(g + 1) * GW]

        def tmp_of(which):
            return tmp1 if which[0] == "h" else tmp3

        def wait_source(eng, which):
            kind, g = which[0], int(which[1])
            if kind == "h":
                eng.wait_ge(s_xev, 2 * min(3 * (g + 1), NT))
            elif kind == "y":
                eng.wait_ge(s_e2e, KT * (g + 1))
            elif kind == "o":
                eng.wait_ge(s_foe, KT * (g + 1))
            else:
                wait_x(eng, f"y{g}")

        def mm3(pe, out, a_hi, a_lo, b_hi, b_lo, start, stop):
            pe.matmul(out, a_hi, b_hi, start=start, stop=False)
            pe.matmul(out, a_hi, b_lo, start=False, stop=False)
            return pe.matmul(out, a_lo, b_hi, start=False, stop=stop)

        def b3(ap, n):
            return ap.unsqueeze(1).broadcast_to((ap.shape[0], n, ap.shape[1]))

        def last(ap, n):
            return ap.unsqueeze(len(ap.shape)).broadcast_to(tuple(ap.shape) + (n,))

        def ktile(k):
            return slice(k * P, (k + 1) * P)

        def e_unit(g, c):
            return U_E + E_UNITS * g + c

        def f_unit(g, c):
            return U_FF + FF_UNITS * g + c

        def slot_count(n, n0):
            if isinstance(n, int):
                return 16 * (n // RAW + 1)
            return (n - n0) * (16 // RAW) + 16 * (n0 // RAW + 1)

        def chunk(i, d):
            if isinstance(i, int) and i == NT - 1:
                return i
            return i if d == 0 else i * -1 + (NT - 2)

        def gcol(a, d, c, h):
            return a[:, d, :, h][:, c:c + 1] if isinstance(c, int) else a[:, d, :, h][:, bass.ds(c, 1)]

        def grow(a, d, c):
            return a[:, d, c] if isinstance(c, int) else a[:, d, bass.ds(c, 1), :].rearrange("p a h -> p (a h)")

        def dft_place(ab, e):
            if e < 8:
                cs, j, lh = e // 4, e // 2 % 2, e % 2
                return ab[:, cs, j, 512 * lh:512 * lh + 512], bank[2 * j + lh][:, :]
            cs, j = e // 2 % 2, e % 2
            return ab[:, cs, j, LAT:T], bank[e % 4][:, 0:P]

        block = top.enter_context(nc.Block())

        @block.sync
        def _(sp):
            sp.dma_start(base[:], k_base).then_inc(s_const, 16)
            sp.dma_start(cst[:], k_cst).then_inc(s_const, 16)
            sp.dma_start(rows[:], vectors).then_inc(s_rows, 16)

            def load_ada(j, slot, first):
                if not first:
                    sp.wait_ge(s_adam, j - 1)
                sp.dma_start(ada[:, slot], w_ada[bass.ds(j, 1)].rearrange("a p n -> (a p) n")).then_inc(s_ada[slot], 16)

            load_ada(0, 0, True)
            load_ada(1, 1, True)
            with sp.Fori(1, 24) as i:
                for u in range(2):
                    load_ada(i * 2 + u, u, False)

            def unit(n, slot, src, first=False):
                if not first:
                    sp.wait_ge(s_whi, n - RAW + 1)
                    sp.wait_ge(s_wlo, n - RAW + 1)
                sp.dma_start(raw[:, slot], src.rearrange("a p n -> (a p) n")).then_inc(s_raw[slot], 16)

            def units(n0, src, s0, count):
                with sp.Fori(0, count // RAW) as i:
                    for u in range(RAW):
                        unit(i * RAW + n0 + u, (n0 + u) % RAW, src[bass.ds(i * RAW + s0 + u, 1)])

            for u in range(RAW):
                unit(u, u, w_stream[u:u + 1], True)
            units(RAW, w_stream, RAW, U_F - 1 - RAW)
            unit(U_F - 1, (U_F - 1) % RAW, w_stream[U_F - 1:U_F])
            units(U_F, k_dft, 0, F_UNITS - 1)
            unit(U_E - 1, (U_E - 1) % RAW, k_dft[F_UNITS - 1:F_UNITS])
            with sp.Fori(0, NG) as g:
                for i in range(E_UNITS // RAW):
                    for u in range(RAW):
                        m = i * RAW + u
                        unit(g * E_UNITS + U_E + m, (U_E + m) % RAW, w_stream[U_F + m:U_F + m + 1])
            with sp.Fori(0, NG) as g:
                with sp.Fori(0, FF_UNITS // RAW) as i:
                    for u in range(RAW):
                        unit(g * FF_UNITS + i * RAW + U_FF + u, (U_FF + u) % RAW,
                             w_stream[bass.ds(i * RAW + U_F + E_UNITS + u, 1)])

        @block.tensor
        def _(pe):
            def unit_ready(n):
                pe.wait_ge(s_wlo, n + 1)

            def W(slot, k):
                return w_hi[:, slot, ktile(k)], w_lo[:, slot, ktile(k)]

            pe.wait_ge(s_const, 32)
            pe.wait_ge(s_rows, 16)
            pe.transpose(bank[4][:, 0:V_ROWS], rows[:, :], ident[0:V_ROWS, 0:V_ROWS]).then_inc(s_vec, 1)

            def x_pair(base_i, first, n):
                for u in range(n):
                    pe.wait_ge(s_xin[u], base_i * 16 + 16)
                    if not first:
                        pe.wait_ge(s_xev, base_i * 4 + 2 * u - 2)
                    for k in range(KT):
                        m = pe.transpose(bank[2 * u + k // 4][:, ktile(k % 4)], x_in[:, u, ktile(k)], ident)
                        if k % 4 == 3:
                            m.then_inc(s_xt, 1)

            x_pair(0, True, 2)
            with pe.Fori(1, 4) as i:
                x_pair(i, False, 2)
            x_pair(4, False, 1)

            pe.wait_ge(s_silu, 1)
            with pe.Fori(0, 24) as i:
                for u in range(2):
                    pe.wait_ge(s_ada[u], i * 16 + 16)
                    for k in range(KT):
                        m = pe.matmul(bank[5][:, bass.ds(i * 4 + 2 * u, 2)], ada[:, u, ktile(k)], silu_c[:, k, :],
                                      start=k == 0, stop=k == KT - 1)
                    m.then_inc(s_adam, 1)

            def stat(which):
                q = number["ST", which]
                pe.wait_ge(s_accs, KT * (q + 1))
                if which == "h0":
                    pe.wait_ge(s_const, 32)
                if q:
                    pe.wait_ge(s_sd, q)
                pe.matmul(bank[7][:, 0:GW], ones, acc[:, :], start=True, stop=True).then_inc(s_st, 1)

            def z_unit(n, n0, slot, first):
                unit_ready(n)
                for b in range(NG):
                    j = 3 * n0 + b
                    if not (first and j < 4):
                        pe.wait_ge(s_zev, 3 * n + b - 3)
                    for k in range(KT):
                        wh, wl = W(slot, k)
                        r = slice(b * GW, (b + 1) * GW)
                        m = mm3(pe, bank[j % 4][:, 0:GW], wh, wl, h_hi[:, k, r], h_lo[:, k, r], k == 0, k == KT - 1)
                    m.then_inc(s_unit if b == NG - 1 else s_zmm, 1)

            def z_units(n0, count, first):
                if first:
                    for u in range(4):
                        z_unit(n0 + u, n0 + u, (n0 + u) % SPL, True)
                with pe.Fori(1 if first else 0, count // 4) as i:
                    for u in range(4):
                        z_unit(i * 4 + n0 + u, n0 + u, (n0 + u) % SPL, False)

            def t_pair(i, us, first):
                for u in us:
                    pe.wait_ge(s_zt[u], i * 32 + 32)
                    if not (first and u == 0):
                        pe.wait_ge(s_tact, i * 4 + 2 * u)
                        pe.wait_ge(s_tdve, i * 6 + 3 * u)
                    for k in range(12):
                        m = pe.transpose(bank[4 + k // 4][:, ktile(k % 4)], zt[:, u, k, :], ident)
                        if k % 4 == 3:
                            m.then_inc(s_tmm, 1)

            def mixers():
                t_pair(0, (0, 1), True)
                with pe.Fori(1, 4) as i:
                    t_pair(i, (0, 1), False)
                t_pair(4, (0,), False)
                for i in range(2 * (LAT // P)):
                    n = U_F + i
                    unit_ready(n)
                    cs, tt = divmod(i, LAT // P)
                    if i == 0:
                        pe.wait_ge(s_tdve, 3 * NT)
                        pe.wait_ge(s_zev, 3 * (Z1_UNITS + 1 + Z2_UNITS))
                    if i == LAT // P:
                        pe.wait_ge(s_flo, 4)
                    for j in range(2):
                        for lh in range(2):
                            r = slice(lh * 512, (lh + 1) * 512)
                            m = mm3(pe, bank[2 * j + lh][:, :], uf_hi[:, tt, ktile(j)], uf_lo[:, tt, ktile(j)],
                                    w_hi[:, n % SPL, r], w_lo[:, n % SPL, r], tt == 0, tt == LAT // P - 1)
                            if tt == LAT // P - 1 and (j, lh) != (1, 1):
                                m.then_inc(s_fmm, 1)
                    m.then_inc(s_unit, 1)
                n = U_F + F_UNITS - 1
                unit_ready(n)
                for cs in range(2):
                    for j in range(2):
                        e = 8 + 2 * cs + j
                        pe.wait_ge(s_flo, e - 3)
                        m = mm3(pe, bank[e % 4][:, 0:P], uf_hi[:, NT - 1, ktile(j)], uf_lo[:, NT - 1, ktile(j)],
                                w_hi[:, n % SPL, ktile(cs)], w_lo[:, n % SPL, ktile(cs)], True, True)
                        m.then_inc(s_unit if e == 11 else s_fmm, 1)
                pe.wait_ge(s_cbl, 1)
                pe.wait_ge(s_flo, 12)
                for x in range(6):
                    j, g = divmod(x, NG)
                    if x >= 2:
                        pe.wait_ge(s_mev, x - 1)
                    r = slice(g * GW, (g + 1) * GW)
                    for cs in range(2):
                        m = mm3(pe, bank[4 + x % 2][:, 0:GW], cb_hi[:, cs, :], cb_lo[:, cs, :],
                                ab_hi[:, cs, j, r], ab_lo[:, cs, j, r], cs == 0, cs == 1)
                    m.then_inc(s_cmm, 1)
                pe.wait_ge(s_mev, 6)
                pe.wait_ge(s_wp, 16 * 4)
                for g in range(NG):
                    if g:
                        pe.wait_ge(s_pa, g)
                        pe.wait_ge(s_pd, g)
                    for i in range(3 * g, 3 * g + 3):
                        kind = int(i == NT - 1)
                        for w in range(4):
                            o = bank[4 + w // 2][GD * (w % 2):GD * (w % 2) + GD, ktile(i - 3 * g)]
                            m = pe.matmul(o, up[:, i, GD * w:GD * (w + 1)],
                                          K["pool"][:, (4 * kind + w) * P:(4 * kind + w + 1) * P],
                                          start=True, stop=True)
                    m.then_inc(s_pmm, 1)
                    pe.wait_ge(s_pa, g + 1)
                    pe.wait_ge(s_pd, g + 1)
                    for j in range(2):
                        if g:
                            pe.wait_ge(s_mev, 6 + 2 * g - 1 + j)
                        pe.matmul(bank[6 + j][:, 0:GW], wp[:, j, :], pT[:, j, :], start=True,
                                  stop=True).then_inc(s_cmm, 1)
                gates()
                mlstm()

            def gates():
                pe.wait_ge(s_pa, NG)
                pe.wait_ge(s_pd, NG)
                pe.wait_ge(s_mev, 12)
                for i in range(NT):
                    m = pe.matmul(bank[4][:, NGC * i:NGC * (i + 1)], gz[0:NGC, ktile(i)], ident[0:NGC, 0:NGC],
                                  start=True, stop=True)
                m.then_inc(s_gp, 1)
                pe.wait_ge(s_gd, GD_LF)
                pe.matmul(bank[5][:, 0:NJ], K["tri_f"], lf[:, 0].rearrange("p c h -> p (c h)"), start=True, stop=True)
                pe.matmul(bank[5][:, NJ:2 * NJ], K["tri_b"], lf[:, 1].rearrange("p c h -> p (c h)"), start=True,
                          stop=True)
                pe.matmul(bank[6][:, 0:2 * NJ], ones, lf[:].rearrange("p d c h -> p (d c h)"), start=True,
                          stop=True).then_inc(s_gp, 1)
                pe.wait_ge(s_gd, GD_AL)
                pe.matmul(bank[4][0:NJ, 0:P], al[:, 0].rearrange("p c h -> p (c h)"), ident, start=True, stop=True)
                pe.matmul(bank[7][0:NJ, 0:P], al[:, 1].rearrange("p c h -> p (c h)"), K["rev"], start=True,
                          stop=True).then_inc(s_gp, 1)
                pe.wait_ge(s_gd, GD_SCAN)
                pe.matmul(bank[5][:, 0:NJ], rows_m[:, 0, :], ident[0:NJ, 0:NJ], start=True, stop=True)
                pe.matmul(bank[6][:, 0:NJ], rows_m[:, 1, :], ident[0:NJ, 0:NJ], start=True,
                          stop=True).then_inc(s_gp, 1)
                pe.wait_ge(s_gd, GD_MCOPY)
                pe.matmul(bank[4][:, 0:NJ], K["rev"], mrev[:, :], start=True, stop=True).then_inc(s_gp, 1)
                pe.wait_ge(s_gd, GD_MTOK)
                pe.matmul(bank[7][:, 0:NJ], K["last"], mtok[:, 0].rearrange("p c h -> p (c h)"), start=True,
                          stop=True)
                pe.matmul(bank[7][:, NJ:2 * NJ], K["first"], mtok[:, 1].rearrange("p c h -> p (c h)"), start=True,
                          stop=True).then_inc(s_gp, 1)
                pe.wait_ge(s_gd, GD_G)
                pe.matmul(bank[5][0:2 * NJ, 0:P], gneg[:].rearrange("p d c h -> p (d c h)"), ident, start=True,
                          stop=True).then_inc(s_gp, 1)

            def ml(i, d, st, first):
                x = i * 2 + d
                pe.wait_ge(s_ld[d], i * 80 + 80)
                if not (first and d == 0):
                    pe.wait_ge(s_num, x)
                    pe.wait_ge(s_cup, x)
                for h in range(H):
                    m = pe.matmul(bank[4][:, ktile(h)], k_sb[:, d, h, :], q_sb[:, d, h, :], start=True, stop=True)
                m.then_inc(s_qk, 1)
                for h in range(H):
                    m = pe.matmul(bank[5 + h // 2][:, C1 * (h % 2):C1 * (h % 2 + 1)], q_sb[:, d, h, :],
                                  st[:, d, h, :], start=True, stop=True)
                m.then_inc(s_int, 1)
                pe.wait_ge(s_p, x + 1)
                for h in range(H):
                    m = pe.matmul(bank[7 if h < 2 else 4][:, C1 * (h % 2):C1 * (h % 2 + 1)], ew[:, d, h, :],
                                  v_sb[:, d, h, :], start=True, stop=True)
                m.then_inc(s_intra, 1)
                pe.wait_ge(s_wv, x + 1)
                pe.wait_ge(s_iev, x + 1)
                for h in range(H):
                    m = pe.matmul(bank[5 + h // 2][:, C1 * (h % 2):C1 * (h % 2 + 1)], kt_sb[:, d, ktile(h)],
                                  wv[:, d, h, :], start=True, stop=True)
                m.then_inc(s_kvm, 1)

            def mlstm():
                pe.wait_ge(s_gd, GD_END)
                pe.wait_ge(s_st0, 64)
                pe.wait_ge(s_set, 3)
                for d in range(2):
                    ml(0, d, st_lat, True)
                with pe.Fori(1, NT - 1) as i:
                    for d in range(2):
                        ml(i, d, st_lat, False)
                for d in range(2):
                    ml(NT - 1, d, st_ctx, False)
                pe.wait_ge(s_num, 2 * NT)
                pe.wait_ge(s_cup, 2 * NT)

                def hm(i, us, first):
                    for u in us:
                        pe.wait_ge(s_hs, i * 2 + u + 1)
                        if not first:
                            pe.wait_ge(s_ho, i * 2 + u - 1)
                        for h in range(H):
                            m = pe.transpose(bank[4 + u][:, ktile(h)], hs[:, u, ktile(h)], ident)
                        m.then_inc(s_ht, 1)

                hm(0, (0, 1), True)
                with pe.Fori(1, 4) as i:
                    hm(i, (0, 1), False)
                hm(4, (0,), False)

            def e1(g):
                pe.wait_ge(s_mxl, KT * (g + 1))
                if g == 0:
                    pe.wait_ge(s_ho, NT)
                if g:
                    pe.wait_ge(s_sd, number["ST", "h2"] + 1)

                def one(c, c0, first):
                    n = c + (U_E + g * E_UNITS)
                    unit_ready(n)
                    if not (first and c0 < 2):
                        pe.wait_ge(s_ym, c * 3 + (3 * KT * g - 3))
                    for b, ks in enumerate(((0, 1), (2, 3), (4, 5, 6, 7))):
                        for k in ks:
                            wh, wl = W((U_E + c0) % SPL, k)
                            m = mm3(pe, bank[3 * (c0 % 2) + b][:, 0:GW], wh, wl, mx_hi[:, k, :], mx_lo[:, k, :],
                                    k == ks[0], k == ks[-1])
                    m.then_inc(s_unit, 1)

                for c in range(4):
                    one(c, c, g == 0)
                for c in range(4, 8):
                    one(c, c, False)

            def e2(g):
                pe.wait_ge(s_yl, KT * (g + 1))
                pe.wait_ge(s_sd, max(q + 1 for (s, w), q in number.items() if s == "ST" and
                                     ORDER.index((s, w)) < ORDER.index(("E2", g))))
                for c in range(KT):
                    n = U_E + g * E_UNITS + KT + c
                    unit_ready(n)
                    if g or c >= 2:
                        pe.wait_ge(s_e2e, KT * g + c - 1)
                    for k in range(KT):
                        wh, wl = W(n % SPL, k)
                        m = mm3(pe, bank[6 + c % 2][:, 0:GW], wh, wl, yy_hi[:, k, :], yy_lo[:, k, :], k == 0,
                                k == KT - 1)
                    m.then_inc(s_unit, 1)

            def fi(g):
                pe.wait_ge(s_nl, KT * (number["HN", f"x{g}"] + 1))
                if g == 0:
                    pe.wait_ge(s_ym, 3 * KT * NG)
                n0 = U_FF + g * FF_UNITS

                def turn(i, first):
                    for u in range(4):
                        unit_ready(i * 4 + (n0 + u))
                        if not (first and g == 0):
                            if u % 2 == 0:
                                pe.wait_ge(s_sa, i * 2 + (FT * g + u // 2 - 1))
                            else:
                                pe.wait_ge(s_ff, i * 2 + (FT * g + u // 2 - 1))
                        for k in range(KT):
                            wh, wl = W((n0 + u) % SPL, k)
                            m = mm3(pe, bank[u][:, 0:GW], wh, wl, h2_hi[:, k, :], h2_lo[:, k, :], k == 0,
                                    k == KT - 1)
                        m.then_inc(s_unit, 1)

                turn(0, True)
                with pe.Fori(1, FT // 2) as i:
                    turn(i, False)

            def fo(g):
                pe.wait_ge(s_fl, FT * (g + 1))
                n0 = U_FF + g * FF_UNITS + 2 * FT

                def turn(i, first):
                    for c in range(4):
                        if not (first and c < 2 and g == 0):
                            pe.wait_ge(s_foe, i * 4 + (KT * g + c - 1))
                        k0 = 0
                        for part, nk in enumerate(FO_K):
                            u = 3 * c + part
                            unit_ready(i * 12 + (n0 + u))
                            for k in range(nk):
                                wh, wl = W((n0 + u) % SPL, k)
                                m = mm3(pe, bank[4 + c % 2][:, 0:GW], wh, wl, f_hi[:, k0 + k, :],
                                        f_lo[:, k0 + k, :], k0 + k == 0, k0 + k == FT - 1)
                            k0 += nk
                            m.then_inc(s_unit, 1)

                turn(0, True)
                turn(1, False)

            def ot(g):
                wait_x(pe, f"o{g}")
                for x in range(6):
                    t, half = divmod(x, 2)
                    if g or x >= 2:
                        pe.wait_ge(s_oe, 6 * g + x - 1)
                    for k in range(4):
                        m = pe.transpose(bank[6 + half][:, ktile(k)], y2[:, 4 * half + k, ktile(t)], ident)
                    m.then_inc(s_ot, 1)

            pe.wait_ge(s_vecc, 1)
            for stage, w in ORDER:
                if stage == "ST":
                    turned = sum(s == "OT" for s, _ in ORDER[:ORDER.index((stage, w))])
                    projected = sum(s == "E2" for s, _ in ORDER[:ORDER.index((stage, w))])
                    if projected:
                        pe.wait_ge(s_e2e, KT * projected)
                    if turned:
                        pe.wait_ge(s_oe, 6 * turned)
                    stat(w)
                elif stage == "MIX":
                    pe.wait_ge(s_nl, KT * NG)
                    z_units(0, Z1_UNITS, True)
                    z_unit(U_ZG, U_ZG, U_ZG % SPL, False)
                    z_units(U_Z2, Z2_UNITS, False)
                    mixers()
                elif stage == "E1":
                    e1(w)
                elif stage == "E2":
                    e2(w)
                elif stage == "FI":
                    fi(w)
                elif stage == "FO":
                    fo(w)
                elif stage == "OT":
                    pe.wait_ge(s_sd, max(q + 1 for (s, v), q in number.items() if s == "ST" and
                                         ORDER.index((s, v)) < ORDER.index(("OT", w))))
                    ot(w)

        @block.scalar
        def _(act):
            def split(n, n0):
                slot = n0 % RAW
                act.wait_ge(s_raw[slot], slot_count(n, n0))
                if not (isinstance(n, int) and n < SPL):
                    act.wait_ge(s_unit, n - SPL + 1)
                act.copy(w_hi[:, slot], raw[:, slot]).then_inc(s_whi, 1)

            def silu_vectors():
                act.wait_ge(s_vecc, 1)
                act.activation(silu_c[:].rearrange("p k v -> p v k"),
                               vec[:, V_C:V_C + 2 * KT].rearrange("p (v k) -> p v k", v=2), ACT.Silu).then_inc(s_silu, 1)

            def sq(which):
                q, m0, tmp = number["SQ", which], tmp_at["SQ", which], tmp_of(which)
                src = source(which)
                wait_source(act, which)
                for j in range(KT):
                    m = m0 + j
                    if m >= 4:
                        wait_tmp(act, m)
                    act.activation(tmp[:, m % 4], src[:, j], ACT.Square).then_inc(s_sq, 1)

            def stat(which):
                q = number["ST", which]
                act.wait_ge(s_st, q + 1)
                if q:
                    wait_applied(act, q)
                else:
                    act.wait_ge(s_set, 1)
                act.activation(rstd[:, :], bank[7][:, 0:GW], ACT.Sqrt, bias=eps[:, 0:1], scale=1.0 / D).then_inc(s_sd, 1)

            def hn(which):
                q, m0, tmp, g = number["HN", which], tmp_at["HN", which], tmp_of(which), int(which[1])
                first = which[0] == "h"
                scale, shift = (A1, mod[:, 0:8]) if first else (A2, mod[:, 24:32])
                if which == "h0":
                    act.wait_ge(s_mod, 1)
                if not first and g:
                    act.wait_ge(s_unit, f_unit(g - 1, 2 * FT))
                if which == "x0":
                    act.wait_ge(s_host[0], 80)
                    act.wait_ge(s_host[1], 64)
                nf = KT * q + sum(len(halves(int(w[1]))) * KT - KT for w in [w for s, w in ORDER if s == "HN"][:q])
                for j in range(KT):
                    t = tmp[:, (m0 + j) % 4]
                    act.wait_ge(s_nx, KT * q + j + 1)
                    for a, b, col in halves(g):
                        act.activation(t[:, a:b], t[:, a:b], ACT.Identity, bias=shift[:, j, col:col + 1],
                                       scale=scale[:, j, col:col + 1]).then_inc(s_nf, 1)
                        nf += 1
                    act.wait_ge(s_nf, nf)
                    out = h_hi[:, j, g * GW:(g + 1) * GW] if first else h2_hi[:, j]
                    act.copy(out, t).then_inc(s_nh, 1)

            def z_turn(i, n0, z0, us, func, first, scale=1.0):
                for u in us:
                    n = i * 4 + (n0 + u)
                    split(n + 2, n0 + u + 2)
                    for b in range(NG):
                        if b == NG - 1:
                            act.wait_ge(s_unit, n + 1)
                        else:
                            act.wait_ge(s_zmm, i * 8 + (2 * (n0 + u) + b + 1))
                        if b == 0 and not (first and z0 + u < 2):
                            act.wait_ge(s_zst[u % 2], i * 32 + 16 * ((z0 + u) // 2))
                        act.activation(z_st[:, u % 2, b * GW:(b + 1) * GW], bank[(3 * (n0 + u) + b) % 4][:, 0:GW],
                                       func, scale=scale).then_inc(s_zev, 1)

            def project():
                z_turn(0, 0, 0, range(4), ACT.Copy, True)
                z_turn(1, 0, 0, range(4), ACT.Copy, False)
                z_turn(2, 0, 0, range(4), ACT.Copy, False, scale=DH ** -0.5)
                z_turn(3, 0, 0, range(4), ACT.Copy, False)
                split(U_ZG + 2, U_ZG + 2)
                for b in range(NG):
                    if b == NG - 1:
                        act.wait_ge(s_unit, U_ZG + 1)
                    else:
                        act.wait_ge(s_zmm, 2 * U_ZG + b + 1)
                    act.copy(gz[:, b * GW:(b + 1) * GW], bank[(3 * U_ZG + b) % 4][:, 0:GW]).then_inc(s_zev, 1)
                with act.Fori(0, Z2_UNITS // 4) as i:
                    z_turn(i, U_Z2, Z1_UNITS, range(4), ACT.Sigmoid, False)

            def t_tile(i, u, first):
                act.wait_ge(s_tmm, i * 6 + 3 * u + 1)
                act.copy(uf_hi[:, bass.ds(i * 2 + u, 1), :].rearrange("p a c -> p (a c)"),
                         bank[4][:, 0:FW]).then_inc(s_tact, 1)
                act.wait_ge(s_tmm, i * 6 + 3 * u + 2)
                if not first:
                    act.wait_ge(s_kvst[u], i * 16)
                act.copy(kv_st[:, u, 0:MW], bank[5][:, :]).then_inc(s_tact, 1)

            def mixers():
                t_tile(0, 0, True)
                t_tile(0, 1, True)
                with act.Fori(1, 4) as i:
                    t_tile(i, 0, False)
                    t_tile(i, 1, False)
                t_tile(4, 0, False)
                act.copy(cb_hi[:].rearrange("p a c -> p (a c)"), K["cb"]).then_inc(s_cbh, 1)
                for i in range(F_UNITS):
                    n = U_F + i
                    split(n + 2, n + 2)
                    if i == 0:
                        act.wait_ge(s_kvst[0], 80)
                        act.wait_ge(s_kvst[1], 64)
                    if i in (7, 15, 16):
                        for e in range({7: 0, 15: 4, 16: 8}[i], {7: 4, 15: 8, 16: 12}[i]):
                            if e % 4 == 3:
                                act.wait_ge(s_unit, n + 1)
                            else:
                                act.wait_ge(s_fmm, e // 4 * 3 + e % 4 + 1)
                            out, ps = dft_place(ab_hi, e)
                            act.copy(out, ps).then_inc(s_fhi, 1)
                for x in range(6):
                    act.wait_ge(s_cmm, x + 1)
                    if x >= 2:
                        act.wait_ge(s_mst[x % 2], 16 * (x // 2))
                    act.copy(m_st[:, x % 2], bank[4 + x % 2][:, 0:GW]).then_inc(s_mev, 1)
                for g in range(NG):
                    act.wait_ge(s_pmm, g + 1)
                    if g:
                        act.wait_ge(s_cmm, 6 + 2 * g)
                    act.copy(pT[:, 0], bank[4][:, 0:GW]).then_inc(s_pa, 1)
                    for j in range(2):
                        x = 6 + 2 * g + j
                        act.wait_ge(s_cmm, x + 1)
                        act.wait_ge(s_mst[x % 2], 16 * (x // 2))
                        act.activation(m_st[:, x % 2], bank[6 + j][:, 0:GW], ACT.Copy,
                                       scale=vec[:, V_PSC + j:V_PSC + j + 1]).then_inc(s_mev, 1)
                act.wait_ge(s_gd, GD_ABS)
                flat = "p d c h -> p (d c h)"
                act.activation(lse[:].rearrange(flat), absf[:].rearrange(flat), ACT.Exp, scale=-1.0).then_inc(s_ga, 1)
                act.wait_ge(s_ga, 1)
                act.activation(lse[:].rearrange(flat), lse[:].rearrange(flat), ACT.Ln, bias=1.0).then_inc(s_ga, 1)
                act.wait_ge(s_gd, GD_LOGS)
                for a in (em, sdec, wst, carry):
                    act.activation(a[:].rearrange(flat), a[:].rearrange(flat), ACT.Exp).then_inc(s_ga, 1)
                act.wait_ge(s_ga, 6)
                for d in range(2):
                    ml(0, d, True)
                with act.Fori(1, NT - 1) as i:
                    for d in range(2):
                        ml(i, d, False)
                for d in range(2):
                    ml(NT - 1, d, False)

            def ml(i, d, first):
                x = i * 2 + d
                c = chunk(i, d)
                act.wait_ge(s_t, x + 1)
                if not first:
                    act.wait_ge(s_intra, x - 1)
                act.activation(ew[:, d].rearrange("p h t -> p (h t)"), lw[:, d].rearrange("p h t -> p (h t)"),
                               ACT.Exp).then_inc(s_e, 1)
                act.copy(sdec_now[:, d], grow(sdec, d, c)).then_inc(s_sn, 1)
                act.wait_ge(s_sn, x + 1)
                act.wait_ge(s_int, x + 1)
                if not first:
                    act.wait_ge(s_num, x - 1)
                for h in range(H):
                    m = act.activation(inter[:, d, h, :], bank[5 + h // 2][:, C1 * (h % 2):C1 * (h % 2 + 1)],
                                       ACT.Copy, scale=sdec_now[:, d, h:h + 1])
                m.then_inc(s_iev, 1)

            def mx(g):
                for k in range(KT):
                    x = KT * g + k
                    act.wait_ge(s_mx[k % 2], 16 * (x // 2 + 1))
                    if g:
                        act.wait_ge(s_unit, e_unit(g - 1, KT))
                    act.copy(mx_hi[:, k], mx_in[:, k % 2]).then_inc(s_mxh, 1)

            def e1(g):
                if g:
                    act.wait_ge(s_unit, e_unit(g, 0))
                for c in range(KT):
                    n = U_E + g * E_UNITS + c
                    split(n + 2, n + 2)
                    if c:
                        yhigh(g, c - 1)
                yhigh(g, KT - 1)

            def yhigh(g, c):
                act.wait_ge(s_ya, 2 * (KT * g + c + 1))
                act.copy(yy_hi[:, c], ya[:, c % 2, 0]).then_inc(s_yh, 1)

            def e2(g):
                if g:
                    wait_x(act, f"y{g - 1}")
                for c in range(KT):
                    n = U_E + g * E_UNITS + KT + c
                    split(n + 2, n + 2)
                    act.wait_ge(s_unit, n + 1)
                    act.copy(y2[:, c], bank[6 + c % 2][:, 0:GW]).then_inc(s_e2e, 1)

            def fi(g):
                n0 = U_FF + g * FF_UNITS
                if g:
                    act.wait_ge(s_unit, f_unit(g, 0))

                def high(j, slot):
                    act.wait_ge(s_ff, j + FT * g + 1)
                    act.copy(f_hi[:, bass.ds(j, 1), :].rearrange("p a n -> p (a n)"), ff[:, slot]).then_inc(s_fh, 1)

                def turn(i, first):
                    for u in range(4):
                        split(i * 4 + (n0 + u + 2), n0 + u + 2)
                        if u % 2 == 0:
                            continue
                        p = u // 2
                        act.wait_ge(s_unit, i * 4 + (n0 + 2 * p + 1))
                        if not (first and g == 0):
                            act.wait_ge(s_ff, i * 2 + (FT * g + p - 1))
                        act.activation(sa[:, p], bank[2 * p][:, 0:GW], ACT.Silu).then_inc(s_sa, 1)
                        if not (first and p == 0):
                            high(i * 2 + (p - 1), (p - 1) % 2)

                turn(0, True)
                with act.Fori(1, FT // 2) as i:
                    turn(i, False)
                high(FT - 1, 1)

            def fo(g):
                n0 = U_FF + g * FF_UNITS + 2 * FT
                if g == 0:
                    wait_x(act, "y2")
                else:
                    act.wait_ge(s_ot, 6 * g)

                def turn(i):
                    for c in range(4):
                        for part in range(3):
                            u = 3 * c + part
                            if n0 + 12 * i + u + 2 < U_END:
                                split(i * 12 + (n0 + u + 2), n0 + u + 2)
                        act.wait_ge(s_unit, n0 + 12 * i + 3 * (c + 1))
                        act.copy(y2[:, i * 4 + c], bank[4 + c % 2][:, 0:GW]).then_inc(s_foe, 1)

                turn(0)
                turn(1)

            def ot(g):
                for x in range(6):
                    half = x % 2
                    xx = 6 * g + x
                    act.wait_ge(s_ot, xx + 1)
                    if xx >= 2:
                        act.wait_ge(s_ost[half], 16 * (xx // 2))
                    act.copy(o_st[:, half], bank[6 + half][:, :]).then_inc(s_oe, 1)

            silu_vectors()
            split(0, 0)
            split(1, 1)
            stages = {"SQ": sq, "ST": stat, "HN": hn, "MX": mx, "E1": e1, "E2": e2, "FI": fi, "FO": fo, "OT": ot}
            for stage, w in ORDER:
                if stage == "MIX":
                    project()
                    mixers()
                elif stage != "X":
                    stages[stage](w)

        @block.vector
        def _(dve):
            def split(n, n0):
                slot = n0 % RAW
                dve.wait_ge(s_whi, n + 1)
                dve.tensor_tensor(w_lo[:, slot], raw[:, slot], w_hi[:, slot].bitcast(F32),
                                  ALU.subtract).then_inc(s_wlo, 1)

            def x_evac(i, us, first):
                for u in us:
                    for half in range(2):
                        dve.wait_ge(s_xt, i * 4 + 2 * u + half + 1)
                        ps = bank[2 * u + half][:, :].rearrange("p (k r w) -> p k r w", k=4, r=2)
                        out = xT[:, 4 * half:4 * half + 4, bass.ds(i * 2 * P + u * P, P)]
                        out = out.rearrange("p k (r w) -> p k r w", r=2)
                        if half == 0:
                            pos = K["pos_r"].rearrange("p (k r) -> p k r", k=4)[:, :, bass.ds(i * 4 + 2 * u, 2)]
                            pos = last(pos, GRID_W)
                        else:
                            pos = K["pos_c"].rearrange("p (k w) -> p k w", k=4).unsqueeze(2).broadcast_to(
                                (P, 4, 2, GRID_W))
                        dve.tensor_tensor(out, ps, pos, ALU.add).then_inc(s_xev, 1)

            def modulation():
                dve.wait_ge(s_adam, 48)
                n = [0]

                def link(m):
                    n[0] += 1
                    m.then_inc(s_modc, 1)

                link(dve.tensor_tensor(mod[:], bank[5][:, 0:96].rearrange("p (j v) -> p j v", v=2),
                                       last(vec[:, V_BADA:V_BADA + 48], 2), ALU.add))
                dve.wait_ge(s_modc, 1)

                def gain(i):
                    return last(vec[:, V_NORM + 8 * i:V_NORM + 8 * (i + 1)], 2)

                link(dve.scalar_tensor_tensor(A1[:], mod[:, 8:16], 1.0, gain(0), ALU.add, ALU.mult))
                link(dve.scalar_tensor_tensor(A2[:], mod[:, 32:40], 1.0, gain(2), ALU.add, ALU.mult))
                link(dve.tensor_tensor(G1[:], mod[:, 16:24], gain(1), ALU.mult))
                link(dve.tensor_tensor(G2[:], mod[:, 40:48], gain(3), ALU.mult))
                dve.wait_ge(s_modc, 5)
                dve.engine_nop().then_inc(s_mod, 1)

            def sq(which):
                q, m0, tmp = number["SQ", which], tmp_at["SQ", which], tmp_of(which)
                if q:
                    dve.wait_ge(s_st, q)
                for j in range(KT):
                    t = tmp[:, (m0 + j) % 4]
                    dve.wait_ge(s_sq, KT * q + j + 1)
                    if j == 0:
                        m = dve.tensor_copy(acc[:, :], t)
                    else:
                        dve.wait_ge(s_accs, KT * q + j)
                        m = dve.tensor_tensor(acc[:, :], acc[:, :], t, ALU.add)
                    m.then_inc(s_accs, 1)

            def stat(which):
                q = number["ST", which]
                dve.wait_ge(s_sd, q + 1)
                dve.reciprocal(rstd[:, :], rstd[:, :]).then_inc(s_rs, 1)
                dve.wait_ge(s_rs, q + 1)

            def hn(which):
                q, m0, tmp, g = number["HN", which], tmp_at["HN", which], tmp_of(which), int(which[1])
                src = source(which)
                first = which[0] == "h"
                for j in range(KT + 2):
                    if j < KT:
                        if m0 + j >= 4:
                            wait_tmp(dve, m0 + j)
                        dve.tensor_tensor(tmp[:, (m0 + j) % 4], src[:, j], rstd[:, :], ALU.mult).then_inc(s_nx, 1)
                    if j >= 2:
                        jj = j - 2
                        dve.wait_ge(s_nh, KT * q + jj + 1)
                        hi, lo = (h_hi, h_lo) if first else (h2_hi, h2_lo)
                        r = slice(g * GW, (g + 1) * GW) if first else slice(0, GW)
                        m = dve.tensor_tensor(lo[:, jj, r], tmp[:, (m0 + jj) % 4], hi[:, jj, r].bitcast(F32),
                                              ALU.subtract)
                        m.then_inc(s_nl, 1)

            xs = [0]

            def xstage(which):
                g = int(which[1])
                dve.tensor_tensor(y2[:, :, :], y2[:, :, :], b3(rstd[:, :], KT), ALU.mult).then_inc(s_xs, 1)
                xs[0] += 1
                dve.wait_ge(s_xs, xs[0])
                G = G1 if which[0] == "y" else G2
                for j in range(KT):
                    for a, b, col in halves(g):
                        x = xT[:, j, g * GW + a:g * GW + b]
                        out = x if which[0] == "y" else y2[:, j, a:b]
                        m = dve.scalar_tensor_tensor(out, y2[:, j, a:b], G[:, j, col:col + 1], x, ALU.mult, ALU.add)
                m.then_inc(s_app, 1)

            def project():
                with dve.Fori(0, Z1_UNITS // 4) as i:
                    for u in range(4):
                        split(i * 4 + (u + 2), u + 2)
                split(U_ZG + 2, U_ZG + 2)
                with dve.Fori(0, Z2_UNITS // 4) as i:
                    for u in range(4):
                        split(i * 4 + (U_Z2 + u + 2), U_Z2 + u + 2)

            def t_tile(i, u, first):
                dve.wait_ge(s_tact, i * 4 + 2 * u + 1)
                sl = bass.ds(i * 2 + u, 1)
                one = "p a c -> p (a c)"
                dve.tensor_tensor(uf_lo[:, sl, :].rearrange(one), bank[4][:, 0:FW],
                                  uf_hi[:, sl, :].rearrange(one).bitcast(F32), ALU.subtract).then_inc(s_tdve, 1)
                dve.tensor_copy(up[:, sl, :].rearrange(one), bank[4][:, FW:2 * FW]).then_inc(s_tdve, 1)
                dve.wait_ge(s_tmm, i * 6 + 3 * u + 3)
                if not first:
                    dve.wait_ge(s_kvst[u], i * 16)
                dve.tensor_copy(kv_st[:, u, MW:2 * MW], bank[6][:, :]).then_inc(s_tdve, 1)

            def mixers():
                t_tile(0, 0, True)
                t_tile(0, 1, True)
                with dve.Fori(1, 4) as i:
                    t_tile(i, 0, False)
                    t_tile(i, 1, False)
                t_tile(4, 0, False)
                dve.wait_ge(s_cbh, 1)
                dve.tensor_tensor(cb_lo[:].rearrange("p a c -> p (a c)"), K["cb"],
                                  cb_hi[:].rearrange("p a c -> p (a c)").bitcast(F32),
                                  ALU.subtract).then_inc(s_cbl, 1)
                dve.memset(wp[:], 0.0).then_inc(s_wp0, 1)
                for i in range(F_UNITS):
                    n = U_F + i
                    split(n + 2, n + 2)
                    if i in (7, 15, 16):
                        for e in range({7: 0, 15: 4, 16: 8}[i], {7: 4, 15: 8, 16: 12}[i]):
                            dve.wait_ge(s_fhi, e + 1)
                            out, ps = dft_place(ab_lo, e)
                            hi, _ = dft_place(ab_hi, e)
                            dve.tensor_tensor(out, ps, hi.bitcast(F32), ALU.subtract).then_inc(s_flo, 1)
                for g in range(NG):
                    dve.wait_ge(s_pmm, g + 1)
                    if g:
                        dve.wait_ge(s_cmm, 6 + 2 * g)
                    dve.tensor_copy(pT[:, 1], bank[5][:, 0:GW]).then_inc(s_pd, 1)
                gates()
                mlstm()

            def gates():
                n = [0]

                def link(m):
                    n[0] += 1
                    m.then_inc(s_gd, 1)
                    dve.wait_ge(s_gd, n[0])

                flat = "p d c h -> p (d c h)"
                half = "p c h -> p (c h)"
                dve.wait_ge(s_gp, 1)
                dve.wait_ge(s_gl, 32)
                link(dve.tensor_tensor(gts[:], bank[4][:, 0:NT * NGC].rearrange("p (c g) -> p c g", c=NT),
                                       b3(bg[:], NT), ALU.add))

                def col(d, kind):
                    return gts[:, :, 8 * d + 4 * kind:8 * d + 4 * kind + 4]

                for d in range(2):
                    link(dve.scalar_tensor_tensor(absf[:, d], col(d, 1), -1.0, col(d, 1), ALU.mult, ALU.max))
                assert n[0] == GD_ABS
                dve.wait_ge(s_ga, 2)
                for d in range(2):
                    link(dve.scalar_tensor_tensor(lf[:, d], col(d, 1), 0.0, lse[:, d], ALU.min, ALU.subtract))
                assert n[0] == GD_LF
                dve.wait_ge(s_gp, 2)
                link(dve.tensor_copy(cum[:].rearrange(flat), bank[5][:, 0:2 * NJ]))
                link(dve.tensor_copy(blast[:].rearrange(flat), bank[6][:, 0:2 * NJ]))
                for d in range(2):
                    link(dve.tensor_tensor(al[:, d], col(d, 0), cum[:, d], ALU.subtract))
                assert n[0] == GD_AL
                dve.wait_ge(s_gp, 3)
                for d in range(2):
                    link(dve.tensor_copy(rows_a[:, d], bank[4 + 3 * d][0:NJ, 0:P]))
                for d in range(2):
                    link(dve.tensor_tensor_scan(rows_m[:, d], rows_a[:, d], rows_a[:, d], -3e38, ALU.max, ALU.max))
                assert n[0] == GD_SCAN
                dve.wait_ge(s_gp, 4)
                link(dve.tensor_copy(mtok[:, 0].rearrange(half), bank[5][:, 0:NJ]))
                link(dve.tensor_copy(mrev[:, :], bank[6][:, 0:NJ]))
                assert n[0] == GD_MCOPY
                dve.wait_ge(s_gp, 5)
                link(dve.tensor_copy(mtok[:, 1].rearrange(half), bank[4][:, 0:NJ]))
                assert n[0] == GD_MTOK
                dve.wait_ge(s_gp, 6)
                link(dve.tensor_copy(mlast[:].rearrange(flat), bank[7][:, 0:2 * NJ]))
                NL = NT - 1
                link(dve.tensor_copy(mprev[:, 0, 0], sm[:, 0]))
                link(dve.tensor_copy(mprev[:, 1, NL - 1], sm[:, 1]))
                link(dve.memset(mprev[:, :, NL], 0.0))
                for s in range(NL):
                    for d in range(2):
                        c = s if d == 0 else NL - 1 - s
                        before = mprev[:, d, c] if s == 0 else mnew[:, d, c + (1 if d else -1)]
                        link(dve.tensor_tensor(mnew[:, d, c], before, mlast[:, d, c], ALU.max))
                        link(dve.tensor_tensor(mnew[:, d, c], mnew[:, d, c], blast[:, d, c], ALU.add))
                link(dve.tensor_tensor(mnew[:, :, NL], mprev[:, :, NL], mlast[:, :, NL], ALU.max))
                link(dve.tensor_tensor(mnew[:, :, NL], mnew[:, :, NL], blast[:, :, NL], ALU.add))
                link(dve.tensor_copy(mprev[:, 0, 1:NL], mnew[:, 0, 0:NL - 1]))
                link(dve.tensor_copy(mprev[:, 1, 0:NL - 1], mnew[:, 1, 1:NL]))
                link(dve.tensor_tensor(gneg[:], mprev[:], mtok[:], ALU.max))
                link(dve.tensor_scalar(gneg[:], gneg[:], -1.0, None, ALU.mult))
                assert n[0] == GD_G
                link(dve.tensor_tensor(em[:], gneg[:], cum[:], ALU.subtract))
                link(dve.tensor_tensor(sdec[:], mprev[:], gneg[:], ALU.add))
                link(dve.tensor_tensor(wst[:], al[:], blast[:], ALU.add))
                link(dve.tensor_tensor(wst[:], wst[:], mnew[:], ALU.subtract))
                link(dve.tensor_tensor(carry[:], blast[:], mprev[:], ALU.add))
                link(dve.tensor_tensor(carry[:], carry[:], mnew[:], ALU.subtract))
                assert n[0] == GD_LOGS
                dve.wait_ge(s_gp, 7)
                link(dve.tensor_copy(g_rows[:, :], bank[5][0:2 * NJ, 0:P]))
                assert n[0] == GD_END

            dn = [0]

            def ml(i, d, st, first, base_den):
                x = i * 2 + d
                c = chunk(i, d)
                mask = K["mask_b"] if d else K["mask_f"]
                dve.wait_ge(s_ld[d], i * 80 + 80)
                for h in range(H):
                    m = dve.scalar_tensor_tensor(lw[:, d, h], g_sb[:, d, h], gcol(al, d, c, h), mask, ALU.add,
                                                 ALU.min)
                m.then_inc(s_t, 1)
                if not first:
                    dve.wait_ge(s_kvm, x - 1)
                dve.tensor_tensor(wv[:, d], v_sb[:, d], last(grow(wst, d, c), C1), ALU.mult).then_inc(s_wv, 1)
                dve.wait_ge(s_e, x + 1)
                dve.wait_ge(s_qk, x + 1)
                dve.tensor_tensor(ew[:, d].rearrange("p h t -> p (h t)"), ew[:, d].rearrange("p h t -> p (h t)"),
                                  bank[4][:, :], ALU.mult).then_inc(s_p, 1)
                dve.wait_ge(s_iev, x + 1)
                dve.wait_ge(s_intra, x + 1)
                for hh in range(2):
                    r = slice(2 * hh, 2 * hh + 2)
                    m = dve.tensor_tensor(num[:, d, r].rearrange("p h e -> p (h e)"),
                                          inter[:, d, r].rearrange("p h e -> p (h e)"),
                                          bank[7 if hh == 0 else 4][:, 0:2 * C1], ALU.add)
                m.then_inc(s_num, 1)
                dve.wait_ge(s_num, x + 1)
                dd = num[:, d, :, DH]
                dve.scalar_tensor_tensor(den[:, d], dd, -1.0, dd, ALU.mult, ALU.max).then_inc(s_den, 1)
                dve.wait_ge(s_den, x * 3 + 1)
                dve.tensor_tensor(den[:, d], den[:, d], grow(em, d, c), ALU.max).then_inc(s_den, 1)
                dve.wait_ge(s_den, x * 3 + 2)
                dve.reciprocal(den[:, d], den[:, d]).then_inc(s_den, 1)
                dve.wait_ge(s_den, x * 3 + 3)
                if not first:
                    dve.wait_ge(s_hst[d], i * 16)
                dve.tensor_tensor(h_out[:, d], num[:, d, :, 0:DH], last(den[:, d], DH), ALU.mult).then_inc(s_hd, 1)
                dve.wait_ge(s_kvm, x + 1)
                for h in range(H):
                    m = dve.scalar_tensor_tensor(st[:, d, h], st[:, d, h], gcol(carry, d, c, h),
                                                 bank[5 + h // 2][:, C1 * (h % 2):C1 * (h % 2 + 1)], ALU.mult,
                                                 ALU.add)
                m.then_inc(s_cup, 1)

            def mlstm():
                dve.memset(v_sb[:], 1.0).then_inc(s_set, 1)
                dve.memset(st_ctx[:], 0.0).then_inc(s_set, 1)
                dve.wait_ge(s_ga, 6)
                dve.wait_ge(s_st0, 64)
                for d in range(2):
                    ml(0, d, st_lat, True, 0)
                with dve.Fori(1, NT - 1) as i:
                    for d in range(2):
                        ml(i, d, st_lat, False, 0)
                for d in range(2):
                    ml(NT - 1, d, st_ctx, False, 0)

                def hm_sum(i, u, first):
                    dve.wait_ge(s_hl[u], i * 48 + 48)
                    if not first:
                        dve.wait_ge(s_ht, i * 2 + u - 1)
                    dve.tensor_tensor(hs[:, u], hf_sb[:, u, 0], hf_sb[:, u, 1], ALU.add).then_inc(s_hs, 1)

                def hm_gate(i, u, first):
                    dve.wait_ge(s_ht, i * 2 + u + 1)
                    if not first:
                        dve.wait_ge(s_host[u], i * 16)
                    dve.tensor_tensor(ho[:, u].rearrange("p h t -> p (h t)"),
                                      o_sb[:, u].rearrange("p h t -> p (h t)"), bank[4 + u][:, :],
                                      ALU.mult).then_inc(s_ho, 1)

                def hm(i, us, first):
                    for u in us:
                        hm_sum(i, u, first)
                    for u in us:
                        hm_gate(i, u, first)

                hm(0, (0, 1), True)
                with dve.Fori(1, 4) as i:
                    hm(i, (0, 1), False)
                hm(4, (0,), False)

            def mx(g):
                for k in range(KT):
                    dve.wait_ge(s_mxh, KT * g + k + 1)
                    dve.tensor_tensor(mx_lo[:, k], mx_in[:, k % 2], mx_hi[:, k].bitcast(F32),
                                      ALU.subtract).then_inc(s_mxl, 1)

            def ylow(g, c):
                dve.wait_ge(s_yh, KT * g + c + 1)
                dve.tensor_tensor(yy_lo[:, c], ya[:, c % 2, 0], yy_hi[:, c].bitcast(F32),
                                  ALU.subtract).then_inc(s_yl, 1)

            def e1(g):
                for c in range(KT):
                    n = U_E + g * E_UNITS + c
                    split(n + 2, n + 2)
                    dve.wait_ge(s_unit, n + 1)
                    x = KT * g + c
                    dve.wait_ge(s_mg[c % 2], 16 * (x // 2 + 1))
                    if x >= 2:
                        dve.wait_ge(s_yl, x - 1)
                    for b in range(3):
                        dve.tensor_tensor(ya[:, c % 2, b], mg[:, c % 2, b], bank[3 * (c % 2) + b][:, 0:GW],
                                          ALU.mult).then_inc(s_ym, 1)
                    if c:
                        ylow(g, c - 1)
                ylow(g, KT - 1)

            def e2(g):
                for c in range(KT):
                    n = U_E + g * E_UNITS + KT + c
                    split(n + 2, n + 2)

            def fi(g):
                n0 = U_FF + g * FF_UNITS

                def low(j, slot):
                    dve.wait_ge(s_fh, j + FT * g + 1)
                    sl = bass.ds(j, 1)
                    dve.tensor_tensor(f_lo[:, sl, :].rearrange("p a n -> p (a n)"), ff[:, slot],
                                      f_hi[:, sl, :].rearrange("p a n -> p (a n)").bitcast(F32),
                                      ALU.subtract).then_inc(s_fl, 1)

                def turn(i, first):
                    for u in range(4):
                        split(i * 4 + (n0 + u + 2), n0 + u + 2)
                        if u % 2 == 0:
                            continue
                        p = u // 2
                        dve.wait_ge(s_unit, i * 4 + (n0 + 2 * p + 2))
                        dve.wait_ge(s_sa, i * 2 + (FT * g + p + 1))
                        if not (first and g == 0):
                            dve.wait_ge(s_fl, i * 2 + (FT * g + p - 1))
                        dve.tensor_tensor(ff[:, p], sa[:, p], bank[2 * p + 1][:, 0:GW], ALU.mult).then_inc(s_ff, 1)
                        if not (first and p == 0):
                            low(i * 2 + (p - 1), (p - 1) % 2)

                turn(0, True)
                with dve.Fori(1, FT // 2) as i:
                    turn(i, False)
                low(FT - 1, 1)

            def fo(g):
                n0 = U_FF + g * FF_UNITS + 2 * FT
                for u in range(3 * KT):
                    if n0 + u + 2 < U_END:
                        split(n0 + u + 2, n0 + u + 2)

            dve.memset(eps[:], EPS).then_inc(s_set, 1)
            dve.wait_ge(s_vec, 1)
            dve.tensor_copy(vec[:], bank[4][:, 0:V_ROWS]).then_inc(s_vecc, 1)
            dve.wait_ge(s_vecc, 1)
            dve.wait_ge(s_const, 32)
            with dve.Fori(0, 4) as i:
                x_evac(i, (0, 1), False)
            for half in range(2):
                dve.wait_ge(s_xt, 16 + half + 1)
                dve.tensor_copy(xT[:, 4 * half:4 * half + 4, LAT:T],
                                bank[half][:, :].rearrange("p (k t) -> p k t", k=4)).then_inc(s_xev, 1)
            split(0, 0)
            split(1, 1)
            modulation()
            stages = {"SQ": sq, "ST": stat, "HN": hn, "X": xstage, "MX": mx, "E1": e1, "E2": e2, "FI": fi, "FO": fo}
            for stage, w in ORDER:
                if stage == "MIX":
                    project()
                    mixers()
                elif stage != "OT":
                    stages[stage](w)

        @block.gpsimd
        def _(pool):
            def one(ap):
                return ap.rearrange("a p n -> (a p) n")

            def x_load(i, us, first):
                for u in us:
                    if not first:
                        pool.wait_ge(s_xt, i * 4 + 2 * u - 2)
                    pool.dma_start(x_in[:, u], x_sample[0, bass.ds(i * 2 * P + u * P, P), :]).then_inc(s_xin[u], 16)

            x_load(0, (0, 1), True)
            with pool.Fori(1, 4) as i:
                x_load(i, (0, 1), False)
            pool.wait_ge(s_xt, 14)
            pool.dma_start(x_in[:, 0], x_prompt[0]).then_inc(s_xin[0], 16)

            def z_store(i, u, z0, shift):
                z = i * 4 + (z0 + u)
                pool.wait_ge(s_zev, i * 12 + 3 * (z0 + u + shift + 1))
                pool.dma_start(one(z_dram[bass.ds(z, 1)]), z_st[:, u % 2]).then_inc(s_zst[u % 2], 16)

            with pool.Fori(0, Z1_UNITS // 4) as i:
                for u in range(4):
                    z_store(i, u, 0, 0)
            with pool.Fori(0, Z2_UNITS // 4) as i:
                for u in range(4):
                    z_store(i, u, Z1_UNITS, 1)
            z_total = 16 * (Z1_UNITS + Z2_UNITS) // 2
            pool.wait_ge(s_zst[0], z_total)
            pool.wait_ge(s_zst[1], z_total)

            def t_load(i, u, first):
                if not first:
                    pool.wait_ge(s_tmm, i * 6 + 3 * u - 3)
                t = bass.ds(i * 2 * P + u * P, P)
                pool.dma_start(zt[:, u, 0:4], z_dram[0:4, :, t].rearrange("a p t -> p a t")).then_inc(s_zt[u], 16)
                pool.dma_start(zt[:, u, 4:12], z_dram[8:16, :, t].rearrange("a p t -> p a t")).then_inc(s_zt[u], 16)

            def kv_store(i, u):
                pool.wait_ge(s_tact, i * 4 + 2 * u + 2)
                pool.wait_ge(s_tdve, i * 6 + 3 * u + 3)
                pool.dma_start(one(kv_dram[bass.ds(i * 2 + u, 1)]), kv_st[:, u]).then_inc(s_kvst[u], 16)

            pool.wait_ge(s_unit, U_F)
            t_load(0, 0, True)
            t_load(0, 1, True)
            with pool.Fori(1, 4) as i:
                kv_store(i - 1, 0)
                t_load(i, 0, False)
                kv_store(i - 1, 1)
                t_load(i, 1, False)
            kv_store(3, 0)
            t_load(4, 0, False)
            kv_store(3, 1)
            kv_store(4, 0)
            pool.wait_ge(s_wp0, 1)
            for w in range(4):
                r = slice(GD * (w % 2), GD * (w % 2) + GD)
                pool.dma_start(wp[r, w // 2, r], w_pool[0, w]).then_inc(s_wp, 16)
            for x in range(12):
                pool.wait_ge(s_mev, x + 1)
                if x < 6:
                    tile, g = divmod(x, NG)
                else:
                    g, tile = divmod(x - 6, 2)
                    tile += 2
                pool.dma_start(mix_dram[tile, :, g * GW:(g + 1) * GW], m_st[:, x % 2]).then_inc(s_mst[x % 2], 16)
            pool.wait_ge(s_mst[0], 96)
            pool.wait_ge(s_mst[1], 96)
            pool.wait_ge(s_kvst[0], 80)
            pool.wait_ge(s_kvst[1], 64)
            pool.dma_start(bg[:], b_gate.rearrange("a d i h -> a (d i h)").broadcast_to((P, NGC))).then_inc(s_gl, 16)
            pool.dma_start(sm[:].rearrange("p d h -> p (d h)"),
                           state_m.rearrange("a e d h -> (a e) (d h)").broadcast_to((P, 2 * H))).then_inc(s_gl, 16)
            for d in range(2):
                pool.dma_start(st_lat[:, d, :, 0:DH], state_C[0, 0, d].rearrange("h k v -> k h v")).then_inc(s_st0, 16)
                pool.dma_start(st_lat[:, d, :, DH], state_n[0, 0, d].rearrange("h k -> k h"), allow_slow_non_contiguous=True).then_inc(s_st0, 16)
            pool.wait_ge(s_gd, GD_END)
            pool.dma_start(g_dram.rearrange("a (h t) -> (a h) t", h=H), g_rows[:, :]).then_inc(s_gst, 16)
            pool.wait_ge(s_gst, 16)
            pool.wait_ge(s_set, 2)

            def ml_load(i, d, first):
                c = chunk(i, d)
                if not first:
                    pool.wait_ge(s_kvm, i * 2 + d - 1)
                t = bass.ds(c * P, P)
                pool.dma_start(q_sb[:, d], z_dram[4:8, :, t].rearrange("a p t -> p a t")).then_inc(s_ld[d], 16)
                pool.dma_start(k_sb[:, d], z_dram[8:12, :, t].rearrange("a p t -> p a t")).then_inc(s_ld[d], 16)
                kv = one(kv_dram[bass.ds(c, 1)])
                pool.dma_start(kt_sb[:, d], kv[:, 0:MW]).then_inc(s_ld[d], 16)
                pool.dma_start(v_sb[:, d, :, 0:DH], kv[:, MW:2 * MW].rearrange("p (h e) -> p h e", h=H)).then_inc(s_ld[d], 16)
                pool.dma_start(g_sb[:, d].rearrange("p h t -> p (h t)"),
                               g_dram[bass.ds(c + NT * d, 1), :].broadcast_to((P, H * P))).then_inc(s_ld[d], 16)

            def ml_store(i, d):
                pool.wait_ge(s_hd, i * 2 + d + 1)
                pool.dma_start(one(h_dram[bass.ds(chunk(i, d) + NT * d, 1)]),
                               h_out[:, d].rearrange("p h e -> p (h e)")).then_inc(s_hst[d], 16)

            for d in range(2):
                ml_load(0, d, True)
            with pool.Fori(1, NT - 1) as i:
                for d in range(2):
                    ml_store(i - 1, d)
                    ml_load(i, d, False)
            for d in range(2):
                ml_store(NT - 2, d)
                ml_load(NT - 1, d, False)
            for d in range(2):
                ml_store(NT - 1, d)
                pool.wait_ge(s_cup, 2 * NT - 1 + d)
                pool.dma_start(new_C[0, 0, d].rearrange("h k v -> k h v"), st_ctx[:, d, :, 0:DH]).then_inc(s_new, 16)
                pool.dma_start(new_n[0, 0, d].rearrange("h k -> k h"), st_ctx[:, d, :, DH], allow_slow_non_contiguous=True).then_inc(s_new, 16)
            pool.dma_start(new_m[0], mnew[0:1, :, NT - 1]).then_inc(s_new, 16)
            pool.wait_ge(s_hst[0], 16 * NT)
            pool.wait_ge(s_hst[1], 16 * NT)

            def hm_load(i, u, first):
                if not first:
                    pool.wait_ge(s_ho, i * 2 + u - 1)
                c = i * 2 + u
                pool.dma_start(hf_sb[:, u, 0], one(h_dram[bass.ds(c, 1)])).then_inc(s_hl[u], 16)
                pool.dma_start(hf_sb[:, u, 1], one(h_dram[bass.ds(c + NT, 1)])).then_inc(s_hl[u], 16)
                pool.dma_start(o_sb[:, u], z_dram[16:20, :, bass.ds(c * P, P)].rearrange("a p t -> p a t")).then_inc(s_hl[u], 16)

            def hm_store(i, u):
                pool.wait_ge(s_ho, i * 2 + u + 1)
                c = i * 2 + u
                pool.dma_start(mix_dram[4:8, :, bass.ds(c * P, P)].rearrange("a p t -> p a t"), ho[:, u]).then_inc(s_host[u], 16)

            for u in range(2):
                hm_load(0, u, True)
            with pool.Fori(1, 4) as i:
                for u in range(2):
                    hm_store(i - 1, u)
                    hm_load(i, u, False)
            hm_store(3, 0)
            hm_load(4, 0, False)
            hm_store(3, 1)
            hm_store(4, 0)
            pool.wait_ge(s_host[0], 80)
            pool.wait_ge(s_host[1], 64)
            pool.wait_ge(s_new, 80)

            def mx(g):
                for k in range(KT):
                    x = KT * g + k
                    if x >= 2:
                        pool.wait_ge(s_mxl, x - 1)
                    pool.dma_start(mx_in[:, k % 2], mix_dram[k, :, g * GW:(g + 1) * GW]).then_inc(s_mx[k % 2], 16)

            merge = z_dram[Z1_UNITS + 4:Z1_UNITS + Z2_UNITS].rearrange("(b c) p t -> c p b t", b=3)

            def mg_load(g, c):
                x = KT * g + c
                if x >= 2:
                    pool.wait_ge(s_ym, 3 * (x - 1))
                pool.dma_start(mg[:, c % 2], merge[c, :, :, g * GW:(g + 1) * GW]).then_inc(s_mg[c % 2], 16)

            def e1(g):
                mg_load(g, 0)
                mg_load(g, 1)
                for c in range(KT):
                    x = KT * g + c
                    for b in (1, 2):
                        pool.wait_ge(s_ym, 3 * x + b + 1)
                        if b == 2:
                            pool.wait_ge(s_ya, 2 * x + 1)
                        pool.tensor_tensor(ya[:, c % 2, 0], ya[:, c % 2, 0], ya[:, c % 2, b], ALU.add).then_inc(s_ya, 1)
                    if c + 2 < KT:
                        mg_load(g, c + 2)

            def ot(g):
                for x in range(6):
                    t, half = divmod(x, 2)
                    pool.wait_ge(s_oe, 6 * g + x + 1)
                    tok = (3 * g + t) * P
                    cols = slice(512 * half, 512 * half + 512)
                    dst = y_sample[0, tok:tok + P, cols] if tok < LAT else y_prompt[0, :, cols]
                    pool.dma_start(dst, o_st[:, half]).then_inc(s_ost[half], 16)

            for stage, w in ORDER:
                if stage == "MX":
                    mx(w)
                elif stage == "E1":
                    e1(w)
                elif stage == "OT":
                    ot(w)
            pool.wait_ge(s_ost[0], 16 * 3 * NG)
            pool.wait_ge(s_ost[1], 16 * 3 * NG)


def _tiles(w, cols=P):
    k, n = w.shape
    u = np.ascontiguousarray(w.reshape(k // P, P, n // cols, cols).transpose(2, 1, 0, 3)).reshape(n // cols, P, k // P * cols)
    return u


def kernel(**inputs):
    import concourse.bacc as _bacc
    from concourse.bass_utils import run_bass_kernel_spmd as _run

    a = {k: np.asarray(v) for k, v in inputs.items()}
    w_in = a["w_in"][0]
    w_proj = np.concatenate([a["w_proj_f"][0], a["w_proj_p"][0], a["w_proj_m"][0]])
    ffn_in = _tiles(a["w_ffn_in"][0])
    ffn_in = np.stack([ffn_in[:FT], ffn_in[FT:]], axis=1).reshape(2 * FT, P, D)
    ffn_out = np.concatenate([
        _tiles(a["w_ffn_out"][0][sum(FO_K[:i]) * P:sum(FO_K[:i + 1]) * P]) if n == 8 else
        np.concatenate([_tiles(a["w_ffn_out"][0][sum(FO_K[:i]) * P:sum(FO_K[:i + 1]) * P]),
                        np.zeros((KT, P, D - n * P), np.float32)], axis=2)
        for i, n in enumerate(FO_K)])
    ffn_out = ffn_out.reshape(3, KT, P, D).transpose(1, 0, 2, 3).reshape(3 * KT, P, D)
    w_stream = np.concatenate([
        _tiles(w_in[:, :O_COL]), _tiles(w_in[:, GATE_COL:GATE_COL + P]), _tiles(w_in[:, O_COL:GATE_COL]),
        _tiles(w_in[:, MERGE_COL:]), _tiles(w_proj), _tiles(a["w_out"][0]), ffn_in, ffn_out])
    vectors = np.concatenate([a["c"].reshape(-1, P), a["c_ctx"].reshape(-1, P), a["b_ada"].reshape(-1, P),
                              a["norm_g"].reshape(-1, P), a["pool_scale"].reshape(-1, P)])
    base, cst, dft = shape_constants()
    ins = {"x_prompt": a["x_prompt"], "x_sample": a["x_sample"], "state_C": a["state_C"], "state_n": a["state_n"],
           "state_m": a["state_m"], "vectors": vectors, "w_ada": _tiles(a["w_ada"][0]), "w_stream": w_stream,
           "b_gate": a["b_gate"], "w_pool": a["w_pool"], "k_base": base, "k_cst": cst, "k_dft": dft}
    outs = [("y_prompt", (1, CTX, D)), ("y_sample", (1, LAT, D)), ("new_C", (1, 1, 2, H, DH, DH)),
            ("new_n", (1, 1, 2, H, DH)), ("new_m", (1, 1, 2, H))]
    nc = _bacc.Bacc("TRN2", target_bir_lowering=False, num_devices=1)
    arrays, args = {}, {}
    for name, v in ins.items():
        arrays[f"in_{name}"] = np.ascontiguousarray(v)
        args[name] = nc.dram_tensor(f"in_{name}", v.shape, F32, kind="ExternalInput").ap()
    for name, shape in outs:
        args[name] = nc.dram_tensor(f"out_{name}", shape, F32, kind="ExternalOutput").ap()
    build(nc, **args)
    r = _run(nc, [arrays], core_ids=[0])
    return tuple(r.results[0][f"out_{name}"] for name, _ in outs)
```

```python
from contextlib import ExitStack

import concourse.bass as bass
import numpy as np
from concourse import mybir

F32 = mybir.dt.float32
F32R = mybir.dt.float32r
ACT = mybir.ActivationFunctionType
ALU = mybir.AluOpType
AX = mybir.AxisListType

P = 128
D = 1024
KT = D // P
LAT, CTX = 1024, 128
T = LAT + CTX
NT = T // P
GW = 384
NG = T // GW
GRID_W = 64
FW = 256
GD = 64
MW = 512
H, DH = 4, 128
ADA_FIRST = 2 * KT
NGC = 16
DFF = 2816
FT = DFF // P
WINDOWS = (2, 4, 8, 16)
EPS = 1e-6
RAW, SPL = 4, 4
NEG = -1e30
NJ = NT * H
C1 = DH + 1

Z1_UNITS = (2 * FW + 3 * MW) // P
O_COL = 2 * FW + 3 * MW
GATE_COL = O_COL + MW
MERGE_COL = GATE_COL + NGC
Z2_UNITS = (MW + 3 * D) // P
ZA_UNITS = 4
U_ZG, U_ZA = Z1_UNITS, Z1_UNITS + 1
U_F = U_ZA + ZA_UNITS
F_UNITS = 2 * (LAT // P) + 1
U_ZB = U_F + F_UNITS
U_E = U_ZB + Z2_UNITS - ZA_UNITS
ZI_T = U_ZA
ZI_G = ZI_T + ZA_UNITS
ZI_M = ZI_G + 4
ZI_C = ZI_M + 2 * (LAT // P)
ZI_H = ZI_C + 2
Z_COUNT = Z1_UNITS + 1 + Z2_UNITS
assert ZI_H + 2 == Z_COUNT
GATE_PHASE = ("Pa0", "z", "Pb0", "Pa1", "z", "Pb1", "Pa2", "z", "Pb2", "z", "G1", "z", "G2", "z", "G3", "z", "G4",
              "z", "G5", "z", "G6", "z", "z", "z", "G7")
E_UNITS = 2 * KT
U_FF = U_E + NG * E_UNITS
FO_K = (8, 7, 7)
FF_UNITS = 2 * FT + len(FO_K) * KT
U_END = U_FF + NG * FF_UNITS

V_C, V_CTX, V_BADA, V_NORM, V_PSC, V_ROWS = 0, 8, 16, 64, 96, 98

CB = {}
_at = 0
for _name, _w in (("rev", P), ("tri_f", P), ("tri_b", P), ("last", P), ("first", P), ("mask_f", P),
                  ("mask_b", P), ("pool", 8 * P), ("pos_r", 4 * 16), ("pos_c", 4 * 64), ("cb", 2 * P)):
    CB[_name] = slice(_at, _at + _w)
    _at += _w
CB_W = _at


def shape_constants():
    c = np.zeros((P, CB_W), np.float32)
    s, t = np.arange(P)[:, None], np.arange(P)[None, :]
    c[:, CB["rev"]] = (s + t == P - 1)
    c[:, CB["tri_f"]] = (s <= t)
    c[:, CB["tri_b"]] = (s >= t)
    c[P - 1, CB["last"]] = 1
    c[0, CB["first"]] = 1
    c[:, CB["mask_f"]] = np.where(s <= t, 0, NEG)
    c[:, CB["mask_b"]] = np.where(s >= t, 0, NEG)
    for kind, width in enumerate((GRID_W, CTX)):
        for g, w in enumerate(WINDOWS):
            m = np.zeros((P, P), np.float64)
            for x in range(P):
                row, pos = x // width * width, x % width
                lo, hi = max(pos - w // 2, 0), min(pos + w - 1 - w // 2, width - 1)
                m[row + lo:row + hi + 1, x] = 1.0 / (hi - lo + 1)
                m[x, x] -= 1.0
            c[:, CB["pool"].start + (kind * 4 + g) * P:][:, :P] = m
    quarter = D // 4
    omega = (np.float32(1.0) / np.float32(10000.0) ** (np.arange(quarter, dtype=np.float32) / np.float32(quarter)))
    for name, n in (("pos_r", 16), ("pos_c", 64)):
        arg = omega.astype(np.float32)[:, None] * np.arange(n, dtype=np.float32)[None, :]
        table = np.concatenate([np.sin(arg), np.cos(arg)]).astype(np.float32)
        c[:, CB[name]] = table.reshape(4, P, n).transpose(1, 0, 2).reshape(P, 4 * n)
    k = np.arange(GD)
    ang = 2 * np.pi * (k[:, None] * k[None, :] % GD) / GD
    for i, m in enumerate((np.cos(ang), -np.sin(ang))):
        for b in range(2):
            at = CB["cb"].start + i * P + b * GD
            c[b * GD:(b + 1) * GD, at:at + GD] = m
    dft = np.zeros((F_UNITS, P, D), np.float32)
    for n in (LAT, CTX):
        k = np.arange(n)
        ang = 2 * np.pi * (k[:, None] * k[None, :] % n) / n
        cs = np.stack([np.cos(ang), np.sin(ang)]) / np.sqrt(float(n) * GD)
        if n == LAT:
            dft[:-1] = cs.reshape(2 * LAT // P, P, LAT)
        else:
            dft[-1, :, :2 * CTX] = np.concatenate([cs[0], cs[1]], axis=1)
    base = np.concatenate([np.eye(P), np.ones((P, P))], axis=1).astype(np.float32)
    return base, c, dft


GD_ABS, GD_LF, GD_AL, GD_SCAN, GD_MCOPY, GD_MTOK = 3, 5, 9, 13, 15, 16
GD_G = GD_MTOK + 1 + 3 + 4 * (NT - 1) + 2 + 2 + 2
GD_LOGS = GD_G + 6
GD_END = GD_LOGS + 1


def build(nc, x_prompt, x_sample, state_C, state_n, state_m, vectors, w_ada, w_stream, b_gate, w_pool,
          k_base, k_cst, k_dft, y_prompt, y_sample, new_C, new_n, new_m):
    z_dram = nc.dram_tensor("z_scratch", (Z1_UNITS + Z2_UNITS, P, T), F32).ap()
    mix_dram = nc.dram_tensor("mix_scratch", (KT, P, T), F32).ap()
    kv_dram = nc.dram_tensor("kv_scratch", (NT, P, 2 * MW), F32).ap()
    x_dram = nc.dram_tensor("x_scratch", (KT, P, T), F32).ap()
    g_dram = nc.dram_tensor("g_scratch", (2 * NT, H * P), F32).ap()
    h_dram = nc.dram_tensor("h_scratch", (2 * NT, P, MW), F32).ap()

    with ExitStack() as top:
        def sb(stack, name, shape, dt=F32):
            return stack.enter_context(nc.sbuf_tensor(name, shape, dt))

        def sem(name):
            return top.enter_context(nc.semaphore(name))

        bank = [top.enter_context(nc.psum_tensor(f"bank{i}", [P, 512], F32)) for i in range(8)]

        raw = sb(top, "raw", [P, RAW, D])
        w_hi = sb(top, "w_hi", [P, SPL, D], F32R)
        w_lo = sb(top, "w_lo", [P, SPL, D], F32R)
        base = sb(top, "base", [P, 2 * P])
        ident, ones = base[:, 0:P], base[:, P:2 * P]
        vec = sb(top, "vec", [P, V_ROWS])
        silu_c = sb(top, "silu_c", [P, KT, 2])
        mod = sb(top, "mod", [P, 48, 2])
        A1 = sb(top, "A1", [P, KT, 2])
        A2 = sb(top, "A2", [P, KT, 2])
        G1 = sb(top, "G1", [P, KT, 2])
        G2 = sb(top, "G2", [P, KT, 2])
        eps = sb(top, "eps", [P, 1])
        acc = sb(top, "acc", [P, GW])
        rstd = sb(top, "rstd", [P, GW])

        s1 = ExitStack()
        cst = sb(s1, "cst", [P, CB_W])
        K = {n: cst[:, s] for n, s in CB.items()}
        s1r = ExitStack()
        rstd1 = sb(s1r, "rstd1", [P, T])
        s1r.close()
        gz = sb(s1, "gz", [P, T])
        s1z = ExitStack()
        ada_b = sb(s1z, "ada_b", [P, 2, D])
        s1z.close()
        z_st = sb(s1, "z_st", [P, 2, T])
        h_hi = sb(s1, "h_hi", [P, KT, T], F32R)
        h_lo = sb(s1, "h_lo", [P, KT, T], F32R)
        s2 = ExitStack()
        xT = sb(s2, "xT", [P, KT, T])
        ada_a = sb(s2, "ada_a", [P, 2, D])
        tmp1 = sb(s2, "tmp1", [P, 4, GW])
        x_in = sb(s2, "x_in", [P, 2, D])
        rows = sb(s2, "rows", [V_ROWS, P])
        s2.close()
        s2 = ExitStack()
        ab_hi = sb(s2, "ab_hi", [P, NT, 2 * FW], F32R)
        ab_lo = sb(s2, "ab_lo", [P, NT, 2 * FW], F32R)
        up = sb(s2, "up", [P, NT, FW])
        s2t = ExitStack()
        zt = sb(s2t, "zt", [P, 3, 4, P])
        kv_st = sb(s2t, "kv_st", [P, 2, MW])
        s2t.close()
        m_st = sb(s2, "m_st", [P, 2, 512])
        pT = sb(s2, "pT", [P, 2, GW])
        wp = sb(s2, "wp", [P, 2, P])
        s2.close()
        s2 = ExitStack()
        st_lat = sb(s2, "st_lat", [P, 2, H, C1])
        st_ctx = sb(s2, "st_ctx", [P, 2, H, C1])
        inter = sb(s2, "inter", [P, 2, H, C1])
        den = sb(s2, "den", [P, 2, H])
        sdec_now = sb(s2, "sdec_now", [P, 2, H])
        bg = sb(s2, "bg", [P, NGC])
        sm = sb(s2, "sm", [P, 2, H])
        gts = sb(s2, "gts", [P, NT, NGC])

        def gate(name):
            return sb(s2, name, [P, 2, NT, H])

        lf, absf, lse, cum, al, mtok, mprev, mnew, gneg, em, sdec, wst, carry, blast, mlast = (
            gate(n) for n in ("lf", "absf", "lse", "cum", "al", "mtok", "mprev", "mnew", "gneg", "em", "sdec",
                              "wst", "carry", "blast", "mlast"))
        mrev = sb(s2, "mrev", [P, NJ])
        rows_a = sb(s2, "rows_a", [NJ, 2, P])
        rows_m = sb(s2, "rows_m", [NJ, 2, P])
        g_rows = sb(s2, "g_rows", [2 * NJ, P])
        s2m = ExitStack()
        q_sb = sb(s2m, "q_sb", [P, 2, H, P])
        k_sb = sb(s2m, "k_sb", [P, 2, H, P])
        kt_sb = sb(s2m, "kt_sb", [P, 2, MW])
        v_sb = sb(s2m, "v_sb", [P, 2, H, C1])
        g_sb = sb(s2m, "g_sb", [P, 2, H, P])
        ew = sb(s2m, "ew", [P, 2, H, P])
        wv = sb(s2m, "wv", [P, 2, H, C1])
        num = sb(s2m, "num", [P, 2, H, C1])
        s2m.close()
        hf_sb = sb(s2, "hf_sb", [P, 2, 2, MW])
        o_sb = sb(s2, "o_sb", [P, 2, H, P])
        hs = sb(s2, "hs", [P, 2, MW])
        ho = sb(s2, "ho", [P, 2, H, P])
        s2.close()
        s1.close()

        s3 = ExitStack()
        xT2 = sb(s3, "xT2", [P, KT, T])
        y2 = sb(s3, "y2", [P, KT, GW])
        h2_hi = sb(s3, "h2_hi", [P, KT, GW], F32R)
        h2_lo = sb(s3, "h2_lo", [P, KT, GW], F32R)
        tmp3 = sb(s3, "tmp3", [P, 4, GW])
        s3a = ExitStack()
        mx_in = sb(s3a, "mx_in", [P, 2, GW])
        mx_hi = sb(s3a, "mx_hi", [P, KT, GW], F32R)
        mx_lo = sb(s3a, "mx_lo", [P, KT, GW], F32R)
        mg = sb(s3a, "mg", [P, 2, 3, GW])
        ya = sb(s3a, "ya", [P, 2, 3, GW])
        yy_hi = sb(s3a, "yy_hi", [P, KT, GW], F32R)
        yy_lo = sb(s3a, "yy_lo", [P, KT, GW], F32R)
        s3a.close()
        o_st = sb(s3, "o_st", [P, 2, 512])
        sa = sb(s3, "sa", [P, 2, GW])
        ff = sb(s3, "ff", [P, 2, GW])
        f_hi = sb(s3, "f_hi", [P, FT, GW], F32R)
        f_lo = sb(s3, "f_lo", [P, FT, GW], F32R)
        s3.close()

        s_raw = [sem(f"raw_landed{i}") for i in range(RAW)]
        s_whi, s_wlo, s_unit = sem("w_hi_ready"), sem("w_lo_ready"), sem("unit_multiplied")
        s_const, s_rows, s_vec, s_vecc, s_silu = (sem(n) for n in ("const_landed", "rows_landed", "vec_transposed",
                                                                   "vec_ready", "silu_ready"))
        s_set = sem("memsets_done")
        s_xin = [sem(f"x_landed{i}") for i in range(2)]
        s_xt, s_xev = sem("x_transposed"), sem("xT_ready")
        s_ada = [sem(f"ada_landed{i}") for i in range(4)]
        s_adam, s_modc, s_mod = sem("ada_multiplied"), sem("mod_chain"), sem("mod_ready")
        s_sq, s_accs, s_st, s_sd, s_rs = (sem(n) for n in ("square_ready", "square_summed", "mean_ready",
                                                           "root_ready", "rstd_ready"))
        s_nx, s_nf, s_nh, s_nl, s_app, s_xs = (
            sem(n) for n in ("norm_scaled", "norm_full", "norm_high", "norm_low", "residual_ready", "x_step"))
        s_zmm, s_zev = sem("z_multiplied"), sem("z_evacuated")
        s_zst = [sem(f"z_stored{i}") for i in range(2)]
        s_zt = [sem(f"zt_landed{i}") for i in range(3)]
        s_spill, s_back = sem("x_spilled"), sem("x_back")
        s_tmm, s_tact, s_tdve = sem("t_transposed"), sem("t_act"), sem("t_dve")
        s_kvst = sem("kv_stored")
        s_fmm = sem("dft_multiplied")
        s_cmm, s_mev = sem("mix_multiplied"), sem("mix_evacuated")
        s_mst = [sem(f"mix_stored{i}") for i in range(2)]
        s_pmm, s_pa, s_pd, s_wp = sem("pooled"), sem("pool_act"), sem("pool_dve"), sem("w_pool_landed")
        s_wp0 = sem("w_pool_zeroed")
        s_gl, s_gp, s_gd, s_ga, s_gst = (sem(n) for n in ("gate_inputs_landed", "gate_pe", "gate_dve", "gate_act",
                                                          "g_rows_stored"))
        s_ld = [sem(f"chunk_landed{i}") for i in range(2)]
        s_st0 = sem("state_landed")
        s_qk, s_int, s_iev, s_t, s_e, s_p, s_wv, s_intra, s_kvm, s_num, s_den, s_hd, s_cup = (
            sem(n) for n in ("scores_ready", "inter_ready", "inter_evacuated", "logw_ready", "expw_ready",
                             "probs_ready", "wv_ready", "intra_ready", "kv_ready", "num_ready", "den_chain",
                             "h_ready", "state_updated"))
        s_sn = sem("decays_ready")
        s_hst = [sem(f"h_stored{i}") for i in range(2)]
        s_hl = [sem(f"h_landed{i}") for i in range(2)]
        s_hs, s_ht, s_ho, s_so = sem("h_summed"), sem("h_transposed"), sem("h_gated"), sem("o_sigmoid_ready")
        s_host = [sem(f"hm_stored{i}") for i in range(2)]
        s_new = sem("new_state_stored")
        s_mx = [sem(f"mx_landed{i}") for i in range(2)]
        s_mxh, s_mxl = sem("mx_high"), sem("mx_low")
        s_mg = [sem(f"merge_landed{i}") for i in range(2)]
        s_sg = sem("merge_sigmoid_ready")
        s_ym, s_ya, s_yh, s_yl = (sem(n) for n in ("branches_gated", "y_summed", "y_high", "y_low"))
        s_e2e = sem("out_evacuated")
        s_sa, s_ff, s_fh, s_fl = (sem(n) for n in ("silu_a_ready", "f_ready", "f_high", "f_low"))
        s_foe = sem("ffn_out_evacuated")
        s_ot, s_oe = sem("out_transposed"), sem("out_staged")
        s_ost = [sem(f"out_stored{i}") for i in range(2)]

        ORDER = [("ADA", 0), ("SQ", "h0"), ("ADA", 1), ("ST", "h0"), ("SQ", "h1"), ("ADA", 2), ("ST", "h1"),
                 ("SQ", "h2"), ("ADA", 3), ("ST", "h2"), ("MOD", None), ("HN", "h0"), ("HN", "h1"), ("HN", "h2"),
                 ("MIX", None),
                 ("MX", 0), ("E1", 0), ("MX", 1), ("E2", 0), ("SQ", "y0"), ("E1", 1), ("ST", "y0"), ("X", "y0"),
                 ("MX", 2), ("SQ", "x0"), ("E2", 1), ("ST", "x0"), ("HN", "x0"), ("SQ", "y1"), ("E1", 2),
                 ("ST", "y1"), ("X", "y1"), ("E2", 2), ("SQ", "y2"), ("FI", 0), ("ST", "y2"), ("X", "y2"),
                 ("SQ", "x1"), ("ST", "x1"), ("FO", 0), ("HN", "x1"), ("SQ", "o0"), ("FI", 1), ("ST", "o0"),
                 ("X", "o0"), ("OT", 0), ("SQ", "x2"), ("ST", "x2"), ("FO", 1), ("HN", "x2"), ("SQ", "o1"),
                 ("FI", 2), ("ST", "o1"), ("X", "o1"), ("OT", 1), ("FO", 2), ("SQ", "o2"), ("ST", "o2"),
                 ("X", "o2"), ("OT", 2)]
        number = {}
        tmp_at, uses = {}, 0
        for stage, which in ORDER:
            if stage in ("SQ", "ST", "HN", "X"):
                number[stage, which] = sum(1 for k in number if k[0] == stage)
                if stage in ("SQ", "HN"):
                    tmp_at[stage, which] = uses
                    uses += KT
        apply_order = [(s, w) for s, w in ORDER if s in ("HN", "X")]

        def wait_applied(eng, n):
            s, w = apply_order[n - 1]
            if s == "HN":
                eng.wait_ge(s_nl, KT * (number[s, w] + 1))
            else:
                eng.wait_ge(s_app, number[s, w] + 1)

        def wait_x(eng, which):
            eng.wait_ge(s_app, number["X", which] + 1)

        def wait_tmp(eng, m):
            for (stage, w), at in tmp_at.items():
                if at <= m - 4 < at + KT:
                    n = KT * number[stage, w] + m - 4 - at + 1
                    eng.wait_ge(s_accs if stage == "SQ" else s_nl, n)

        def halves(g):
            return [(0, GW, 0)] if g < NG - 1 else [(0, LAT - g * GW, 0), (LAT - g * GW, GW, 1)]

        def source(which):
            g = int(which[1])
            if which[0] in "yo":
                return y2[:, :, :]
            return (xT if which[0] == "h" else xT2)[:, :, g * GW:(g + 1) * GW]

        def tmp_of(which):
            return tmp1 if which[0] == "h" else tmp3

        def rstd_of(which):
            return rstd1[:, int(which[1]) * GW:(int(which[1]) + 1) * GW] if which[0] == "h" else rstd[:, :]

        def ada_slot(slot):
            return (ada_a if slot < 2 else ada_b)[:, slot % 2]

        def wait_source(eng, which):
            kind, g = which[0], int(which[1])
            if kind == "h":
                eng.wait_ge(s_xev, 2 * min(3 * (g + 1), NT))
            elif kind == "y":
                eng.wait_ge(s_e2e, KT * (g + 1))
            elif kind == "o":
                eng.wait_ge(s_foe, KT * (g + 1))
            else:
                wait_x(eng, f"y{g}")

        def mm3(pe, out, a_hi, a_lo, b_hi, b_lo, start, stop):
            pe.matmul(out, a_hi, b_hi, start=start, stop=False)
            pe.matmul(out, a_hi, b_lo, start=False, stop=False)
            return pe.matmul(out, a_lo, b_hi, start=False, stop=stop)

        def b3(ap, n):
            return ap.unsqueeze(1).broadcast_to((ap.shape[0], n, ap.shape[1]))

        def last(ap, n):
            return ap.unsqueeze(len(ap.shape)).broadcast_to(tuple(ap.shape) + (n,))

        def ktile(k):
            return slice(k * P, (k + 1) * P)

        def e_unit(g, c):
            return U_E + E_UNITS * g + c

        def f_unit(g, c):
            return U_FF + FF_UNITS * g + c

        def slot_count(n, n0):
            if isinstance(n, int):
                return 16 * (n // RAW + 1)
            return (n - n0) * (16 // RAW) + 16 * (n0 // RAW + 1)

        def chunk(i, d):
            if isinstance(i, int) and i == NT - 1:
                return i
            return i if d == 0 else i * -1 + (NT - 2)

        def gcol(a, d, c, h):
            return a[:, d, :, h][:, c:c + 1] if isinstance(c, int) else a[:, d, :, h][:, bass.ds(c, 1)]

        def grow(a, d, c):
            return a[:, d, c] if isinstance(c, int) else a[:, d, bass.ds(c, 1), :].rearrange("p a h -> p (a h)")

        def z_row(zi):
            return zi - 1

        def dft_place(x):
            if x < 4:
                j, lh = divmod(x, 2)
                return mix_dram[j, :, 512 * lh:512 * lh + 512], bank[x][:, :]
            return mix_dram[0:2, :, LAT:T].rearrange("a p t -> p a t"), bank[6][:, 0:2 * P]

        block = top.enter_context(nc.Block())

        @block.sync
        def _(sp):
            sp.dma_start(base[:], k_base).then_inc(s_const, 16)
            sp.dma_start(cst[:], k_cst).then_inc(s_const, 16)
            sp.dma_start(rows[:], vectors).then_inc(s_rows, 16)

            def load_ada(j, slot, before):
                if before is not None:
                    sp.wait_ge(s_adam, before + 1)
                sp.dma_start(ada_slot(slot), w_ada[bass.ds(j, 1)].rearrange("a p n -> (a p) n")).then_inc(s_ada[slot], 16)

            for j in range(4):
                load_ada(j, j, None)
            with sp.Fori(1, ADA_FIRST // 4) as i:
                for u in range(4):
                    load_ada(i * 4 + u, u, i * 4 + (u - 4))

            def unit(n, slot, src, first=False):
                if not first:
                    sp.wait_ge(s_whi, n - RAW + 1)
                    sp.wait_ge(s_wlo, n - RAW + 1)
                sp.dma_start(raw[:, slot], src.rearrange("a p n -> (a p) n")).then_inc(s_raw[slot], 16)

            def units(n0, src, s0, count):
                with sp.Fori(0, count // RAW) as i:
                    for u in range(RAW):
                        unit(i * RAW + n0 + u, (n0 + u) % RAW, src[bass.ds(i * RAW + s0 + u, 1)])

            for u in range(RAW):
                unit(u, u, w_stream[u:u + 1], True)
            for u in range(2):
                load_ada(ADA_FIRST + u, u, ADA_FIRST + u - 4)

            def unit_and_ada(i, us):
                for u in us:
                    n = i * RAW + (u + RAW)
                    unit(n, u, w_stream[bass.ds(n, 1)])
                    for v in range(2):
                        j = i * (2 * RAW) + (ADA_FIRST + 2 * u + 2 + v)
                        load_ada(j, v, j - 2)

            with sp.Fori(0, Z1_UNITS // RAW - 1) as i:
                unit_and_ada(i, range(RAW))
            unit_and_ada(Z1_UNITS // RAW - 1, range(RAW - 1))
            for n in range(Z1_UNITS + RAW - 1, U_F):
                unit(n, n % RAW, w_stream[n:n + 1])
            units(U_F, k_dft, 0, F_UNITS - 1)
            unit(U_ZB - 1, (U_ZB - 1) % RAW, k_dft[F_UNITS - 1:F_UNITS])
            units(U_ZB, w_stream, U_F, Z2_UNITS - ZA_UNITS)
            with sp.Fori(0, NG) as g:
                for i in range(E_UNITS // RAW):
                    for u in range(RAW):
                        m = i * RAW + u
                        unit(g * E_UNITS + U_E + m, (U_E + m) % RAW, w_stream[Z_COUNT + m:Z_COUNT + m + 1])
            with sp.Fori(0, NG) as g:
                with sp.Fori(0, FF_UNITS // RAW) as i:
                    for u in range(RAW):
                        unit(g * FF_UNITS + i * RAW + U_FF + u, (U_FF + u) % RAW,
                             w_stream[bass.ds(i * RAW + Z_COUNT + E_UNITS + u, 1)])

        @block.tensor
        def _(pe):
            def unit_ready(n):
                pe.wait_ge(s_wlo, n + 1)

            def W(slot, k):
                return w_hi[:, slot, ktile(k)], w_lo[:, slot, ktile(k)]

            pe.wait_ge(s_const, 32)
            pe.wait_ge(s_rows, 16)
            pe.transpose(bank[4][:, 0:V_ROWS], rows[:, :], ident[0:V_ROWS, 0:V_ROWS]).then_inc(s_vec, 1)

            def x_pair(base_i, first, n):
                for u in range(n):
                    pe.wait_ge(s_xin[u], base_i * 16 + 16)
                    if not first:
                        pe.wait_ge(s_xev, base_i * 4 + 2 * u - 2)
                    for k in range(KT):
                        m = pe.transpose(bank[2 * u + k // 4][:, ktile(k % 4)], x_in[:, u, ktile(k)], ident)
                        if k % 4 == 3:
                            m.then_inc(s_xt, 1)

            x_pair(0, True, 2)
            with pe.Fori(1, 4) as i:
                x_pair(i, False, 2)
            x_pair(4, False, 1)

            def ada_tile(j, slot, landed):
                pe.wait_ge(s_ada[slot], landed)
                for k in range(KT):
                    m = pe.matmul(bank[5][:, bass.ds(j * 2, 2)], ada_slot(slot)[:, ktile(k)], silu_c[:, k, :],
                                  start=k == 0, stop=k == KT - 1)
                m.then_inc(s_adam, 1)

            def ada(q):
                if q == 0:
                    pe.wait_ge(s_silu, 1)
                for u in range(4):
                    ada_tile(4 * q + u, u, 16 * (q + 1))

            def stat(which):
                q = number["ST", which]
                pe.wait_ge(s_accs, KT * (q + 1))
                if which == "h0":
                    pe.wait_ge(s_const, 32)
                if q:
                    pe.wait_ge(s_sd, q)
                pe.matmul(bank[7][:, 0:GW], ones, acc[:, :], start=True, stop=True).then_inc(s_st, 1)

            def z_part(zi, zi0, shift, b, first=False):
                if b == 0:
                    unit_ready(zi + shift)
                j = 3 * zi0 + b
                if first and zi0 == 0:
                    pe.wait_ge(s_nl, KT * (b + 1))
                if not (first and j < 4):
                    pe.wait_ge(s_zev, zi * 3 + b - 3)
                for k in range(KT):
                    wh, wl = W((zi0 + shift) % SPL, k)
                    r = slice(b * GW, (b + 1) * GW)
                    m = mm3(pe, bank[j % 4][:, 0:GW], wh, wl, h_hi[:, k, r], h_lo[:, k, r], k == 0, k == KT - 1)
                m.then_inc(s_unit if b == NG - 1 else s_zmm, 1)

            def z_unit(zi, zi0, first):
                for b in range(NG):
                    z_part(zi, zi0, 0, b, first)
                    if b < 2:
                        ada_tile(zi * 2 + (ADA_FIRST + b), b, zi * 16 + 16 * (ADA_FIRST // 4 + 1))

            def project():
                for u in range(4):
                    z_unit(u, u, True)
                with pe.Fori(1, Z1_UNITS // 4) as i:
                    for u in range(4):
                        z_unit(i * 4 + u, u, False)
                for b in range(NG):
                    z_part(U_ZG, U_ZG, 0, b)

            def t_tile(c):
                pe.wait_ge(s_zt[0], 16 * (c + 1))
                if c == 0:
                    pe.wait_ge(s_mod, 2)
                if c:
                    pe.wait_ge(s_tact, 2 * c)
                    pe.wait_ge(s_tdve, 3 * c)
                for j in range(2):
                    m = pe.matmul(bank[4][:, FW * j:FW * (j + 1)], zt[:, 0, j, :], K["cb"], start=True, stop=True)
                m.then_inc(s_tmm, 1)
                for j in range(2):
                    m = pe.transpose(bank[5][:, ktile(j)], zt[:, 0, 2 + j, :], ident)
                m.then_inc(s_tmm, 1)
                for piece in (1, 2):
                    pe.wait_ge(s_zt[piece], 16 * (c + 1))
                    for k in range(4):
                        m = pe.transpose(bank[5 + piece][:, ktile(k)], zt[:, piece, k, :], ident)
                    m.then_inc(s_tmm, 1)

            def token_major():
                for q in range(ZA_UNITS):
                    for b in range(NG):
                        z_part(ZI_T + q, ZI_T + q, 0, b)
                    t_tile(2 * q)
                    t_tile(2 * q + 1)
                t_tile(NT - 1)

            def fourier():
                pe.wait_ge(s_tdve, 3 * NT)
                pe.wait_ge(s_zev, 3 * ZI_G)
                for i in range(2 * (LAT // P)):
                    n = U_F + i
                    unit_ready(n)
                    cs, tt = divmod(i, LAT // P)
                    for j in range(2):
                        c = slice(FW * j + P * cs, FW * j + P * (cs + 1))
                        for lh in range(2):
                            r = slice(lh * 512, (lh + 1) * 512)
                            m = mm3(pe, bank[2 * j + lh][:, :], ab_hi[:, tt, c], ab_lo[:, tt, c],
                                    w_hi[:, n % SPL, r], w_lo[:, n % SPL, r], i == 0, i == 2 * (LAT // P) - 1)
                            if i == 2 * (LAT // P) - 1 and (j, lh) != (1, 1):
                                m.then_inc(s_fmm, 1)
                    m.then_inc(s_unit, 1)
                n = U_F + F_UNITS - 1
                unit_ready(n)
                for j in range(2):
                    for cs in range(2):
                        c = slice(FW * j + P * cs, FW * j + P * (cs + 1))
                        m = mm3(pe, bank[6][:, ktile(j)], ab_hi[:, NT - 1, c], ab_lo[:, NT - 1, c],
                                w_hi[:, n % SPL, ktile(cs)], w_lo[:, n % SPL, ktile(cs)], cs == 0, cs == 1)
                m.then_inc(s_unit, 1)

            def pool_a(g):
                if g:
                    pe.wait_ge(s_pa, g)
                    pe.wait_ge(s_pd, g)
                for i in range(3 * g, 3 * g + 3):
                    kind = int(i == NT - 1)
                    for w in range(4):
                        o = bank[4 + w // 2][GD * (w % 2):GD * (w % 2) + GD, ktile(i - 3 * g)]
                        m = pe.matmul(o, up[:, i, GD * w:GD * (w + 1)],
                                      K["pool"][:, (4 * kind + w) * P:(4 * kind + w + 1) * P],
                                      start=True, stop=True)
                m.then_inc(s_pmm, 1)

            def pool_b(g):
                if g == 0:
                    pe.wait_ge(s_wp, 16 * 4)
                pe.wait_ge(s_pa, g + 1)
                pe.wait_ge(s_pd, g + 1)
                for j in range(2):
                    pe.wait_ge(s_mev, 5 if g == 0 else 5 + 2 * g - 1 + j)
                    pe.matmul(bank[6 + j][:, 0:GW], wp[:, j, :], pT[:, j, :], start=True,
                              stop=True).then_inc(s_cmm, 1)

            flat, half = "p d c h -> p (d c h)", "p c h -> p (c h)"

            def gates(step):
                if step == 1:
                    pe.wait_ge(s_pa, NG)
                    pe.wait_ge(s_pd, NG)
                    pe.wait_ge(s_mev, 5 + 2 * NG)
                    for i in range(NT):
                        m = pe.matmul(bank[4][:, NGC * i:NGC * (i + 1)], gz[0:NGC, ktile(i)], ident[0:NGC, 0:NGC],
                                      start=True, stop=True)
                elif step == 2:
                    pe.wait_ge(s_gd, GD_LF)
                    pe.matmul(bank[5][:, 0:NJ], K["tri_f"], lf[:, 0].rearrange(half), start=True, stop=True)
                    pe.matmul(bank[5][:, NJ:2 * NJ], K["tri_b"], lf[:, 1].rearrange(half), start=True, stop=True)
                    m = pe.matmul(bank[6][:, 0:2 * NJ], ones, lf[:].rearrange(flat), start=True, stop=True)
                elif step == 3:
                    pe.wait_ge(s_gd, GD_AL)
                    pe.matmul(bank[4][0:NJ, 0:P], al[:, 0].rearrange(half), ident, start=True, stop=True)
                    m = pe.matmul(bank[7][0:NJ, 0:P], al[:, 1].rearrange(half), K["rev"], start=True, stop=True)
                elif step == 4:
                    pe.wait_ge(s_gd, GD_SCAN)
                    pe.matmul(bank[5][:, 0:NJ], rows_m[:, 0, :], ident[0:NJ, 0:NJ], start=True, stop=True)
                    m = pe.matmul(bank[6][:, 0:NJ], rows_m[:, 1, :], ident[0:NJ, 0:NJ], start=True, stop=True)
                elif step == 5:
                    pe.wait_ge(s_gd, GD_MCOPY)
                    m = pe.matmul(bank[4][:, 0:NJ], K["rev"], mrev[:, :], start=True, stop=True)
                elif step == 6:
                    pe.wait_ge(s_gd, GD_MTOK)
                    pe.matmul(bank[7][:, 0:NJ], K["last"], mtok[:, 0].rearrange(half), start=True, stop=True)
                    m = pe.matmul(bank[7][:, NJ:2 * NJ], K["first"], mtok[:, 1].rearrange(half), start=True,
                                  stop=True)
                else:
                    pe.wait_ge(s_gd, GD_G)
                    m = pe.matmul(bank[5][0:2 * NJ, 0:P], gneg[:].rearrange(flat), ident, start=True, stop=True)
                m.then_inc(s_gp, 1)

            def pooling_and_gates():
                part = 0
                for what in GATE_PHASE:
                    if what == "z":
                        zi = ZI_G + part // NG
                        if part == 0:
                            pe.wait_ge(s_mev, 4)
                        z_part(zi, zi, F_UNITS, part % NG)
                        part += 1
                    elif what[0] == "G":
                        gates(int(what[1]))
                    elif what[1] == "a":
                        pool_a(int(what[2]))
                    else:
                        pool_b(int(what[2]))

            def ml_scores(i, d, st, first):
                x = i * 2 + d
                pe.wait_ge(s_ld[d], i * 80 + 80)
                if not (first and d == 0):
                    pe.wait_ge(s_num, x)
                    pe.wait_ge(s_cup, x)
                for h in range(H):
                    m = pe.matmul(bank[4][:, ktile(h)], k_sb[:, d, h, :], q_sb[:, d, h, :], start=True, stop=True)
                m.then_inc(s_qk, 1)
                for h in range(H):
                    m = pe.matmul(bank[5 + h // 2][:, C1 * (h % 2):C1 * (h % 2 + 1)], q_sb[:, d, h, :],
                                  st[:, d, h, :], start=True, stop=True)
                m.then_inc(s_int, 1)

            def ml_values(i, d):
                pe.wait_ge(s_p, i * 2 + d + 1)
                for h in range(H):
                    m = pe.matmul(bank[7 if h < 2 else 4][:, C1 * (h % 2):C1 * (h % 2 + 1)], ew[:, d, h, :],
                                  v_sb[:, d, h, :], start=True, stop=True)
                m.then_inc(s_intra, 1)

            def ml_state(i, d):
                pe.wait_ge(s_wv, i * 2 + d + 1)
                pe.wait_ge(s_iev, i * 2 + d + 1)
                for h in range(H):
                    m = pe.matmul(bank[5 + h // 2][:, C1 * (h % 2):C1 * (h % 2 + 1)], kt_sb[:, d, ktile(h)],
                                  wv[:, d, h, :], start=True, stop=True)
                m.then_inc(s_kvm, 1)

            def ml_step(i, d, st, first, zi, zi0):
                z_part(zi, zi0, F_UNITS, 0)
                ml_scores(i, d, st, first)
                z_part(zi, zi0, F_UNITS, 1)
                ml_values(i, d)
                z_part(zi, zi0, F_UNITS, 2)
                ml_state(i, d)

            def mlstm():
                def turn(t, first):
                    for s in range(2):
                        for d in range(2):
                            ml_step(t * 2 + s, d, st_lat, first and s == 0, t * 4 + (ZI_M + 2 * s + d),
                                    ZI_M + 2 * s + d)

                pe.wait_ge(s_st0, 64)
                pe.wait_ge(s_set, 3)
                turn(0, True)
                with pe.Fori(1, (NT - 1) // 2) as t:
                    turn(t, False)
                for d in range(2):
                    ml_step(NT - 1, d, st_ctx, False, ZI_C + d, ZI_C + d)

            def hm():
                for part in range(2 * NG):
                    z_part(ZI_H + part // NG, ZI_H + part // NG, F_UNITS, part % NG)
                    if part == 0:
                        pe.wait_ge(s_num, 2 * NT)
                        pe.wait_ge(s_cup, 2 * NT)
                    for c in range(2 * part, min(2 * part + 2, NT)):
                        pe.wait_ge(s_hs, c + 1)
                        if c >= 2:
                            pe.wait_ge(s_ho, c - 1)
                        for h in range(H):
                            m = pe.transpose(bank[6 + c % 2][:, ktile(h)], hs[:, c % 2, ktile(h)], ident)
                        m.then_inc(s_ht, 1)

            def mixers():
                token_major()
                fourier()
                pooling_and_gates()
                mlstm()
                hm()

            def e1(g):
                if g == 0:
                    pe.wait_ge(s_zev, 3 * Z_COUNT)
                if g:
                    pe.wait_ge(s_sd, number["ST", "h2"] + 1)

                def one(c, c0, first):
                    n = c + (U_E + g * E_UNITS)
                    unit_ready(n)
                    if not (first and c0 < 2):
                        pe.wait_ge(s_ym, c * 3 + (3 * KT * g - 3))
                    for b, ks in enumerate(((0, 1), (2, 3), (4, 5, 6, 7))):
                        for k in ks:
                            if c0 == 0:
                                pe.wait_ge(s_mxl, KT * g + k + 1)
                            wh, wl = W((U_E + c0) % SPL, k)
                            m = mm3(pe, bank[3 * (c0 % 2) + b][:, 0:GW], wh, wl, mx_hi[:, k, :], mx_lo[:, k, :],
                                    k == ks[0], k == ks[-1])
                    m.then_inc(s_unit, 1)

                for c in range(4):
                    one(c, c, g == 0)
                for c in range(4, 8):
                    one(c, c, False)

            def e2(g):
                pe.wait_ge(s_yl, KT * (g + 1))
                pe.wait_ge(s_sd, max(q + 1 for (s, w), q in number.items() if s == "ST" and
                                     ORDER.index((s, w)) < ORDER.index(("E2", g))))
                for c in range(KT):
                    n = U_E + g * E_UNITS + KT + c
                    unit_ready(n)
                    if g or c >= 2:
                        pe.wait_ge(s_e2e, KT * g + c - 1)
                    for k in range(KT):
                        wh, wl = W(n % SPL, k)
                        m = mm3(pe, bank[6 + c % 2][:, 0:GW], wh, wl, yy_hi[:, k, :], yy_lo[:, k, :], k == 0,
                                k == KT - 1)
                    m.then_inc(s_unit, 1)

            def fi(g):
                pe.wait_ge(s_nl, KT * (number["HN", f"x{g}"] + 1))
                if g == 0:
                    pe.wait_ge(s_ym, 3 * KT * NG)
                n0 = U_FF + g * FF_UNITS

                def turn(i, first):
                    for u in range(4):
                        unit_ready(i * 4 + (n0 + u))
                        if not (first and g == 0):
                            if u % 2 == 0:
                                pe.wait_ge(s_sa, i * 2 + (FT * g + u // 2 - 1))
                            else:
                                pe.wait_ge(s_ff, i * 2 + (FT * g + u // 2 - 1))
                        for k in range(KT):
                            wh, wl = W((n0 + u) % SPL, k)
                            m = mm3(pe, bank[u][:, 0:GW], wh, wl, h2_hi[:, k, :], h2_lo[:, k, :], k == 0,
                                    k == KT - 1)
                        m.then_inc(s_unit, 1)

                turn(0, True)
                with pe.Fori(1, FT // 2) as i:
                    turn(i, False)

            def fo(g):
                pe.wait_ge(s_fl, FT * (g + 1))
                n0 = U_FF + g * FF_UNITS + 2 * FT

                def turn(i, first):
                    for c in range(4):
                        if not (first and c < 2 and g == 0):
                            pe.wait_ge(s_foe, i * 4 + (KT * g + c - 1))
                        k0 = 0
                        for part, nk in enumerate(FO_K):
                            u = 3 * c + part
                            unit_ready(i * 12 + (n0 + u))
                            for k in range(nk):
                                wh, wl = W((n0 + u) % SPL, k)
                                m = mm3(pe, bank[4 + c % 2][:, 0:GW], wh, wl, f_hi[:, k0 + k, :],
                                        f_lo[:, k0 + k, :], k0 + k == 0, k0 + k == FT - 1)
                            k0 += nk
                            m.then_inc(s_unit, 1)

                turn(0, True)
                turn(1, False)

            def ot(g):
                wait_x(pe, f"o{g}")
                for x in range(6):
                    t, half = divmod(x, 2)
                    if g or x >= 2:
                        pe.wait_ge(s_oe, 6 * g + x - 1)
                    for k in range(4):
                        m = pe.transpose(bank[6 + half][:, ktile(k)], y2[:, 4 * half + k, ktile(t)], ident)
                    m.then_inc(s_ot, 1)

            pe.wait_ge(s_vecc, 1)
            for stage, w in ORDER:
                if stage == "ADA":
                    ada(w)
                elif stage == "ST":
                    turned = sum(s == "OT" for s, _ in ORDER[:ORDER.index((stage, w))])
                    projected = sum(s == "E2" for s, _ in ORDER[:ORDER.index((stage, w))])
                    if projected:
                        pe.wait_ge(s_e2e, KT * projected)
                    if turned:
                        pe.wait_ge(s_oe, 6 * turned)
                    stat(w)
                elif stage == "MIX":
                    project()
                    mixers()
                elif stage == "E1":
                    e1(w)
                elif stage == "E2":
                    e2(w)
                elif stage == "FI":
                    fi(w)
                elif stage == "FO":
                    fo(w)
                elif stage == "OT":
                    pe.wait_ge(s_sd, max(q + 1 for (s, v), q in number.items() if s == "ST" and
                                         ORDER.index((s, v)) < ORDER.index(("OT", w))))
                    ot(w)

        @block.scalar
        def _(act):
            def split(n, n0):
                slot = n0 % RAW
                act.wait_ge(s_raw[slot], slot_count(n, n0))
                if not (isinstance(n, int) and n < SPL):
                    act.wait_ge(s_unit, n - SPL + 1)
                act.copy(w_hi[:, slot], raw[:, slot]).then_inc(s_whi, 1)

            def silu_vectors():
                act.wait_ge(s_vecc, 1)
                act.activation(silu_c[:].rearrange("p k v -> p v k"),
                               vec[:, V_C:V_C + 2 * KT].rearrange("p (v k) -> p v k", v=2), ACT.Silu).then_inc(s_silu, 1)

            def sq(which):
                q, m0, tmp = number["SQ", which], tmp_at["SQ", which], tmp_of(which)
                src = source(which)
                wait_source(act, which)
                for j in range(KT):
                    m = m0 + j
                    if m >= 4:
                        wait_tmp(act, m)
                    act.activation(tmp[:, m % 4], src[:, j], ACT.Square).then_inc(s_sq, 1)

            def stat(which):
                q = number["ST", which]
                act.wait_ge(s_st, q + 1)
                if q == 0:
                    act.wait_ge(s_set, 1)
                if q > NG:
                    wait_applied(act, q)
                act.activation(rstd_of(which), bank[7][:, 0:GW], ACT.Sqrt, bias=eps[:, 0:1], scale=1.0 / D).then_inc(s_sd, 1)

            def hn(which):
                q, m0, tmp, g = number["HN", which], tmp_at["HN", which], tmp_of(which), int(which[1])
                first = which[0] == "h"
                scale, shift = (A1, mod[:, 0:8]) if first else (A2, mod[:, 24:32])
                if which == "h0":
                    act.wait_ge(s_mod, 1)
                if which == "x0":
                    act.wait_ge(s_mod, 2)
                if not first and g:
                    act.wait_ge(s_unit, f_unit(g - 1, 2 * FT))
                if which == "x0":
                    act.wait_ge(s_host[0], 80)
                    act.wait_ge(s_host[1], 64)
                nf = KT * q + sum(len(halves(int(w[1]))) * KT - KT for w in [w for s, w in ORDER if s == "HN"][:q])
                for j in range(KT):
                    t = tmp[:, (m0 + j) % 4]
                    act.wait_ge(s_nx, KT * q + j + 1)
                    for a, b, col in halves(g):
                        act.activation(t[:, a:b], t[:, a:b], ACT.Identity, bias=shift[:, j, col:col + 1],
                                       scale=scale[:, j, col:col + 1]).then_inc(s_nf, 1)
                        nf += 1
                    act.wait_ge(s_nf, nf)
                    out = h_hi[:, j, g * GW:(g + 1) * GW] if first else h2_hi[:, j]
                    act.copy(out, t).then_inc(s_nh, 1)

            def z_evac(zi, zi0, shift, b, scale=1.0):
                z, z0 = (zi, zi0) if zi0 < U_ZG else (z_row(zi), z_row(zi0))
                if b == NG - 1:
                    act.wait_ge(s_unit, zi + (shift + 1))
                else:
                    act.wait_ge(s_zmm, zi * 2 + (b + 1))
                if b == 0 and z0 >= 2:
                    act.wait_ge(s_zst[z0 % 2], 16 * (z // 2) if isinstance(z, int) else (z - z0) * 8 + 16 * (z0 // 2))
                act.activation(z_st[:, z0 % 2, b * GW:(b + 1) * GW], bank[(3 * zi0 + b) % 4][:, 0:GW],
                               ACT.Copy, scale=scale).then_inc(s_zev, 1)
                if b == NG - 1:
                    act.wait_ge(s_zev, zi * 3 + 3)
                    act.dma_start(z_dram[bass.ds(z, 1)].rearrange("a p n -> (a p) n"), z_st[:, z0 % 2]).then_inc(s_zst[z0 % 2], 16)

            def z_unit(zi, zi0, shift, scale=1.0):
                split(zi + (shift + 2), zi0 + shift + 2)
                for b in range(NG):
                    z_evac(zi, zi0, shift, b, scale)

            def project():
                for zi in range(Z1_UNITS):
                    z_unit(zi, zi, 0, DH ** -0.5 if 8 <= zi < 12 else 1.0)
                split(U_ZG + 2, U_ZG + 2)
                for b in range(NG):
                    if b == NG - 1:
                        act.wait_ge(s_unit, U_ZG + 1)
                    else:
                        act.wait_ge(s_zmm, 2 * U_ZG + b + 1)
                    act.copy(gz[:, b * GW:(b + 1) * GW], bank[(3 * U_ZG + b) % 4][:, 0:GW]).then_inc(s_zev, 1)

            def t_tile(c):
                act.wait_ge(s_tmm, 4 * c + 1)
                act.copy(ab_hi[:, c], bank[4][:, :]).then_inc(s_tact, 1)
                act.wait_ge(s_tmm, 4 * c + 3)
                if c:
                    act.wait_ge(s_kvst, 16 * c)
                act.copy(kv_st[:, 0], bank[6][:, :]).then_inc(s_tact, 1)

            def pool_a(g):
                act.wait_ge(s_pmm, g + 1)
                if g:
                    act.wait_ge(s_cmm, 2 * g)
                act.copy(pT[:, 0], bank[4][:, 0:GW]).then_inc(s_pa, 1)

            def pool_b(g):
                for j in range(2):
                    x = 5 + 2 * g + j
                    act.wait_ge(s_cmm, x - 4)
                    act.wait_ge(s_mst[x % 2], 16 * (x // 2))
                    act.activation(m_st[:, x % 2, 0:GW], bank[6 + j][:, 0:GW], ACT.Copy,
                                   scale=vec[:, V_PSC + j:V_PSC + j + 1]).then_inc(s_mev, 1)

            def mixers():
                for q in range(ZA_UNITS):
                    z_unit(ZI_T + q, ZI_T + q, 0)
                    t_tile(2 * q)
                    t_tile(2 * q + 1)
                t_tile(NT - 1)
                for i in range(F_UNITS):
                    split(U_F + i + 2, U_F + i + 2)
                for x in range(5):
                    if x in (3, 4):
                        act.wait_ge(s_unit, U_F + 2 * (LAT // P) + x - 3)
                    else:
                        act.wait_ge(s_fmm, x + 1)
                    if x == 0:
                        act.wait_ge(s_kvst, 16 * NT)
                    if x >= 2:
                        act.wait_ge(s_mst[x % 2], 16 * (x // 2))
                    _, ps = dft_place(x)
                    act.copy(m_st[:, x % 2, 0:ps.shape[1]], ps).then_inc(s_mev, 1)
                flat = "p d c h -> p (d c h)"
                part = 0
                for what in GATE_PHASE:
                    if what == "z":
                        zi = ZI_G + part // NG
                        if part % NG == 0:
                            split(zi + F_UNITS + 2, zi + F_UNITS + 2)
                        z_evac(zi, zi, F_UNITS, part % NG)
                        part += 1
                    elif what[:2] == "Pa":
                        pool_a(int(what[2]))
                    elif what[:2] == "Pb":
                        pool_b(int(what[2]))
                    elif what == "G1":
                        act.wait_ge(s_gd, GD_ABS)
                        act.activation(lse[:].rearrange(flat), absf[:].rearrange(flat), ACT.Exp, scale=-1.0).then_inc(s_ga, 1)
                        act.wait_ge(s_ga, 1)
                        act.activation(lse[:].rearrange(flat), lse[:].rearrange(flat), ACT.Ln, bias=1.0).then_inc(s_ga, 1)
                    elif what == "G7":
                        act.wait_ge(s_gd, GD_LOGS)
                        for a in (em, sdec, wst, carry):
                            act.activation(a[:].rearrange(flat), a[:].rearrange(flat), ACT.Exp).then_inc(s_ga, 1)
                        act.wait_ge(s_ga, 6)

                def turn(t):
                    for s in range(2):
                        for d in range(2):
                            ml_step(t * 2 + s, d, t * 4 + (ZI_M + 2 * s + d), ZI_M + 2 * s + d)

                turn(0)
                with act.Fori(1, (NT - 1) // 2) as t:
                    turn(t)
                for d in range(2):
                    ml_step(NT - 1, d, ZI_C + d, ZI_C + d)
                for part in range(2 * NG):
                    zi = ZI_H + part // NG
                    if part % NG == 0:
                        split(zi + F_UNITS + 2, zi + F_UNITS + 2)
                    z_evac(zi, zi, F_UNITS, part % NG)
                    for c in range(2 * part, min(2 * part + 2, NT)):
                        act.wait_ge(s_hl[c % 2], 48 * (c // 2 + 1))
                        act.activation(o_sb[:, c % 2].rearrange("p h t -> p (h t)"),
                                       o_sb[:, c % 2].rearrange("p h t -> p (h t)"), ACT.Sigmoid).then_inc(s_so, 1)

            def ml_step(i, d, zi, zi0):
                x = i * 2 + d
                c = chunk(i, d)
                split(zi + (F_UNITS + 2), zi0 + F_UNITS + 2)
                act.wait_ge(s_t, x + 1)
                act.activation(ew[:, d].rearrange("p h t -> p (h t)"), ew[:, d].rearrange("p h t -> p (h t)"),
                               ACT.Exp).then_inc(s_e, 1)
                act.copy(sdec_now[:, d], grow(sdec, d, c)).then_inc(s_sn, 1)
                z_evac(zi, zi0, F_UNITS, 0)
                act.wait_ge(s_sn, x + 1)
                act.wait_ge(s_int, x + 1)
                if zi0 >= ZI_M + 2:
                    act.wait_ge(s_num, x - 1)
                for h in range(H):
                    m = act.activation(inter[:, d, h, :], bank[5 + h // 2][:, C1 * (h % 2):C1 * (h % 2 + 1)],
                                       ACT.Copy, scale=sdec_now[:, d, h:h + 1])
                m.then_inc(s_iev, 1)
                z_evac(zi, zi0, F_UNITS, 1)
                z_evac(zi, zi0, F_UNITS, 2)

            def mx(g):
                for k in range(KT):
                    x = KT * g + k
                    act.wait_ge(s_mx[k % 2], 16 * (x // 2 + 1))
                    if g:
                        act.wait_ge(s_unit, e_unit(g - 1, KT))
                    act.copy(mx_hi[:, k], mx_in[:, k % 2]).then_inc(s_mxh, 1)

            def e1(g):
                if g:
                    act.wait_ge(s_unit, e_unit(g, 0))
                for c in range(KT):
                    n = U_E + g * E_UNITS + c
                    split(n + 2, n + 2)
                    act.wait_ge(s_mg[c % 2], 16 * ((KT * g + c) // 2 + 1))
                    act.activation(mg[:, c % 2], mg[:, c % 2], ACT.Sigmoid).then_inc(s_sg, 1)
                    if c:
                        yhigh(g, c - 1)
                yhigh(g, KT - 1)

            def yhigh(g, c):
                act.wait_ge(s_ya, 2 * (KT * g + c + 1))
                act.copy(yy_hi[:, c], ya[:, c % 2, 0]).then_inc(s_yh, 1)

            def e2(g):
                if g:
                    wait_x(act, f"y{g - 1}")
                for c in range(KT):
                    n = U_E + g * E_UNITS + KT + c
                    split(n + 2, n + 2)
                    act.wait_ge(s_unit, n + 1)
                    act.copy(y2[:, c], bank[6 + c % 2][:, 0:GW]).then_inc(s_e2e, 1)

            def fi(g):
                n0 = U_FF + g * FF_UNITS
                if g:
                    act.wait_ge(s_unit, f_unit(g, 0))

                def high(j, slot):
                    act.wait_ge(s_ff, j + FT * g + 1)
                    act.copy(f_hi[:, bass.ds(j, 1), :].rearrange("p a n -> p (a n)"), ff[:, slot]).then_inc(s_fh, 1)

                def turn(i, first):
                    for u in range(4):
                        split(i * 4 + (n0 + u + 2), n0 + u + 2)
                        if u % 2 == 0:
                            continue
                        p = u // 2
                        act.wait_ge(s_unit, i * 4 + (n0 + 2 * p + 1))
                        if not (first and g == 0):
                            act.wait_ge(s_ff, i * 2 + (FT * g + p - 1))
                        act.activation(sa[:, p], bank[2 * p][:, 0:GW], ACT.Silu).then_inc(s_sa, 1)
                        if not (first and p == 0):
                            high(i * 2 + (p - 1), (p - 1) % 2)

                turn(0, True)
                with act.Fori(1, FT // 2) as i:
                    turn(i, False)
                high(FT - 1, 1)

            def fo(g):
                n0 = U_FF + g * FF_UNITS + 2 * FT
                if g == 0:
                    wait_x(act, "y2")
                else:
                    act.wait_ge(s_ot, 6 * g)

                def turn(i):
                    for c in range(4):
                        for part in range(3):
                            u = 3 * c + part
                            if n0 + 12 * i + u + 2 < U_END:
                                split(i * 12 + (n0 + u + 2), n0 + u + 2)
                        act.wait_ge(s_unit, n0 + 12 * i + 3 * (c + 1))
                        act.copy(y2[:, i * 4 + c], bank[4 + c % 2][:, 0:GW]).then_inc(s_foe, 1)

                turn(0)
                turn(1)

            def ot(g):
                for x in range(6):
                    half = x % 2
                    xx = 6 * g + x
                    act.wait_ge(s_ot, xx + 1)
                    if xx >= 2:
                        act.wait_ge(s_ost[half], 16 * (xx // 2))
                    act.copy(o_st[:, half], bank[6 + half][:, :]).then_inc(s_oe, 1)

            silu_vectors()
            stages = {"SQ": sq, "ST": stat, "HN": hn, "MX": mx, "E1": e1, "E2": e2, "FI": fi, "FO": fo, "OT": ot}
            for stage, w in ORDER:
                if stage == "MOD":
                    split(0, 0)
                    split(1, 1)
                elif stage == "MIX":
                    project()
                    mixers()
                elif stage in stages:
                    stages[stage](w)

        @block.vector
        def _(dve):
            def split(n, n0):
                slot = n0 % RAW
                dve.wait_ge(s_whi, n + 1)
                dve.tensor_tensor(w_lo[:, slot], raw[:, slot], w_hi[:, slot].bitcast(F32),
                                  ALU.subtract).then_inc(s_wlo, 1)

            def x_evac(i, us, first):
                for u in us:
                    for half in range(2):
                        dve.wait_ge(s_xt, i * 4 + 2 * u + half + 1)
                        ps = bank[2 * u + half][:, :].rearrange("p (k r w) -> p k r w", k=4, r=2)
                        out = xT[:, 4 * half:4 * half + 4, bass.ds(i * 2 * P + u * P, P)]
                        out = out.rearrange("p k (r w) -> p k r w", r=2)
                        if half == 0:
                            pos = K["pos_r"].rearrange("p (k r) -> p k r", k=4)[:, :, bass.ds(i * 4 + 2 * u, 2)]
                            pos = last(pos, GRID_W)
                        else:
                            pos = K["pos_c"].rearrange("p (k w) -> p k w", k=4).unsqueeze(2).broadcast_to(
                                (P, 4, 2, GRID_W))
                        dve.tensor_tensor(out, ps, pos, ALU.add).then_inc(s_xev, 1)

            def gain(i):
                return last(vec[:, V_NORM + 8 * i:V_NORM + 8 * (i + 1)], 2)

            def mod_columns(a, b, chain):
                dve.wait_ge(s_adam, b)
                dve.tensor_tensor(mod[:, a:b], bank[5][:, 2 * a:2 * b].rearrange("p (j v) -> p j v", v=2),
                                  last(vec[:, V_BADA + a:V_BADA + b], 2), ALU.add).then_inc(s_modc, 1)
                dve.wait_ge(s_modc, chain)

            def modulation():
                mod_columns(0, ADA_FIRST, 1)
                dve.scalar_tensor_tensor(A1[:], mod[:, 8:16], 1.0, gain(0), ALU.add, ALU.mult).then_inc(s_mod, 1)

            def modulation_rest():
                mod_columns(ADA_FIRST, 48, 2)
                dve.tensor_tensor(G1[:], mod[:, 16:24], gain(1), ALU.mult).then_inc(s_modc, 1)
                dve.tensor_tensor(G2[:], mod[:, 40:48], gain(3), ALU.mult).then_inc(s_modc, 1)
                dve.scalar_tensor_tensor(A2[:], mod[:, 32:40], 1.0, gain(2), ALU.add, ALU.mult).then_inc(s_mod, 1)
                dve.wait_ge(s_modc, 4)
                dve.wait_ge(s_mod, 2)

            def sq(which):
                q, m0, tmp = number["SQ", which], tmp_at["SQ", which], tmp_of(which)
                if q:
                    dve.wait_ge(s_st, q)
                for j in range(KT):
                    t = tmp[:, (m0 + j) % 4]
                    dve.wait_ge(s_sq, KT * q + j + 1)
                    if j == 0:
                        m = dve.tensor_copy(acc[:, :], t)
                    else:
                        dve.wait_ge(s_accs, KT * q + j)
                        m = dve.tensor_tensor(acc[:, :], acc[:, :], t, ALU.add)
                    m.then_inc(s_accs, 1)

            def stat(which):
                q = number["ST", which]
                dve.wait_ge(s_sd, q + 1)
                dve.reciprocal(rstd_of(which), rstd_of(which)).then_inc(s_rs, 1)
                dve.wait_ge(s_rs, q + 1)

            def hn(which):
                q, m0, tmp, g = number["HN", which], tmp_at["HN", which], tmp_of(which), int(which[1])
                src = source(which)
                first = which[0] == "h"
                for j in range(KT + 2):
                    if j < KT:
                        if m0 + j >= 4:
                            wait_tmp(dve, m0 + j)
                        dve.tensor_tensor(tmp[:, (m0 + j) % 4], src[:, j], rstd_of(which), ALU.mult).then_inc(s_nx, 1)
                    if j >= 2:
                        jj = j - 2
                        dve.wait_ge(s_nh, KT * q + jj + 1)
                        hi, lo = (h_hi, h_lo) if first else (h2_hi, h2_lo)
                        r = slice(g * GW, (g + 1) * GW) if first else slice(0, GW)
                        m = dve.tensor_tensor(lo[:, jj, r], tmp[:, (m0 + jj) % 4], hi[:, jj, r].bitcast(F32),
                                              ALU.subtract)
                        m.then_inc(s_nl, 1)

            xs = [0]

            def xstage(which):
                g = int(which[1])
                dve.tensor_tensor(y2[:, :, :], y2[:, :, :], b3(rstd[:, :], KT), ALU.mult).then_inc(s_xs, 1)
                xs[0] += 1
                dve.wait_ge(s_xs, xs[0])
                if which == "y0":
                    dve.wait_ge(s_back, 16 * KT)
                G = G1 if which[0] == "y" else G2
                for j in range(KT):
                    for a, b, col in halves(g):
                        x = xT2[:, j, g * GW + a:g * GW + b]
                        out = x if which[0] == "y" else y2[:, j, a:b]
                        m = dve.scalar_tensor_tensor(out, y2[:, j, a:b], G[:, j, col:col + 1], x, ALU.mult, ALU.add)
                m.then_inc(s_app, 1)

            def project():
                with dve.Fori(0, Z1_UNITS // 4) as i:
                    for u in range(4):
                        split(i * 4 + (u + 2), u + 2)
                split(U_ZG + 2, U_ZG + 2)
                modulation_rest()

            def t_tile(c):
                dve.wait_ge(s_tact, 2 * c + 1)
                dve.tensor_tensor(ab_lo[:, c], bank[4][:, :], ab_hi[:, c].bitcast(F32), ALU.subtract).then_inc(s_tdve, 1)
                dve.wait_ge(s_tmm, 4 * c + 2)
                dve.tensor_copy(up[:, c], bank[5][:, 0:FW]).then_inc(s_tdve, 1)
                dve.wait_ge(s_tmm, 4 * c + 4)
                if c:
                    dve.wait_ge(s_kvst, 16 * c)
                dve.tensor_copy(kv_st[:, 1], bank[7][:, :]).then_inc(s_tdve, 1)

            n_gd = [0]

            def link(m):
                n_gd[0] += 1
                m.then_inc(s_gd, 1)
                dve.wait_ge(s_gd, n_gd[0])

            def gates(step):
                flat, half = "p d c h -> p (d c h)", "p c h -> p (c h)"

                def col(d, kind):
                    return gts[:, :, 8 * d + 4 * kind:8 * d + 4 * kind + 4]

                dve.wait_ge(s_gp, step)
                if step == 1:
                    dve.wait_ge(s_gl, 32)
                    link(dve.tensor_tensor(gts[:], bank[4][:, 0:NT * NGC].rearrange("p (c g) -> p c g", c=NT),
                                           b3(bg[:], NT), ALU.add))
                    for d in range(2):
                        link(dve.scalar_tensor_tensor(absf[:, d], col(d, 1), -1.0, col(d, 1), ALU.mult, ALU.max))
                    assert n_gd[0] == GD_ABS
                    dve.wait_ge(s_ga, 2)
                    for d in range(2):
                        link(dve.scalar_tensor_tensor(lf[:, d], col(d, 1), 0.0, lse[:, d], ALU.min, ALU.subtract))
                    assert n_gd[0] == GD_LF
                elif step == 2:
                    link(dve.tensor_copy(cum[:].rearrange(flat), bank[5][:, 0:2 * NJ]))
                    link(dve.tensor_copy(blast[:].rearrange(flat), bank[6][:, 0:2 * NJ]))
                    for d in range(2):
                        link(dve.tensor_tensor(al[:, d], col(d, 0), cum[:, d], ALU.subtract))
                    assert n_gd[0] == GD_AL
                elif step == 3:
                    for d in range(2):
                        link(dve.tensor_copy(rows_a[:, d], bank[4 + 3 * d][0:NJ, 0:P]))
                    for d in range(2):
                        link(dve.tensor_tensor_scan(rows_m[:, d], rows_a[:, d], rows_a[:, d], -3e38, ALU.max,
                                                    ALU.max))
                    assert n_gd[0] == GD_SCAN
                elif step == 4:
                    link(dve.tensor_copy(mtok[:, 0].rearrange(half), bank[5][:, 0:NJ]))
                    link(dve.tensor_copy(mrev[:, :], bank[6][:, 0:NJ]))
                    assert n_gd[0] == GD_MCOPY
                elif step == 5:
                    link(dve.tensor_copy(mtok[:, 1].rearrange(half), bank[4][:, 0:NJ]))
                    assert n_gd[0] == GD_MTOK
                elif step == 6:
                    stabilisers(flat)
                else:
                    link(dve.tensor_copy(g_rows[:, :], bank[5][0:2 * NJ, 0:P]))
                    assert n_gd[0] == GD_END

            def stabilisers(flat):
                link(dve.tensor_copy(mlast[:].rearrange(flat), bank[7][:, 0:2 * NJ]))
                NL = NT - 1
                link(dve.tensor_copy(mprev[:, 0, 0], sm[:, 0]))
                link(dve.tensor_copy(mprev[:, 1, NL - 1], sm[:, 1]))
                link(dve.memset(mprev[:, :, NL], 0.0))
                for s in range(NL):
                    for d in range(2):
                        c = s if d == 0 else NL - 1 - s
                        before = mprev[:, d, c] if s == 0 else mnew[:, d, c + (1 if d else -1)]
                        link(dve.tensor_tensor(mnew[:, d, c], before, mlast[:, d, c], ALU.max))
                        link(dve.tensor_tensor(mnew[:, d, c], mnew[:, d, c], blast[:, d, c], ALU.add))
                link(dve.tensor_tensor(mnew[:, :, NL], mprev[:, :, NL], mlast[:, :, NL], ALU.max))
                link(dve.tensor_tensor(mnew[:, :, NL], mnew[:, :, NL], blast[:, :, NL], ALU.add))
                link(dve.tensor_copy(mprev[:, 0, 1:NL], mnew[:, 0, 0:NL - 1]))
                link(dve.tensor_copy(mprev[:, 1, 0:NL - 1], mnew[:, 1, 1:NL]))
                link(dve.tensor_tensor(gneg[:], mprev[:], mtok[:], ALU.max))
                link(dve.tensor_scalar(gneg[:], gneg[:], -1.0, None, ALU.mult))
                assert n_gd[0] == GD_G
                link(dve.tensor_tensor(em[:], gneg[:], cum[:], ALU.subtract))
                link(dve.tensor_tensor(sdec[:], mprev[:], gneg[:], ALU.add))
                link(dve.tensor_tensor(wst[:], al[:], blast[:], ALU.add))
                link(dve.tensor_tensor(wst[:], wst[:], mnew[:], ALU.subtract))
                link(dve.tensor_tensor(carry[:], blast[:], mprev[:], ALU.add))
                link(dve.tensor_tensor(carry[:], carry[:], mnew[:], ALU.subtract))
                assert n_gd[0] == GD_LOGS

            def mixers():
                for q in range(ZA_UNITS):
                    split(ZI_T + q + 2, ZI_T + q + 2)
                    t_tile(2 * q)
                    t_tile(2 * q + 1)
                t_tile(NT - 1)
                dve.wait_ge(s_kvst, 16 * NT)
                dve.memset(wp[:], 0.0).then_inc(s_wp0, 1)
                for i in range(F_UNITS):
                    split(U_F + i + 2, U_F + i + 2)
                part = 0
                for what in GATE_PHASE:
                    if what == "z":
                        if part % NG == 0:
                            n = ZI_G + F_UNITS + part // NG + 2
                            split(n, n)
                        part += 1
                    elif what[:2] == "Pa":
                        g = int(what[2])
                        dve.wait_ge(s_pmm, g + 1)
                        if g:
                            dve.wait_ge(s_cmm, 2 * g)
                        dve.tensor_copy(pT[:, 1], bank[5][:, 0:GW]).then_inc(s_pd, 1)
                    elif what[0] == "G":
                        gates(int(what[1]))
                        if what == "G1":
                            dve.wait_ge(s_mst[0], 96)
                            dve.wait_ge(s_mst[1], 80)
                            dve.memset(v_sb[:], 1.0).then_inc(s_set, 1)
                            dve.memset(st_ctx[:], 0.0).then_inc(s_set, 1)
                mlstm()

            def ml_step(i, d, st, first, n, n0):
                x = i * 2 + d
                c = chunk(i, d)
                mask = K["mask_b"] if d else K["mask_f"]
                dve.wait_ge(s_ld[d], i * 80 + 80)
                if not first:
                    dve.wait_ge(s_intra, x - 1)
                for h in range(H):
                    m = dve.scalar_tensor_tensor(ew[:, d, h], g_sb[:, d, h], gcol(al, d, c, h), mask, ALU.add,
                                                 ALU.min)
                m.then_inc(s_t, 1)
                if not first:
                    dve.wait_ge(s_kvm, x - 1)
                dve.tensor_tensor(wv[:, d], v_sb[:, d], last(grow(wst, d, c), C1), ALU.mult).then_inc(s_wv, 1)
                split(n, n0)
                dve.wait_ge(s_e, x + 1)
                dve.wait_ge(s_qk, x + 1)
                dve.tensor_tensor(ew[:, d].rearrange("p h t -> p (h t)"), ew[:, d].rearrange("p h t -> p (h t)"),
                                  bank[4][:, :], ALU.mult).then_inc(s_p, 1)
                dve.wait_ge(s_iev, x + 1)
                if not first:
                    dve.wait_ge(s_hst[d], i * 16)
                dve.wait_ge(s_intra, x + 1)
                for hh in range(2):
                    r = slice(2 * hh, 2 * hh + 2)
                    m = dve.tensor_tensor(num[:, d, r].rearrange("p h e -> p (h e)"),
                                          inter[:, d, r].rearrange("p h e -> p (h e)"),
                                          bank[7 if hh == 0 else 4][:, 0:2 * C1], ALU.add)
                m.then_inc(s_num, 1)
                dve.wait_ge(s_num, x + 1)
                dd = num[:, d, :, DH]
                dve.scalar_tensor_tensor(den[:, d], dd, -1.0, dd, ALU.mult, ALU.max).then_inc(s_den, 1)
                dve.wait_ge(s_den, x * 3 + 1)
                dve.tensor_tensor(den[:, d], den[:, d], grow(em, d, c), ALU.max).then_inc(s_den, 1)
                dve.wait_ge(s_den, x * 3 + 2)
                dve.reciprocal(den[:, d], den[:, d]).then_inc(s_den, 1)
                dve.wait_ge(s_den, x * 3 + 3)
                dve.tensor_tensor(num[:, d, :, 0:DH], num[:, d, :, 0:DH], last(den[:, d], DH),
                                  ALU.mult).then_inc(s_hd, 1)
                dve.wait_ge(s_kvm, x + 1)
                for h in range(H):
                    m = dve.scalar_tensor_tensor(st[:, d, h], st[:, d, h], gcol(carry, d, c, h),
                                                 bank[5 + h // 2][:, C1 * (h % 2):C1 * (h % 2 + 1)], ALU.mult,
                                                 ALU.add)
                m.then_inc(s_cup, 1)

            def mlstm():
                def turn(t, first):
                    for s in range(2):
                        for d in range(2):
                            n0 = ZI_M + F_UNITS + 2 + 2 * s + d
                            ml_step(t * 2 + s, d, st_lat, first and s == 0, t * 4 + n0, n0)

                dve.wait_ge(s_ga, 6)
                dve.wait_ge(s_st0, 64)
                turn(0, True)
                with dve.Fori(1, (NT - 1) // 2) as t:
                    turn(t, False)
                for d in range(2):
                    n = ZI_C + F_UNITS + 2 + d
                    ml_step(NT - 1, d, st_ctx, False, n, n)
                for part in range(2 * NG):
                    if part % NG == 0:
                        n = ZI_H + F_UNITS + 2 + part // NG
                        split(n, n)
                    tiles = range(2 * part, min(2 * part + 2, NT))
                    for c in tiles:
                        dve.wait_ge(s_hl[c % 2], 48 * (c // 2 + 1))
                        if c >= 2:
                            dve.wait_ge(s_ht, c - 1)
                        dve.tensor_tensor(hs[:, c % 2], hf_sb[:, c % 2, 0], hf_sb[:, c % 2, 1], ALU.add).then_inc(s_hs, 1)
                    for c in tiles:
                        dve.wait_ge(s_ht, c + 1)
                        dve.wait_ge(s_so, c + 1)
                        if c >= 2:
                            dve.wait_ge(s_host[c % 2], 16 * (c // 2))
                        dve.tensor_tensor(ho[:, c % 2].rearrange("p h t -> p (h t)"),
                                          o_sb[:, c % 2].rearrange("p h t -> p (h t)"), bank[6 + c % 2][:, :],
                                          ALU.mult).then_inc(s_ho, 1)

            def mx(g):
                for k in range(KT):
                    dve.wait_ge(s_mxh, KT * g + k + 1)
                    dve.tensor_tensor(mx_lo[:, k], mx_in[:, k % 2], mx_hi[:, k].bitcast(F32),
                                      ALU.subtract).then_inc(s_mxl, 1)

            def ylow(g, c):
                dve.wait_ge(s_yh, KT * g + c + 1)
                dve.tensor_tensor(yy_lo[:, c], ya[:, c % 2, 0], yy_hi[:, c].bitcast(F32),
                                  ALU.subtract).then_inc(s_yl, 1)

            def e1(g):
                for c in range(KT):
                    n = U_E + g * E_UNITS + c
                    split(n + 2, n + 2)
                    dve.wait_ge(s_unit, n + 1)
                    x = KT * g + c
                    dve.wait_ge(s_sg, x + 1)
                    if x >= 2:
                        dve.wait_ge(s_yl, x - 1)
                    for b in range(3):
                        dve.tensor_tensor(ya[:, c % 2, b], mg[:, c % 2, b], bank[3 * (c % 2) + b][:, 0:GW],
                                          ALU.mult).then_inc(s_ym, 1)
                    if c:
                        ylow(g, c - 1)
                ylow(g, KT - 1)

            def e2(g):
                for c in range(KT):
                    n = U_E + g * E_UNITS + KT + c
                    split(n + 2, n + 2)

            def fi(g):
                n0 = U_FF + g * FF_UNITS

                def low(j, slot):
                    dve.wait_ge(s_fh, j + FT * g + 1)
                    sl = bass.ds(j, 1)
                    dve.tensor_tensor(f_lo[:, sl, :].rearrange("p a n -> p (a n)"), ff[:, slot],
                                      f_hi[:, sl, :].rearrange("p a n -> p (a n)").bitcast(F32),
                                      ALU.subtract).then_inc(s_fl, 1)

                def turn(i, first):
                    for u in range(4):
                        split(i * 4 + (n0 + u + 2), n0 + u + 2)
                        if u % 2 == 0:
                            continue
                        p = u // 2
                        dve.wait_ge(s_unit, i * 4 + (n0 + 2 * p + 2))
                        dve.wait_ge(s_sa, i * 2 + (FT * g + p + 1))
                        if not (first and g == 0):
                            dve.wait_ge(s_fl, i * 2 + (FT * g + p - 1))
                        dve.tensor_tensor(ff[:, p], sa[:, p], bank[2 * p + 1][:, 0:GW], ALU.mult).then_inc(s_ff, 1)
                        if not (first and p == 0):
                            low(i * 2 + (p - 1), (p - 1) % 2)

                turn(0, True)
                with dve.Fori(1, FT // 2) as i:
                    turn(i, False)
                low(FT - 1, 1)

            def fo(g):
                n0 = U_FF + g * FF_UNITS + 2 * FT
                for u in range(3 * KT):
                    if n0 + u + 2 < U_END:
                        split(n0 + u + 2, n0 + u + 2)

            dve.memset(eps[:], EPS).then_inc(s_set, 1)
            dve.wait_ge(s_vec, 1)
            dve.tensor_copy(vec[:], bank[4][:, 0:V_ROWS]).then_inc(s_vecc, 1)
            dve.wait_ge(s_vecc, 1)
            dve.wait_ge(s_const, 32)
            with dve.Fori(0, 4) as i:
                x_evac(i, (0, 1), False)
            for half in range(2):
                dve.wait_ge(s_xt, 16 + half + 1)
                dve.tensor_copy(xT[:, 4 * half:4 * half + 4, LAT:T],
                                bank[half][:, :].rearrange("p (k t) -> p k t", k=4)).then_inc(s_xev, 1)
            stages = {"SQ": sq, "ST": stat, "HN": hn, "X": xstage, "MX": mx, "E1": e1, "E2": e2, "FI": fi, "FO": fo}
            for stage, w in ORDER:
                if stage == "MOD":
                    modulation()
                    split(0, 0)
                    split(1, 1)
                elif stage == "MIX":
                    project()
                    mixers()
                elif stage in stages:
                    stages[stage](w)

        @block.gpsimd
        def _(pool):
            def one(ap):
                return ap.rearrange("a p n -> (a p) n")

            def x_load(i, us, first):
                for u in us:
                    if not first:
                        pool.wait_ge(s_xt, i * 4 + 2 * u - 2)
                    pool.dma_start(x_in[:, u], x_sample[0, bass.ds(i * 2 * P + u * P, P), :]).then_inc(s_xin[u], 16)

            x_load(0, (0, 1), True)
            with pool.Fori(1, 4) as i:
                x_load(i, (0, 1), False)
            pool.wait_ge(s_xt, 14)
            pool.dma_start(x_in[:, 0], x_prompt[0]).then_inc(s_xin[0], 16)

            pool.wait_ge(s_xev, 2 * NT)
            pool.wait_ge(s_nl, KT * NG)
            for k in range(KT):
                pool.dma_start(x_dram[k], xT[:, k]).then_inc(s_spill, 16)

            def t_load(c):
                t = slice(c * P, (c + 1) * P)
                for piece, z0 in enumerate((0, 8, 12)):
                    if c:
                        pool.wait_ge(s_tmm, 4 * (c - 1) + piece + 2)
                    pool.dma_start(zt[:, piece], z_dram[z0:z0 + 4, :, t].rearrange("a p t -> p a t")).then_inc(s_zt[piece], 16)

            def kv_store(c):
                pool.wait_ge(s_tact, 2 * c + 2)
                pool.wait_ge(s_tdve, 3 * c + 3)
                pool.dma_start(kv_dram[c], kv_st[:].rearrange("p a c -> p (a c)")).then_inc(s_kvst, 16)

            pool.wait_ge(s_spill, 16 * KT)
            pool.wait_ge(s_unit, U_ZG)
            for u in range(2):
                pool.wait_ge(s_zst[u], 16 * Z1_UNITS // 2)
            t_load(0)
            for c in range(1, NT):
                t_load(c)
                kv_store(c - 1)
            kv_store(NT - 1)
            pool.wait_ge(s_wp0, 1)
            for w in range(4):
                r = slice(GD * (w % 2), GD * (w % 2) + GD)
                pool.dma_start(wp[r, w // 2, r], w_pool[0, w]).then_inc(s_wp, 16)
            for x in range(5):
                pool.wait_ge(s_mev, x + 1)
                dst, ps = dft_place(x)
                src = m_st[:, x % 2, 0:ps.shape[1]]
                if x == 4:
                    src = src.rearrange("p (a t) -> p a t", a=2)
                pool.dma_start(dst, src).then_inc(s_mst[x % 2], 16)
            pool.wait_ge(s_unit, U_ZB)
            pool.dma_start(bg[:], b_gate.rearrange("a d i h -> a (d i h)").broadcast_to((P, NGC))).then_inc(s_gl, 16)
            pool.dma_start(sm[:].rearrange("p d h -> p (d h)"),
                           state_m.rearrange("a e d h -> (a e) (d h)").broadcast_to((P, 2 * H))).then_inc(s_gl, 16)
            for x in range(5, 5 + 2 * NG):
                pool.wait_ge(s_mev, x + 1)
                g, j = divmod(x - 5, 2)
                pool.dma_start(mix_dram[2 + j, :, g * GW:(g + 1) * GW], m_st[:, x % 2, 0:GW]).then_inc(s_mst[x % 2], 16)
            for d in range(2):
                pool.dma_start(st_lat[:, d, :, 0:DH], state_C[0, 0, d].rearrange("h k v -> k h v")).then_inc(s_st0, 16)
                pool.dma_start(st_lat[:, d, :, DH], state_n[0, 0, d].rearrange("h k -> k h"), allow_slow_non_contiguous=True).then_inc(s_st0, 16)
            pool.wait_ge(s_mst[0], 96)
            pool.wait_ge(s_mst[1], 80)
            pool.wait_ge(s_gd, GD_END)
            pool.dma_start(g_dram.rearrange("a (h t) -> (a h) t", h=H), g_rows[:, :]).then_inc(s_gst, 16)
            pool.wait_ge(s_gst, 16)
            pool.wait_ge(s_set, 2)

            def ml_load(i, d, first):
                c = chunk(i, d)
                if not first:
                    pool.wait_ge(s_kvm, i * 2 + d - 1)
                t = bass.ds(c * P, P)
                pool.dma_start(q_sb[:, d], z_dram[4:8, :, t].rearrange("a p t -> p a t")).then_inc(s_ld[d], 16)
                pool.dma_start(k_sb[:, d], z_dram[8:12, :, t].rearrange("a p t -> p a t")).then_inc(s_ld[d], 16)
                kv = one(kv_dram[bass.ds(c, 1)])
                pool.dma_start(kt_sb[:, d], kv[:, 0:MW]).then_inc(s_ld[d], 16)
                pool.dma_start(v_sb[:, d, :, 0:DH], kv[:, MW:2 * MW].rearrange("p (h e) -> p h e", h=H)).then_inc(s_ld[d], 16)
                pool.dma_start(g_sb[:, d].rearrange("p h t -> p (h t)"),
                               g_dram[bass.ds(c + NT * d, 1), :].broadcast_to((P, H * P))).then_inc(s_ld[d], 16)

            def ml_store(i, d):
                pool.wait_ge(s_hd, i * 2 + d + 1)
                pool.dma_start(one(h_dram[bass.ds(chunk(i, d) + NT * d, 1)]).rearrange("p (h e) -> p h e", h=H),
                               num[:, d, :, 0:DH]).then_inc(s_hst[d], 16)

            for d in range(2):
                ml_load(0, d, True)
            with pool.Fori(1, NT - 1) as i:
                for d in range(2):
                    ml_store(i - 1, d)
                    ml_load(i, d, False)
            for d in range(2):
                ml_store(NT - 2, d)
                ml_load(NT - 1, d, False)
            for d in range(2):
                ml_store(NT - 1, d)
                pool.wait_ge(s_cup, 2 * NT - 1 + d)
                pool.dma_start(new_C[0, 0, d].rearrange("h k v -> k h v"), st_ctx[:, d, :, 0:DH]).then_inc(s_new, 16)
                pool.dma_start(new_n[0, 0, d].rearrange("h k -> k h"), st_ctx[:, d, :, DH], allow_slow_non_contiguous=True).then_inc(s_new, 16)
            pool.dma_start(new_m[0], mnew[0:1, :, NT - 1]).then_inc(s_new, 16)
            pool.wait_ge(s_hst[0], 16 * NT)
            pool.wait_ge(s_hst[1], 16 * NT)

            def hm_load(c):
                u = c % 2
                if c >= 2:
                    pool.wait_ge(s_ho, c - 1)
                pool.dma_start(hf_sb[:, u, 0], h_dram[c]).then_inc(s_hl[u], 16)
                pool.dma_start(hf_sb[:, u, 1], h_dram[c + NT]).then_inc(s_hl[u], 16)
                pool.dma_start(o_sb[:, u], z_dram[16:20, :, c * P:(c + 1) * P].rearrange("a p t -> p a t")).then_inc(s_hl[u], 16)

            def hm_store(c):
                u = c % 2
                pool.wait_ge(s_ho, c + 1)
                pool.dma_start(mix_dram[4:8, :, c * P:(c + 1) * P].rearrange("a p t -> p a t"), ho[:, u]).then_inc(s_host[u], 16)

            hm_load(0)
            hm_load(1)
            for c in range(NT):
                hm_store(c)
                if c + 2 < NT:
                    hm_load(c + 2)
            pool.wait_ge(s_new, 80)
            pool.wait_ge(s_unit, U_E)
            pool.wait_ge(s_host[0], 80)
            pool.wait_ge(s_host[1], 64)

            def mx(g):
                for k in range(KT):
                    x = KT * g + k
                    if x >= 2:
                        pool.wait_ge(s_mxl, x - 1)
                    pool.dma_start(mx_in[:, k % 2], mix_dram[k, :, g * GW:(g + 1) * GW]).then_inc(s_mx[k % 2], 16)

            merge = z_dram[Z1_UNITS + 4:Z1_UNITS + Z2_UNITS].rearrange("(b c) p t -> c p b t", b=3)

            def mg_load(g, c):
                x = KT * g + c
                if x >= 2:
                    pool.wait_ge(s_ym, 3 * (x - 1))
                pool.dma_start(mg[:, c % 2], merge[c, :, :, g * GW:(g + 1) * GW]).then_inc(s_mg[c % 2], 16)

            def e1(g):
                mg_load(g, 0)
                mg_load(g, 1)
                if g == 0:
                    for k in range(KT):
                        pool.dma_start(xT2[:, k], x_dram[k]).then_inc(s_back, 16)
                for c in range(KT):
                    x = KT * g + c
                    for b in (1, 2):
                        pool.wait_ge(s_ym, 3 * x + b + 1)
                        if b == 2:
                            pool.wait_ge(s_ya, 2 * x + 1)
                        pool.tensor_tensor(ya[:, c % 2, 0], ya[:, c % 2, 0], ya[:, c % 2, b], ALU.add).then_inc(s_ya, 1)
                    if c + 2 < KT:
                        mg_load(g, c + 2)

            def ot(g):
                for x in range(6):
                    t, half = divmod(x, 2)
                    pool.wait_ge(s_oe, 6 * g + x + 1)
                    tok = (3 * g + t) * P
                    cols = slice(512 * half, 512 * half + 512)
                    dst = y_sample[0, tok:tok + P, cols] if tok < LAT else y_prompt[0, :, cols]
                    pool.dma_start(dst, o_st[:, half]).then_inc(s_ost[half], 16)

            for stage, w in ORDER:
                if stage == "MX":
                    mx(w)
                    if w == 0:
                        pool.wait_ge(s_zst[0], 8 * (Z_COUNT - 1))
                        pool.wait_ge(s_zst[1], 8 * (Z_COUNT - 1))
                elif stage == "E1":
                    e1(w)
                elif stage == "OT":
                    ot(w)
            pool.wait_ge(s_ost[0], 16 * 3 * NG)
            pool.wait_ge(s_ost[1], 16 * 3 * NG)


def _tiles(w, cols=P):
    k, n = w.shape
    u = np.ascontiguousarray(w.reshape(k // P, P, n // cols, cols).transpose(2, 1, 0, 3)).reshape(n // cols, P, k // P * cols)
    return u


def kernel(**inputs):
    import concourse.bacc as _bacc
    from concourse.bass_utils import run_bass_kernel_spmd as _run

    a = {k: np.asarray(v) for k, v in inputs.items()}
    w_in = a["w_in"][0]
    w_proj = np.concatenate([a["w_proj_f"][0], a["w_proj_p"][0], a["w_proj_m"][0]])
    ffn_in = _tiles(a["w_ffn_in"][0])
    ffn_in = np.stack([ffn_in[:FT], ffn_in[FT:]], axis=1).reshape(2 * FT, P, D)
    ffn_out = np.concatenate([
        _tiles(a["w_ffn_out"][0][sum(FO_K[:i]) * P:sum(FO_K[:i + 1]) * P]) if n == 8 else
        np.concatenate([_tiles(a["w_ffn_out"][0][sum(FO_K[:i]) * P:sum(FO_K[:i + 1]) * P]),
                        np.zeros((KT, P, D - n * P), np.float32)], axis=2)
        for i, n in enumerate(FO_K)])
    ffn_out = ffn_out.reshape(3, KT, P, D).transpose(1, 0, 2, 3).reshape(3 * KT, P, D)
    w_stream = np.concatenate([
        _tiles(w_in[:, :O_COL]), _tiles(w_in[:, GATE_COL:GATE_COL + P]), _tiles(w_in[:, O_COL:GATE_COL]),
        _tiles(w_in[:, MERGE_COL:]), _tiles(w_proj), _tiles(a["w_out"][0]), ffn_in, ffn_out])
    vectors = np.concatenate([a["c"].reshape(-1, P), a["c_ctx"].reshape(-1, P), a["b_ada"].reshape(-1, P),
                              a["norm_g"].reshape(-1, P), a["pool_scale"].reshape(-1, P)])
    base, cst, dft = shape_constants()
    ins = {"x_prompt": a["x_prompt"], "x_sample": a["x_sample"], "state_C": a["state_C"], "state_n": a["state_n"],
           "state_m": a["state_m"], "vectors": vectors, "w_ada": _tiles(a["w_ada"][0]), "w_stream": w_stream,
           "b_gate": a["b_gate"], "w_pool": a["w_pool"], "k_base": base, "k_cst": cst, "k_dft": dft}
    outs = [("y_prompt", (1, CTX, D)), ("y_sample", (1, LAT, D)), ("new_C", (1, 1, 2, H, DH, DH)),
            ("new_n", (1, 1, 2, H, DH)), ("new_m", (1, 1, 2, H))]
    nc = _bacc.Bacc("TRN2", target_bir_lowering=False, num_devices=1)
    arrays, args = {}, {}
    for name, v in ins.items():
        arrays[f"in_{name}"] = np.ascontiguousarray(v)
        args[name] = nc.dram_tensor(f"in_{name}", v.shape, F32, kind="ExternalInput").ap()
    for name, shape in outs:
        args[name] = nc.dram_tensor(f"out_{name}", shape, F32, kind="ExternalOutput").ap()
    build(nc, **args)
    r = _run(nc, [arrays], core_ids=[0])
    return tuple(r.results[0][f"out_{name}"] for name, _ in outs)
```

```python
from contextlib import ExitStack

import concourse.bass as bass
import numpy as np
from concourse import mybir

F32 = mybir.dt.float32
F32R = mybir.dt.float32r
ACT = mybir.ActivationFunctionType
ALU = mybir.AluOpType
AX = mybir.AxisListType

P = 128
D = 1024
KT = D // P
LAT, CTX = 1024, 128
T = LAT + CTX
NT = T // P
GW = 384
NG = T // GW
GRID_W = 64
FW = 256
GD = 64
MW = 512
H, DH = 4, 128
NGC = 16
DFF = 2816
FT = DFF // P
WINDOWS = (2, 4, 8, 16)
EPS = 1e-6
RAW, SPL = 4, 4
NEG = -1e30
NJ = NT * H
C1 = DH + 1

Z1_UNITS = (2 * FW + 3 * MW) // P
O_COL = 2 * FW + 3 * MW
GATE_COL = O_COL + MW
MERGE_COL = GATE_COL + NGC
Z2_UNITS = (MW + 3 * D) // P
ADA_W = 512
ADA_G = KT * ADA_W // D
ADA_FIRST, ADA_UNITS = 2 * KT, 6 * KT
AHEAD = 3
ZA_UNITS = 4
ZI_G = Z1_UNITS
U_G = ZI_G + ADA_UNITS
U_F = U_G + 1 + ZA_UNITS
F_UNITS = LAT // P + 1
U_ZB = U_F + F_UNITS
U_E = U_ZB + Z2_UNITS - ZA_UNITS
ZI_T = ZI_G + 1
ZI_P = ZI_T + ZA_UNITS
ZI_M = ZI_P + 4
ZI_C = ZI_M + 2 * (LAT // P)
ZI_H = ZI_C + 2
Z_COUNT = Z1_UNITS + 1 + Z2_UNITS
assert ZI_H + 2 == Z_COUNT
SHIFT_A, SHIFT_B = ADA_UNITS, ADA_UNITS + F_UNITS
assert Z1_UNITS * 2 == ADA_UNITS - ADA_FIRST
TURNED = {0: 0, 1: 1, 3: 2, 4: 3, 6: 4, 7: 5, 9: 6, 10: 7, 11: 8}
HM_TILES = ((), (0, 1), (2, 3), (4, 5), (6, 7), (8,))
GATE_PHASE = ("Pa0", "z", "Pb0", "Pa1", "z", "Pb1", "Pa2", "z", "Pb2", "z", "G1", "z", "G2", "z", "G3", "z", "G4",
              "z", "G5", "z", "G6", "z", "z", "z", "G7")
E_UNITS = 2 * KT
U_FF = U_E + NG * E_UNITS
FO_K = (8, 7, 7)
MG, MX = 3, 3
FF_UNITS = 2 * FT + len(FO_K) * KT
U_END = U_FF + NG * FF_UNITS

V_C, V_CTX, V_BADA, V_NORM, V_PSC, V_ROWS = 0, 8, 16, 64, 96, 98

CB = {}
_at = 0
for _name, _w in (("pos_r", 4 * 16), ("pos_c", 4 * 64), ("sum2", 2), ("rev", P), ("tri_f", P), ("tri_b", P), ("last", P), ("first", P), ("mask_f", P),
                  ("mask_b", P), ("pool", 8 * P), ("cb", 2 * P)):
    CB[_name] = slice(_at, _at + _w)
    _at += _w
CB_W, CB_EARLY = _at, CB["sum2"].stop


def shape_constants():
    c = np.zeros((P, CB_W), np.float32)
    s, t = np.arange(P)[:, None], np.arange(P)[None, :]
    c[:, CB["rev"]] = (s + t == P - 1)
    c[:, CB["tri_f"]] = (s <= t)
    c[:, CB["tri_b"]] = (s >= t)
    c[P - 1, CB["last"]] = 1
    c[0, CB["first"]] = 1
    c[:, CB["mask_f"]] = np.where(s <= t, 0, NEG)
    c[:, CB["mask_b"]] = np.where(s >= t, 0, NEG)
    for kind, width in enumerate((GRID_W, CTX)):
        for g, w in enumerate(WINDOWS):
            m = np.zeros((P, P), np.float64)
            for x in range(P):
                row, pos = x // width * width, x % width
                lo, hi = max(pos - w // 2, 0), min(pos + w - 1 - w // 2, width - 1)
                m[row + lo:row + hi + 1, x] = 1.0 / (hi - lo + 1)
                m[x, x] -= 1.0
            c[:, CB["pool"].start + (kind * 4 + g) * P:][:, :P] = m
    quarter = D // 4
    omega = (np.float32(1.0) / np.float32(10000.0) ** (np.arange(quarter, dtype=np.float32) / np.float32(quarter)))
    for name, n in (("pos_r", 16), ("pos_c", 64)):
        arg = omega.astype(np.float32)[:, None] * np.arange(n, dtype=np.float32)[None, :]
        table = np.concatenate([np.sin(arg), np.cos(arg)]).astype(np.float32)
        c[:, CB[name]] = table.reshape(4, P, n).transpose(1, 0, 2).reshape(P, 4 * n)
    c[0:4, CB["sum2"]] = np.tile(np.eye(2), (2, 1))
    k = np.arange(GD)
    ang = 2 * np.pi * (k[:, None] * k[None, :] % GD) / GD
    for i, m in enumerate((np.cos(ang), -np.sin(ang))):
        for b in range(2):
            at = CB["cb"].start + i * P + b * GD
            c[b * GD:(b + 1) * GD, at:at + GD] = m
    dft = np.zeros((F_UNITS, P, D), np.float32)
    for n in (LAT, CTX):
        k = np.arange(n)
        ang = 2 * np.pi * (k[:, None] * k[None, :] % n) / n
        cs = np.stack([np.cos(ang), np.sin(ang)]) / np.sqrt(float(n) * GD)
        if n == LAT:
            dft[:-1] = cs[:, :, :LAT // 2].transpose(1, 0, 2).reshape(LAT // P, P, LAT)
        else:
            dft[-1, :, :2 * CTX] = np.concatenate([cs[0], cs[1]], axis=1)
    base = np.concatenate([np.eye(P), np.ones((P, P))], axis=1).astype(np.float32)
    return base, c, dft


GD_ABS, GD_LF, GD_AL, GD_SCAN, GD_MCOPY, GD_MTOK = 3, 5, 9, 13, 15, 16
GD_G = GD_MTOK + 1 + 3 + 4 * (NT - 1) + 2 + 2 + 2
GD_LOGS = GD_G + 6
GD_END = GD_LOGS + 1


def build(nc, x_prompt, x_sample, state_C, state_n, state_m, vectors, w_ada, w_stream, b_gate, w_pool,
          k_base, k_cst, k_dft, y_prompt, y_sample, new_C, new_n, new_m):
    z_dram = nc.dram_tensor("z_scratch", (Z1_UNITS + Z2_UNITS, P, T), F32).ap()
    mix_dram = nc.dram_tensor("mix_scratch", (KT, P, T), F32).ap()
    kv_dram = nc.dram_tensor("kv_scratch", (NT, P, 2 * MW), F32).ap()
    x_dram = nc.dram_tensor("x_scratch", (KT, P, T), F32).ap()
    g_dram = nc.dram_tensor("g_scratch", (2 * NT, H * P), F32).ap()
    h_dram = nc.dram_tensor("h_scratch", (2 * NT, P, MW), F32).ap()

    with ExitStack() as top:
        def sb(stack, name, shape, dt=F32):
            return stack.enter_context(nc.sbuf_tensor(name, shape, dt))

        def sem(name):
            return top.enter_context(nc.semaphore(name))

        bank = [top.enter_context(nc.psum_tensor(f"bank{i}", [P, 512], F32)) for i in range(8)]

        raw = sb(top, "raw", [P, RAW, D])
        w_hi = sb(top, "w_hi", [P, SPL, D], F32R)
        w_lo = sb(top, "w_lo", [P, SPL, D], F32R)
        base = sb(top, "base", [P, 2 * P])
        ident, ones = base[:, 0:P], base[:, P:2 * P]
        vec = sb(top, "vec", [P, V_ROWS])
        silu_c = sb(top, "silu_c", [P, KT, 2])
        mod = sb(top, "mod", [P, 48, 2])
        A1 = sb(top, "A1", [P, KT, 2])
        A2 = sb(top, "A2", [P, KT, 2])
        G1 = sb(top, "G1", [P, KT, 2])
        G2 = sb(top, "G2", [P, KT, 2])
        eps = sb(top, "eps", [P, 1])
        acc = sb(top, "acc", [P, GW])
        rstd = sb(top, "rstd", [P, GW])

        s1 = ExitStack()
        cst = sb(s1, "cst", [P, CB_W])
        K = {n: cst[:, s] for n, s in CB.items()}
        s1r = ExitStack()
        rstd1 = sb(s1r, "rstd1", [P, T])
        s1r.close()
        gz = sb(s1, "gz", [P, T])
        z_st = sb(s1, "z_st", [P, 2, T])
        s1x = ExitStack()
        x_in = sb(s1x, "x_in", [P, 2, D])
        rows = sb(s1x, "rows", [V_ROWS, P])
        s1x.close()
        h_hi = sb(s1, "h_hi", [P, KT, T], F32R)
        h_lo = sb(s1, "h_lo", [P, KT, T], F32R)
        s2 = ExitStack()
        xT = sb(s2, "xT", [P, KT, T])
        tmp1 = sb(s2, "tmp1", [P, 5, GW])
        c_split = sb(s2, "c_split", [P, KT, P], F32R)
        c_wide = sb(s2, "c_wide", [P, P])
        ada_row = sb(s2, "ada_row", [4, 2, ADA_W])
        s2.close()
        s2 = ExitStack()
        ab_hi = sb(s2, "ab_hi", [P, NT, 2 * FW], F32R)
        ab_lo = sb(s2, "ab_lo", [P, NT, 2 * FW], F32R)
        up = sb(s2, "up", [P, NT, FW])
        wp = sb(s2, "wp", [P, 2, P])
        red = sb(s2, "red", [P, LAT // P, 2, 2])
        red_sum = sb(s2, "red_sum", [P, 2, 2])
        alt = sb(s2, "alt", [P, 2])
        s2t = ExitStack()
        zt = sb(s2t, "zt", [P, 3, 4, P])
        kv_st = sb(s2t, "kv_st", [P, 2, MW])
        s2t.close()
        f_st = sb(s2, "f_st", [P, 2, LAT])
        s2.close()
        s2 = ExitStack()
        st_lat = sb(s2, "st_lat", [P, 2, H, C1])
        st_ctx = sb(s2, "st_ctx", [P, 2, H, C1])
        inter = sb(s2, "inter", [P, 2, H, C1])
        den = sb(s2, "den", [P, 2, H])
        sdec_now = sb(s2, "sdec_now", [P, 2, H])
        bg = sb(s2, "bg", [P, NGC])
        sm = sb(s2, "sm", [P, 2, H])
        gts = sb(s2, "gts", [P, NT, NGC])

        def gate(name):
            return sb(s2, name, [P, 2, NT, H])

        lf, absf, lse, cum, al, mtok, mprev, mnew, gneg, em, sdec, wst, carry, blast, mlast = (
            gate(n) for n in ("lf", "absf", "lse", "cum", "al", "mtok", "mprev", "mnew", "gneg", "em", "sdec",
                              "wst", "carry", "blast", "mlast"))
        mrev = sb(s2, "mrev", [P, NJ])
        rows_a = sb(s2, "rows_a", [NJ, 2, P])
        rows_m = sb(s2, "rows_m", [NJ, 2, P])
        g_rows = sb(s2, "g_rows", [2 * NJ, P])
        s2p = ExitStack()
        m_st = sb(s2p, "m_st", [P, 2, GW])
        pT = sb(s2p, "pT", [P, 2, GW])
        s2p.close()
        s2m = ExitStack()
        q_sb = sb(s2m, "q_sb", [P, 2, H, P])
        k_sb = sb(s2m, "k_sb", [P, 2, H, P])
        kt_sb = sb(s2m, "kt_sb", [P, 2, MW])
        v_sb = sb(s2m, "v_sb", [P, 2, H, C1])
        g_sb = sb(s2m, "g_sb", [P, 2, H, P])
        ew = sb(s2m, "ew", [P, 2, H, P])
        wv = sb(s2m, "wv", [P, 2, H, C1])
        num = sb(s2m, "num", [P, 2, H, C1])
        s2m.close()
        hf_sb = sb(s2, "hf_sb", [P, 3, 2, MW])
        o_sb = sb(s2, "o_sb", [P, 3, H, P])
        hs = sb(s2, "hs", [P, 3, MW])
        ho = sb(s2, "ho", [P, 3, H, P])
        s2.close()
        s1.close()

        s3 = ExitStack()
        xT2 = sb(s3, "xT2", [P, KT, T])
        y2 = sb(s3, "y2", [P, KT, GW])
        h2_hi = sb(s3, "h2_hi", [P, KT, GW], F32R)
        h2_lo = sb(s3, "h2_lo", [P, KT, GW], F32R)
        tmp3 = sb(s3, "tmp3", [P, 4, GW])
        s3a = ExitStack()
        mx_hi = sb(s3a, "mx_hi", [P, KT, GW], F32R)
        mx_lo = sb(s3a, "mx_lo", [P, KT, GW], F32R)
        mg = sb(s3a, "mg", [P, MG, 3, GW])
        ya = sb(s3a, "ya", [P, 2, GW])
        yb = sb(s3a, "yb", [P, 2, GW])
        yy_hi = sb(s3a, "yy_hi", [P, KT, GW], F32R)
        yy_lo = sb(s3a, "yy_lo", [P, KT, GW], F32R)
        acc_x = sb(s3a, "acc_x", [P, GW])
        rstd_x = sb(s3a, "rstd_x", [P, GW])
        mx_in = sb(s3a, "mx_in", [P, MX, GW])
        s3a.close()
        o_st = sb(s3, "o_st", [P, 2, 512])
        sa = sb(s3, "sa", [P, 2, GW])
        ff = sb(s3, "ff", [P, 2, GW])
        f_hi = sb(s3, "f_hi", [P, FT, GW], F32R)
        f_lo = sb(s3, "f_lo", [P, FT, GW], F32R)
        s3.close()

        s_raw = [sem(f"raw_landed{i}") for i in range(RAW)]
        s_whi, s_wlo, s_unit = sem("w_hi_ready"), sem("w_lo_ready"), sem("unit_multiplied")
        s_base, s_early = sem("base_landed"), sem("early_constants_landed")
        s_arow, s_aturn, s_cz = sem("ada_row_ready"), sem("ada_turned"), sem("c_zeroed")
        s_cz0 = sem("zeros_ready")
        s_const, s_rows, s_vec, s_vecc, s_silu = (sem(n) for n in ("const_landed", "rows_landed", "vec_transposed",
                                                                   "vec_ready", "silu_ready"))
        s_set = sem("memsets_done")
        s_xin = [sem(f"x_landed{i}") for i in range(2)]
        s_xt, s_xev = sem("x_transposed"), sem("xT_ready")
        s_chi, s_clo, s_modc, s_mod = sem("c_high"), sem("c_low"), sem("mod_chain"), sem("mod_ready")
        s_sq, s_accs, s_st, s_sd, s_rs = (sem(n) for n in ("square_ready", "square_summed", "mean_ready",
                                                           "root_ready", "rstd_ready"))
        s_nx, s_nf, s_nh, s_nl, s_app, s_xs = (
            sem(n) for n in ("norm_scaled", "norm_full", "norm_high", "norm_low", "residual_ready", "x_step"))
        s_zmm, s_zev = sem("z_multiplied"), sem("z_evacuated")
        s_zst = [sem(f"z_stored{i}") for i in range(2)]
        s_zt = [sem(f"zt_landed{i}") for i in range(3)]
        s_spill, s_back = sem("x_spilled"), sem("x_back")
        s_tmm, s_tact, s_tdve = sem("t_transposed"), sem("t_act"), sem("t_dve")
        s_kvst = sem("kv_stored")
        s_fmm, s_fev, s_fd, s_fout, s_fst = (sem(n) for n in ("dft_multiplied", "dft_cosines_out", "dft_mirrored",
                                                              "dft_ready", "dft_stored"))
        s_red, s_redc, s_alt = sem("u_reduced"), sem("u_chain"), sem("alternating_sum_ready")
        s_cmm, s_mev = sem("mix_multiplied"), sem("mix_evacuated")
        s_mst = [sem(f"mix_stored{i}") for i in range(2)]
        s_pmm, s_pa, s_pd, s_wp = sem("pooled"), sem("pool_act"), sem("pool_dve"), sem("w_pool_landed")
        s_wp0 = sem("w_pool_zeroed")
        s_gl, s_gp, s_gd, s_ga, s_gst = (sem(n) for n in ("gate_inputs_landed", "gate_pe", "gate_dve", "gate_act",
                                                          "g_rows_stored"))
        s_ld = [sem(f"chunk_landed{i}") for i in range(2)]
        s_st0 = sem("state_landed")
        s_qk, s_int, s_iev, s_t, s_e, s_p, s_wv, s_intra, s_kvm, s_num, s_den, s_hd, s_cup = (
            sem(n) for n in ("scores_ready", "inter_ready", "inter_evacuated", "logw_ready", "expw_ready",
                             "probs_ready", "wv_ready", "intra_ready", "kv_ready", "num_ready", "den_chain",
                             "h_ready", "state_updated"))
        s_sn = sem("decays_ready")
        s_hst = [sem(f"h_stored{i}") for i in range(2)]
        s_hl = [sem(f"h_landed{i}") for i in range(3)]
        s_ol = [sem(f"o_landed{i}") for i in range(3)]
        s_hs, s_ht, s_ho, s_so = sem("h_summed"), sem("h_transposed"), sem("h_gated"), sem("o_sigmoid_ready")
        s_host = [sem(f"hm_stored{i}") for i in range(3)]
        s_new = sem("new_state_stored")
        s_mx = [sem(f"mx_landed{i}") for i in range(MX)]
        s_mxh, s_mxl = sem("mx_high"), sem("mx_low")
        s_mg = [sem(f"merge_landed{i}") for i in range(MG)]
        s_sg = sem("merge_sigmoid_ready")
        s_ym, s_ya, s_yh, s_yl = (sem(n) for n in ("branches_gated", "y_summed", "y_high", "y_low"))
        s_e2e = sem("out_evacuated")
        s_sa, s_ff, s_fh, s_fl = (sem(n) for n in ("silu_a_ready", "f_ready", "f_high", "f_low"))
        s_foe = sem("ffn_out_evacuated")
        s_ot, s_oe = sem("out_transposed"), sem("out_staged")
        s_ost = [sem(f"out_stored{i}") for i in range(2)]

        ORDER = [("XT", (0, 3)), ("XT", (3, 6)), ("XT", (6, 7)), ("ST", "h0"), ("XT", (7, NT)), ("ADA", (8, 9)),
                 ("ST", "h1"), ("ADA", (9, 12)), ("ADA", (12, 13)), ("ST", "h2"), ("ADA", (13, ADA_FIRST)), ("MOD", None), ("HN", "h0"), ("HN", "h1"), ("HN", "h2"), ("MIX", None),
                 ("MX", 0), ("E1", (0, 0, 8)), ("E2", (0, 0, 8)), ("E1", (1, 0, 1)), ("ST", "y0"), ("E1", (1, 1, 8)),
                 ("E2", (1, 0, 4)), ("E2", (1, 4, 8)), ("E1", (2, 0, 2)), ("ST", "x0"), ("ST", "y1"),
                 ("E1", (2, 2, 8)), ("E2", (2, 0, 8)),
                 ("FI", (0, 0, 2)), ("ST", "y2"), ("FI", (0, 2, 4)), ("FI", (0, 4, 6)), ("ST", "x1"),
                 ("FI", (0, 6, 11)), ("FO", 0),
                 ("FI", (1, 0, 2)), ("ST", "o0"), ("FI", (1, 2, 4)), ("OT", 0), ("FI", (1, 4, 6)), ("ST", "x2"),
                 ("FI", (1, 6, 11)), ("FO", 1),
                 ("FI", (2, 0, 2)), ("ST", "o1"), ("FI", (2, 2, 4)), ("OT", 1), ("FI", (2, 4, 11)), ("FO", 2),
                 ("ST", "o2"), ("X", "o2"), ("OT", 2)]
        WITH = {("XT", (3, 6)): (("SQ", "h0"),), ("XT", (7, NT)): (("SQ", "h1"),), ("ADA", (9, 12)): (("SQ", "h2"),),
                ("E2", (0, 0, 8)): (("MX", 1), ("SQ", "y0")), ("E1", (1, 1, 8)): (("X", "y0"),),
                ("E2", (1, 0, 4)): (("MX", 2), ("SQ", "x0")), ("E2", (1, 4, 8)): (("SQ", "y1"),),
                ("E1", (2, 2, 8)): (("X", "y1"),), ("E2", (2, 0, 8)): (("HN", "x0"), ("SQ", "y2")), ("FI", (0, 2, 4)): (("X", "y2"),), ("FI", (0, 4, 6)): (("SQ", "x1"),),
                ("FO", 0): (("HN", "x1"), ("SQ", "o0")), ("FI", (1, 2, 4)): (("X", "o0"),),
                ("FI", (1, 4, 6)): (("SQ", "x2"),), ("FO", 1): (("HN", "x2"), ("SQ", "o1")),
                ("FI", (2, 2, 4)): (("X", "o1"),), ("FO", 2): (("SQ", "o2"),)}
        POOL_SQ = ("h1", "h2")
        FLAT = [kw for stage in ORDER for kw in (stage,) + WITH.get(stage, ())]
        number = {}
        for kw in FLAT:
            if kw[0] in ("SQ", "ST", "HN", "X"):
                number[kw] = sum(1 for k in number if k[0] == kw[0])
        stats = [w for s, w in ORDER if s == "ST"]

        def wait_applied(eng, which):
            if which[0] == "h" or which in ("x0", "y0"):
                return
            w = [v for v in stats[:stats.index(which)] if v != "x0"][-1]
            s = "HN" if w[0] in "hx" else "X"
            eng.wait_ge(s_nl if s == "HN" else s_app, KT * (number[s, w] + 1))

        def sq_slot(which, j):
            n = KT * number["SQ", which] + j
            return n, tmp_of(which)[:, n % 2]

        def hn_slot(which, j):
            n = KT * number["HN", which] + j
            return n, tmp_of(which)[:, 2 + n % hn_slots(which)]

        def hn_slots(which):
            return 3 if which[0] == "h" else 2

        def wait_x(eng, which, upto=KT):
            eng.wait_ge(s_app, KT * number["X", which] + upto)

        def sum_square(eng, which, j):
            q = number["SQ", which]
            n, t = sq_slot(which, j)
            eng.wait_ge(s_sq, n + 1)
            if j == 0:
                before = q - 1 if which in ("x0", "y1") else q
                if before:
                    eng.wait_ge(s_st, before)
                if n:
                    eng.wait_ge(s_accs, n)
                m = eng.tensor_copy(acc_of(which), t)
            else:
                eng.wait_ge(s_accs, n)
                m = eng.tensor_tensor(acc_of(which), acc_of(which), t, ALU.add)
            m.then_inc(s_accs, 1)

        def piece_range(kind, i, n):
            if kind == "HN" and n == KT:
                n -= 1
            return range(min(KT * i // n, KT), min(KT * (i + 1) // n, KT))

        def halves(g):
            return [(0, GW, 0)] if g < NG - 1 else [(0, LAT - g * GW, 0), (LAT - g * GW, GW, 1)]

        def source(which):
            g = int(which[1])
            if which[0] in "yo":
                return y2[:, :, :]
            return (xT if which[0] == "h" else xT2)[:, :, g * GW:(g + 1) * GW]

        def tmp_of(which):
            return tmp1 if which[0] == "h" else tmp3

        def rstd_of(which):
            if which[0] == "h":
                return rstd1[:, int(which[1]) * GW:(int(which[1]) + 1) * GW]
            return (rstd_x if which == "x0" else rstd)[:, :]

        def acc_of(which):
            return (acc_x if which == "x0" else acc)[:, :]

        def mg_uses(g, c):
            return g * len(range(c % MG, KT, MG)) + c // MG

        def wait_source(eng, which, j):
            kind, g = which[0], int(which[1])
            if kind == "h":
                eng.wait_ge(s_xev, 2 * min(3 * (g + 1), NT))
            elif kind == "y":
                eng.wait_ge(s_e2e, KT * g + j + 1)
            elif kind == "o":
                eng.wait_ge(s_foe, KT * g + j + 1)
            else:
                wait_x(eng, f"y{g}", j + 1)

        def mm3(pe, out, a_hi, a_lo, b_hi, b_lo, start, stop):
            pe.matmul(out, a_hi, b_hi, start=start, stop=False)
            pe.matmul(out, a_hi, b_lo, start=False, stop=False)
            return pe.matmul(out, a_lo, b_hi, start=False, stop=stop)

        def b3(ap, n):
            return ap.unsqueeze(1).broadcast_to((ap.shape[0], n, ap.shape[1]))

        def last(ap, n):
            return ap.unsqueeze(len(ap.shape)).broadcast_to(tuple(ap.shape) + (n,))

        def ktile(k):
            return slice(k * P, (k + 1) * P)

        def e_unit(g, c):
            return U_E + E_UNITS * g + c

        def f_unit(g, c):
            return U_FF + FF_UNITS * g + c

        def slot_count(n, n0):
            if isinstance(n, int):
                return 16 * (n // RAW + 1)
            return (n - n0) * (16 // RAW) + 16 * (n0 // RAW + 1)

        def chunk(i, d):
            if isinstance(i, int) and i == NT - 1:
                return i
            return i if d == 0 else i * -1 + (NT - 2)

        def gcol(a, d, c, h):
            return a[:, d, :, h][:, c:c + 1] if isinstance(c, int) else a[:, d, :, h][:, bass.ds(c, 1)]

        def grow(a, d, c):
            return a[:, d, c] if isinstance(c, int) else a[:, d, bass.ds(c, 1), :].rearrange("p a h -> p (a h)")

        def z_number(zi, shift):
            return zi * 3 + ADA_FIRST if shift is None else zi + shift

        def z_row(zi):
            return zi - 1

        block = top.enter_context(nc.Block())

        @block.sync
        def _(sp):
            sp.dma_start(base[:], k_base).then_inc(s_base, 16)
            sp.dma_start(rows[:], vectors).then_inc(s_rows, 16)
            sp.dma_start(cst[:, 0:CB_EARLY], k_cst[:, 0:CB_EARLY]).then_inc(s_early, 16)

            def unit(n, slot, src, first=False):
                if not first:
                    sp.wait_ge(s_whi, n - RAW + 1)
                    sp.wait_ge(s_wlo, n - RAW + 1)
                sp.dma_start(raw[:, slot], src.rearrange("a p n -> (a p) n")).then_inc(s_raw[slot], 16)

            def units(n0, src, s0, count):
                with sp.Fori(0, count // RAW) as i:
                    for u in range(RAW):
                        unit(i * RAW + n0 + u, (n0 + u) % RAW, src[bass.ds(i * RAW + s0 + u, 1)])

            for u in range(RAW):
                unit(u, u, w_ada[u:u + 1], True)
            units(RAW, w_ada, RAW, ADA_FIRST - RAW)
            sp.dma_start(cst[:, CB_EARLY:], k_cst[:, CB_EARLY:]).then_inc(s_const, 16)
            with sp.Fori(0, Z1_UNITS // RAW) as i:
                for u in range(RAW):
                    n0 = ADA_FIRST + 3 * u
                    unit(i * 12 + n0, n0 % RAW, w_stream[bass.ds(i * RAW + u, 1)])
                    for v in range(2):
                        unit(i * 12 + (n0 + 1 + v), (n0 + 1 + v) % RAW,
                             w_ada[bass.ds(i * (2 * RAW) + (ADA_FIRST + 2 * u + v), 1)])
            for n in range(U_G, U_F):
                unit(n, n % RAW, w_stream[n - SHIFT_A:n - SHIFT_A + 1])
            units(U_F, k_dft, 0, F_UNITS - 1)
            unit(U_ZB - 1, (U_ZB - 1) % RAW, k_dft[F_UNITS - 1:F_UNITS])
            units(U_ZB, w_stream, U_ZB - SHIFT_B, Z2_UNITS - ZA_UNITS)
            with sp.Fori(0, NG) as g:
                for i in range(E_UNITS // RAW):
                    for u in range(RAW):
                        m = i * RAW + u
                        unit(g * E_UNITS + U_E + m, (U_E + m) % RAW, w_stream[Z_COUNT + m:Z_COUNT + m + 1])
            with sp.Fori(0, NG) as g:
                with sp.Fori(0, FF_UNITS // RAW) as i:
                    for u in range(RAW):
                        unit(g * FF_UNITS + i * RAW + U_FF + u, (U_FF + u) % RAW,
                             w_stream[bass.ds(i * RAW + Z_COUNT + E_UNITS + u, 1)])

        @block.tensor
        def _(pe):
            def unit_ready(n):
                pe.wait_ge(s_wlo, n + 1)

            def W(slot, k):
                return w_hi[:, slot, ktile(k)], w_lo[:, slot, ktile(k)]

            pe.wait_ge(s_base, 16)
            pe.wait_ge(s_rows, 16)
            pe.transpose(bank[4][:, 0:V_ROWS], rows[:, :], ident[0:V_ROWS, 0:V_ROWS]).then_inc(s_vec, 1)

            def ada_unit(n, part, slot, b, before):
                unit_ready(n)
                if part == 0 and before is not None:
                    pe.wait_ge(s_arow, before)
                for kk in range(D // ADA_W):
                    k = part * (D // ADA_W) + kk
                    for w in (w_hi, w_lo):
                        m = pe.matmul(bank[5 + b][:, :], c_split[:, k, :], w[:, slot, kk * ADA_W:(kk + 1) * ADA_W],
                                      start=k == 0 and w is w_hi, stop=k == KT - 1 and w is w_lo)
                m.then_inc(s_unit, 1)

            def ada_turn(blk, b):
                pe.wait_ge(s_arow, blk + 1)
                for q in range(ADA_W // P):
                    m = pe.matmul(bank[4][:, bass.ds(blk * (2 * ADA_W // P) + 2 * q, 2)], ada_row[:, b, ktile(q)],
                                  K["sum2"][0:4, :], start=True, stop=True)
                m.then_inc(s_aturn, 1)

            def ada(which):
                for n in range(*which):
                    blk = n // ADA_G
                    ada_unit(n, n % ADA_G, n % SPL, blk % 2, blk - 1 if blk >= 2 else None)
                    if n % ADA_G == 1 and n > ADA_G:
                        ada_turn(n // ADA_G - 1, (n // ADA_G - 1) % 2)
                if which[1] == ADA_FIRST:
                    ada_turn(ADA_FIRST // ADA_G - 1, 1)

            def x_tile(c):
                u = c % 2
                pe.wait_ge(s_xin[u], 16 * (c // 2 + 1))
                if c >= 2:
                    pe.wait_ge(s_xev, 2 * (c - 1))
                for k in range(KT):
                    m = pe.transpose(bank[2 * u + k // 4][:, ktile(k % 4)], x_in[:, u, ktile(k)], ident)
                    if k % 4 == 3:
                        m.then_inc(s_xt, 1)

            pe.wait_ge(s_vecc, 1)
            pe.wait_ge(s_clo, 1)

            def x_tiles(which):
                for c in range(*which):
                    x_tile(c)
                    if c == 1:
                        pe.wait_ge(s_early, 16)
                    if c < NT - 1:
                        ada((c, c + 1))

            def stat(which):
                q = number["ST", which]
                pe.wait_ge(s_accs, KT * (q + 1))
                if q:
                    pe.wait_ge(s_sd, q)
                pe.matmul(bank[7][:, 0:GW], ones, acc_of(which), start=True, stop=True).then_inc(s_st, 1)

            def z_part(zi, zi0, shift, b, first=False):
                if b == 0:
                    unit_ready(z_number(zi, shift))
                j = 3 * zi0 + b
                if not (first and j < 4):
                    pe.wait_ge(s_zev, zi * 3 + b - 3)
                for k in range(KT):
                    if first and zi0 == 0:
                        pe.wait_ge(s_nl, KT * b + k + 1)
                    wh, wl = W(z_number(zi0, shift) % SPL, k)
                    r = slice(b * GW, (b + 1) * GW)
                    m = mm3(pe, bank[j % 4][:, 0:GW], wh, wl, h_hi[:, k, r], h_lo[:, k, r], k == 0, k == KT - 1)
                m.then_inc(s_unit if b == NG - 1 else s_zmm, 1)

            def z_unit(zi, zi0, first, i):
                blk = ADA_FIRST // ADA_G + zi0 // 2
                for b in range(NG):
                    z_part(zi, zi0, None, b, first)
                    if b == 0 and zi0 % 2 == 0 and not (first and zi0 == 0):
                        ada_turn(i * 2 + (blk - 1), (blk - 1) % 2)
                for v in range(2):
                    n0 = ADA_FIRST + 3 * zi0 + 1 + v
                    ada_unit(zi * 3 + (ADA_FIRST + 1 + v), zi0 % 2 * 2 + v, n0 % SPL, blk % 2, i * 2 + (blk - 1))

            def project():
                for u in range(4):
                    z_unit(u, u, True, 0)
                with pe.Fori(1, Z1_UNITS // 4) as i:
                    for u in range(4):
                        z_unit(i * 4 + u, u, False, i)
                for b in range(NG):
                    z_part(ZI_G, ZI_G, SHIFT_A, b)
                    if b == 0:
                        ada_turn(ADA_UNITS // ADA_G - 1, 1)

            def t_tile(c):
                pe.wait_ge(s_zt[0], 16 * (c + 1))
                if c == 0:
                    pe.wait_ge(s_const, 16)
                    pe.wait_ge(s_mod, 2)
                if c:
                    pe.wait_ge(s_tact, 2 * c)
                    pe.wait_ge(s_tdve, 3 * c)
                for j in range(2):
                    m = pe.matmul(bank[4][:, FW * j:FW * (j + 1)], zt[:, 0, j, :], K["cb"], start=True, stop=True)
                m.then_inc(s_tmm, 1)
                for j in range(2):
                    m = pe.transpose(bank[5][:, ktile(j)], zt[:, 0, 2 + j, :], ident)
                m.then_inc(s_tmm, 1)
                for piece in (1, 2):
                    pe.wait_ge(s_zt[piece], 16 * (c + 1))
                    for k in range(4):
                        m = pe.transpose(bank[5 + piece][:, ktile(k)], zt[:, piece, k, :], ident)
                    m.then_inc(s_tmm, 1)

            def token_major():
                for part in range(NG * ZA_UNITS):
                    zi = ZI_T + part // NG
                    z_part(zi, zi, SHIFT_A, part % NG)
                    if part in TURNED:
                        t_tile(TURNED[part])

            def fourier():
                pe.wait_ge(s_tdve, 3 * NT)
                pe.wait_ge(s_zev, 3 * ZI_P)
                for tt in range(LAT // P):
                    n = U_F + tt
                    unit_ready(n)
                    for j in range(2):
                        for cs in range(2):
                            c = slice(FW * j + P * cs, FW * j + P * (cs + 1))
                            r = slice(cs * LAT // 2, (cs + 1) * LAT // 2)
                            m = mm3(pe, bank[2 * cs + j][:, :], ab_hi[:, tt, c], ab_lo[:, tt, c],
                                    w_hi[:, n % SPL, r], w_lo[:, n % SPL, r], tt == 0, tt == LAT // P - 1)
                            if tt == LAT // P - 1 and (j, cs) != (1, 1):
                                m.then_inc(s_fmm, 1)
                    m.then_inc(s_unit, 1)
                pe.wait_ge(s_alt, 1)
                pe.matmul(bank[7][:, 0:2], K["cb"][:, 0:P], alt[:, :], start=True, stop=True).then_inc(s_fmm, 1)
                n = U_F + F_UNITS - 1
                unit_ready(n)
                for j in range(2):
                    for cs in range(2):
                        c = slice(FW * j + P * cs, FW * j + P * (cs + 1))
                        m = mm3(pe, bank[6][:, ktile(j)], ab_hi[:, NT - 1, c], ab_lo[:, NT - 1, c],
                                w_hi[:, n % SPL, ktile(cs)], w_lo[:, n % SPL, ktile(cs)], cs == 0, cs == 1)
                m.then_inc(s_unit, 1)

            def pool_a(g):
                if g:
                    pe.wait_ge(s_pa, g)
                    pe.wait_ge(s_pd, g)
                for i in range(3 * g, 3 * g + 3):
                    kind = int(i == NT - 1)
                    for w in range(4):
                        o = bank[4 + w // 2][GD * (w % 2):GD * (w % 2) + GD, ktile(i - 3 * g)]
                        m = pe.matmul(o, up[:, i, GD * w:GD * (w + 1)],
                                      K["pool"][:, (4 * kind + w) * P:(4 * kind + w + 1) * P],
                                      start=True, stop=True)
                m.then_inc(s_pmm, 1)

            def pool_b(g):
                if g == 0:
                    pe.wait_ge(s_wp, 16 * 4)
                    pe.wait_ge(s_fout, 2)
                pe.wait_ge(s_pa, g + 1)
                pe.wait_ge(s_pd, g + 1)
                for j in range(2):
                    pe.wait_ge(s_mev, 1 if g == 0 else 2 * g + j)
                    pe.matmul(bank[6 + j][:, 0:GW], wp[:, j, :], pT[:, j, :], start=True,
                              stop=True).then_inc(s_cmm, 1)

            flat, half = "p d c h -> p (d c h)", "p c h -> p (c h)"

            def gates(step):
                if step == 1:
                    pe.wait_ge(s_pa, NG)
                    pe.wait_ge(s_pd, NG)
                    pe.wait_ge(s_mev, 1 + 2 * NG)
                    for i in range(NT):
                        m = pe.matmul(bank[4][:, NGC * i:NGC * (i + 1)], gz[0:NGC, ktile(i)], ident[0:NGC, 0:NGC],
                                      start=True, stop=True)
                elif step == 2:
                    pe.wait_ge(s_gd, GD_LF)
                    pe.matmul(bank[5][:, 0:NJ], K["tri_f"], lf[:, 0].rearrange(half), start=True, stop=True)
                    pe.matmul(bank[5][:, NJ:2 * NJ], K["tri_b"], lf[:, 1].rearrange(half), start=True, stop=True)
                    m = pe.matmul(bank[6][:, 0:2 * NJ], ones, lf[:].rearrange(flat), start=True, stop=True)
                elif step == 3:
                    pe.wait_ge(s_gd, GD_AL)
                    pe.matmul(bank[4][0:NJ, 0:P], al[:, 0].rearrange(half), ident, start=True, stop=True)
                    m = pe.matmul(bank[7][0:NJ, 0:P], al[:, 1].rearrange(half), K["rev"], start=True, stop=True)
                elif step == 4:
                    pe.wait_ge(s_gd, GD_SCAN)
                    pe.matmul(bank[5][:, 0:NJ], rows_m[:, 0, :], ident[0:NJ, 0:NJ], start=True, stop=True)
                    m = pe.matmul(bank[6][:, 0:NJ], rows_m[:, 1, :], ident[0:NJ, 0:NJ], start=True, stop=True)
                elif step == 5:
                    pe.wait_ge(s_gd, GD_MCOPY)
                    m = pe.matmul(bank[4][:, 0:NJ], K["rev"], mrev[:, :], start=True, stop=True)
                elif step == 6:
                    pe.wait_ge(s_gd, GD_MTOK)
                    pe.matmul(bank[7][:, 0:NJ], K["last"], mtok[:, 0].rearrange(half), start=True, stop=True)
                    m = pe.matmul(bank[7][:, NJ:2 * NJ], K["first"], mtok[:, 1].rearrange(half), start=True,
                                  stop=True)
                else:
                    pe.wait_ge(s_gd, GD_G)
                    m = pe.matmul(bank[5][0:2 * NJ, 0:P], gneg[:].rearrange(flat), ident, start=True, stop=True)
                m.then_inc(s_gp, 1)

            def pooling_and_gates():
                part = 0
                for what in GATE_PHASE:
                    if what == "z":
                        zi = ZI_P + part // NG
                        if part == 0:
                            pe.wait_ge(s_fout, 2)
                        z_part(zi, zi, SHIFT_B, part % NG)
                        part += 1
                    elif what[0] == "G":
                        gates(int(what[1]))
                    elif what[1] == "a":
                        pool_a(int(what[2]))
                    else:
                        pool_b(int(what[2]))

            def ml_scores(i, d, st, first):
                x = i * 2 + d
                pe.wait_ge(s_ld[d], i * 80 + 80)
                if not (first and d == 0):
                    pe.wait_ge(s_num, x)
                    pe.wait_ge(s_cup, x)
                for h in range(H):
                    m = pe.matmul(bank[4][:, ktile(h)], k_sb[:, d, h, :], q_sb[:, d, h, :], start=True, stop=True)
                m.then_inc(s_qk, 1)
                for h in range(H):
                    m = pe.matmul(bank[5 + h // 2][:, C1 * (h % 2):C1 * (h % 2 + 1)], q_sb[:, d, h, :],
                                  st[:, d, h, :], start=True, stop=True)
                m.then_inc(s_int, 1)

            def ml_values(i, d):
                pe.wait_ge(s_p, i * 2 + d + 1)
                for h in range(H):
                    m = pe.matmul(bank[7 if h < 2 else 4][:, C1 * (h % 2):C1 * (h % 2 + 1)], ew[:, d, h, :],
                                  v_sb[:, d, h, :], start=True, stop=True)
                m.then_inc(s_intra, 1)

            def ml_state(i, d):
                pe.wait_ge(s_wv, i * 2 + d + 1)
                pe.wait_ge(s_iev, i * 2 + d + 1)
                for h in range(H):
                    m = pe.matmul(bank[5 + h // 2][:, C1 * (h % 2):C1 * (h % 2 + 1)], kt_sb[:, d, ktile(h)],
                                  wv[:, d, h, :], start=True, stop=True)
                m.then_inc(s_kvm, 1)

            def ml_step(i, d, st, first, zi, zi0):
                z_part(zi, zi0, SHIFT_B, 0)
                ml_scores(i, d, st, first)
                z_part(zi, zi0, SHIFT_B, 1)
                ml_values(i, d)
                z_part(zi, zi0, SHIFT_B, 2)
                ml_state(i, d)

            def mlstm():
                def turn(t, first):
                    for s in range(2):
                        for d in range(2):
                            ml_step(t * 2 + s, d, st_lat, first and s == 0, t * 4 + (ZI_M + 2 * s + d),
                                    ZI_M + 2 * s + d)

                pe.wait_ge(s_st0, 64)
                pe.wait_ge(s_set, 3)
                turn(0, True)
                with pe.Fori(1, (NT - 1) // 2) as t:
                    turn(t, False)
                for d in range(2):
                    ml_step(NT - 1, d, st_ctx, False, ZI_C + d, ZI_C + d)

            def hm():
                for part in range(2 * NG):
                    z_part(ZI_H + part // NG, ZI_H + part // NG, SHIFT_B, part % NG)
                    if part == 0:
                        pe.wait_ge(s_num, 2 * NT)
                        pe.wait_ge(s_cup, 2 * NT)
                    for c in HM_TILES[part]:
                        pe.wait_ge(s_hs, c + 1)
                        if c >= 3:
                            pe.wait_ge(s_ho, c - 2)
                        for h in range(H):
                            m = pe.transpose(bank[5 + c % 3][:, ktile(h)], hs[:, c % 3, ktile(h)], ident)
                        m.then_inc(s_ht, 1)

            def mixers():
                token_major()
                fourier()
                pooling_and_gates()
                mlstm()
                hm()

            def e1(which):
                g, c_from, c_to = which
                if g == 0:
                    pe.wait_ge(s_zev, 3 * Z_COUNT)

                def one(c, c0, first):
                    n = c + (U_E + g * E_UNITS)
                    unit_ready(n)
                    if not (first and c0 < 2):
                        pe.wait_ge(s_ym, c * 3 + (3 * KT * g - 3))
                    for b, ks in enumerate(((0, 1), (2, 3), (4, 5, 6, 7))):
                        for k in ks:
                            if c == 0:
                                pe.wait_ge(s_mxl, KT * g + k + 1)
                            wh, wl = W((U_E + c0) % SPL, k)
                            m = mm3(pe, bank[3 * (c0 % 2) + b][:, 0:GW], wh, wl, mx_hi[:, k, :], mx_lo[:, k, :],
                                    k == ks[0], k == ks[-1])
                    m.then_inc(s_unit, 1)

                for c in range(c_from, c_to):
                    if g == 0 and c == 1:
                        pe.wait_ge(s_ho, NT)
                    one(c, c, g == 0)

            def stats_before(stage, which):
                at = ORDER.index((stage, which))
                return sum(s == "ST" for s, _ in ORDER[:at])

            def e2(which):
                g, c_from, c_to = which
                pairs = [(0, 1)] if c_from == 0 else []
                for cs in pairs + [(c,) for c in range(2 if c_from == 0 else c_from, c_to)]:
                    for c in cs:
                        if c % 2 and c - c_from < 2:
                            pe.wait_ge(s_sd, stats_before("E2", which))
                        unit_ready(U_E + g * E_UNITS + KT + c)
                        if g or c >= 2:
                            pe.wait_ge(s_e2e, KT * g + c - 1)
                    for ks in ((range(KT - 2), range(KT - 2, KT)) if cs == (0, 1) else (range(KT),)):
                        for c in cs:
                            n = U_E + g * E_UNITS + KT + c
                            for k in ks:
                                if c == 0:
                                    pe.wait_ge(s_yl, KT * g + k + 1)
                                wh, wl = W(n % SPL, k)
                                m = mm3(pe, bank[6 + c % 2][:, 0:GW], wh, wl, yy_hi[:, k, :], yy_lo[:, k, :],
                                        k == 0, k == KT - 1)
                            if ks[-1] == KT - 1:
                                m.then_inc(s_unit, 1)

            def fi(which):
                g, t_from, t_to = which
                if which == (0, 0, 2):
                    pe.wait_ge(s_ym, 3 * KT * NG)
                n0 = U_FF + g * FF_UNITS

                def turn(i, first):
                    for u in range(4):
                        unit_ready(i * 4 + (n0 + u))
                        if not (first and g == 0):
                            if u % 2 == 0:
                                pe.wait_ge(s_sa, i * 2 + (FT * g + u // 2 - 1))
                            else:
                                pe.wait_ge(s_ff, i * 2 + (FT * g + u // 2 - 1))
                        for k in range(KT):
                            if first and u == 0:
                                pe.wait_ge(s_nl, KT * number["HN", f"x{g}"] + k + 1)
                            wh, wl = W((n0 + u) % SPL, k)
                            m = mm3(pe, bank[u][:, 0:GW], wh, wl, h2_hi[:, k, :], h2_lo[:, k, :], k == 0,
                                    k == KT - 1)
                        m.then_inc(s_unit, 1)

                if t_from == 0:
                    turn(0, True)
                with pe.Fori(max(t_from, 1), t_to) as i:
                    turn(i, False)

            def fo(g):
                n0 = U_FF + g * FF_UNITS + 2 * FT

                def turn(i, first):
                    for c in range(4):
                        if not (first and c < 2 and g == 0):
                            pe.wait_ge(s_foe, i * 4 + (KT * g + c - 1))
                        k0 = 0
                        for part, nk in enumerate(FO_K):
                            u = 3 * c + part
                            unit_ready(i * 12 + (n0 + u))
                            if first and c == 0 and part == 0 and g:
                                pe.wait_ge(s_oe, 6 * g)
                            if first and c == 0:
                                pe.wait_ge(s_fl, FT * g + k0 + nk)
                            for k in range(nk):
                                wh, wl = W((n0 + u) % SPL, k)
                                m = mm3(pe, bank[4 + c % 2][:, 0:GW], wh, wl, f_hi[:, k0 + k, :],
                                        f_lo[:, k0 + k, :], k0 + k == 0, k0 + k == FT - 1)
                            k0 += nk
                            m.then_inc(s_unit, 1)

                turn(0, True)
                turn(1, False)

            def ot(g):
                for x in range(6):
                    half, t = divmod(x, 3)
                    if t == 0:
                        wait_x(pe, f"o{g}", 4 * half + 4)
                    if x >= 4:
                        pe.wait_ge(s_oe, 6 * g + x - 3)
                    for k in range(4):
                        m = pe.transpose(bank[4 + x % 4][:, ktile(k)], y2[:, 4 * half + k, ktile(t)], ident)
                    m.then_inc(s_ot, 1)

            pe.wait_ge(s_vecc, 1)
            for stage, w in ORDER:
                if stage == "XT":
                    x_tiles(w)
                elif stage == "ADA":
                    ada(w)
                elif stage == "ST":
                    turned = sum(s == "OT" for s, _ in ORDER[:ORDER.index((stage, w))])
                    projected = sum(v[2] - v[1] for s, v in ORDER[:ORDER.index((stage, w))] if s == "E2")
                    if projected:
                        pe.wait_ge(s_e2e, projected)
                    if turned:
                        pe.wait_ge(s_oe, 6 * turned)
                    stat(w)
                elif stage == "MIX":
                    project()
                    mixers()
                elif stage == "E1":
                    e1(w)
                elif stage == "E2":
                    e2(w)
                elif stage == "FI":
                    fi(w)
                elif stage == "FO":
                    fo(w)
                elif stage == "OT":
                    pe.wait_ge(s_sd, stats_before("OT", w))
                    pe.wait_ge(s_foe, KT * w + KT)
                    ot(w)

        @block.scalar
        def _(act):
            def split(n, n0):
                slot = n0 % RAW
                act.wait_ge(s_raw[slot], slot_count(n, n0))
                if not (isinstance(n, int) and n < SPL):
                    act.wait_ge(s_unit, n - SPL + 1)
                act.copy(w_hi[:, slot], raw[:, slot]).then_inc(s_whi, 1)

            def silu_vectors():
                act.wait_ge(s_vecc, 1)
                act.activation(silu_c[:].rearrange("p k v -> p v k"),
                               vec[:, V_C:V_C + 2 * KT].rearrange("p (v k) -> p v k", v=2), ACT.Silu).then_inc(s_silu, 1)
                act.wait_ge(s_silu, 1)
                act.wait_ge(s_cz, 1)
                act.copy(c_split[:, :, 0:2], silu_c[:]).then_inc(s_chi, 1)

            def sq_piece(which, j):
                n, t = sq_slot(which, j)
                wait_source(act, which, j)
                if n >= 2:
                    act.wait_ge(s_accs, n - 1)
                act.activation(t, source(which)[:, j], ACT.Square).then_inc(s_sq, 1)

            def stat(which):
                q = number["ST", which]
                act.wait_ge(s_st, q + 1)
                if q == 0:
                    act.wait_ge(s_set, 1)
                wait_applied(act, which)
                act.activation(rstd_of(which), bank[7][:, 0:GW], ACT.Sqrt, bias=eps[:, 0:1], scale=1.0 / D).then_inc(s_sd, 1)

            def hn_piece(which, j):
                g = int(which[1])
                first = which[0] == "h"
                scale, shift = (A1, mod[:, 0:8]) if first else (A2, mod[:, 24:32])
                if (which, j) in (("h0", 0), ("x0", 0)):
                    act.wait_ge(s_mod, 1 if first else 2)
                if not first and g and j == 0:
                    act.wait_ge(s_unit, f_unit(g - 1, 2 * FT))
                n, t = hn_slot(which, j)
                act.wait_ge(s_nx, n + 1)
                nf = 0
                for kw in FLAT:
                    if kw[0] == "HN" and number[kw] < number["HN", which]:
                        nf += KT * len(halves(int(kw[1][1])))
                nf += (j + 1) * len(halves(g))
                for a, b, col in halves(g):
                    act.activation(t[:, a:b], t[:, a:b], ACT.Identity, bias=shift[:, j, col:col + 1],
                                   scale=scale[:, j, col:col + 1]).then_inc(s_nf, 1)
                act.wait_ge(s_nf, nf)
                out = h_hi[:, j, g * GW:(g + 1) * GW] if first else h2_hi[:, j]
                act.copy(out, t).then_inc(s_nh, 1)

            def hn(which):
                for j in range(KT):
                    hn_piece(which, j)

            def z_evac(zi, zi0, shift, b, scale=1.0):
                z, z0 = (zi, zi0) if zi0 < ZI_G else (z_row(zi), z_row(zi0))
                if b == NG - 1:
                    act.wait_ge(s_unit, z_number(zi, shift) + 1)
                else:
                    act.wait_ge(s_zmm, zi * 2 + (b + 1))
                if b == 0 and z0 >= 2:
                    act.wait_ge(s_zst[z0 % 2], 16 * (z // 2) if isinstance(z, int) else (z - z0) * 8 + 16 * (z0 // 2))
                act.activation(z_st[:, z0 % 2, b * GW:(b + 1) * GW], bank[(3 * zi0 + b) % 4][:, 0:GW],
                               ACT.Copy, scale=scale).then_inc(s_zev, 1)
                if b == NG - 1:
                    act.wait_ge(s_zev, zi * 3 + 3)
                    act.dma_start(z_dram[bass.ds(z, 1)].rearrange("a p n -> (a p) n"), z_st[:, z0 % 2]).then_inc(s_zst[z0 % 2], 16)

            def z_unit(zi, zi0, shift, scale=1.0):
                split(z_number(zi, shift) + AHEAD, z_number(zi0, shift) + AHEAD)
                for b in range(NG):
                    z_evac(zi, zi0, shift, b, scale)

            def project():
                for zi in range(Z1_UNITS):
                    z_unit(zi, zi, None, DH ** -0.5 if 8 <= zi < 12 else 1.0)
                    ada(z_number(zi, None) + 1, z_number(zi, None) + 3)
                    if zi % 2:
                        ada_out(ADA_FIRST // ADA_G + zi // 2, z_number(zi, None) + 2)
                split(U_G + AHEAD, U_G + AHEAD)
                for b in range(NG):
                    if b == NG - 1:
                        act.wait_ge(s_unit, U_G + 1)
                    else:
                        act.wait_ge(s_zmm, 2 * ZI_G + b + 1)
                    act.copy(gz[:, b * GW:(b + 1) * GW], bank[(3 * ZI_G + b) % 4][:, 0:GW]).then_inc(s_zev, 1)

            def ada(n_from, n_to):
                for n in range(n_from, n_to):
                    split(n + AHEAD, n + AHEAD)
                    if n < ADA_FIRST and n % ADA_G == ADA_G - 1:
                        ada_out(n // ADA_G, n)

            def ada_out(blk, n):
                act.wait_ge(s_unit, n + 1)
                if blk >= 2:
                    act.wait_ge(s_aturn, blk - 1)
                act.copy(ada_row[:, blk % 2], bank[5 + blk % 2][0:4, :]).then_inc(s_arow, 1)

            def t_tile(c):
                act.wait_ge(s_tmm, 4 * c + 1)
                act.copy(ab_hi[:, c], bank[4][:, :]).then_inc(s_tact, 1)
                act.wait_ge(s_tmm, 4 * c + 3)
                if c:
                    act.wait_ge(s_kvst, 16 * c)
                act.copy(kv_st[:, 0], bank[6][:, :]).then_inc(s_tact, 1)

            def pool_a(g):
                act.wait_ge(s_pmm, g + 1)
                if g:
                    act.wait_ge(s_cmm, 2 * g)
                act.copy(pT[:, 0], bank[4][:, 0:GW]).then_inc(s_pa, 1)

            def pool_b(g):
                for j in range(2):
                    x = 1 + 2 * g + j
                    act.wait_ge(s_cmm, x)
                    if x >= 2:
                        act.wait_ge(s_mst[x % 2], 16 * (x // 2))
                    act.activation(m_st[:, x % 2, 0:GW], bank[6 + j][:, 0:GW], ACT.Copy,
                                   scale=vec[:, V_PSC + j:V_PSC + j + 1]).then_inc(s_mev, 1)

            def mixers():
                for part in range(NG * ZA_UNITS):
                    zi = ZI_T + part // NG
                    if part % NG == 0:
                        split(zi + SHIFT_A + AHEAD, zi + SHIFT_A + AHEAD)
                    z_evac(zi, zi, SHIFT_A, part % NG)
                    if part in TURNED:
                        t_tile(TURNED[part])
                for i in range(F_UNITS):
                    split(U_F + i + AHEAD, U_F + i + AHEAD)
                act.wait_ge(s_kvst, 16 * NT)
                for j in range(2):
                    act.wait_ge(s_fmm, 2 * j + 1)
                    act.copy(f_st[:, j, 0:LAT // 2], bank[j][:, :]).then_inc(s_fev, 1)
                act.wait_ge(s_fmm, 4)
                act.activation(f_st[:, :, LAT // 2], bank[7][:, 0:2], ACT.Copy,
                               scale=1.0 / (LAT * GD) ** 0.5).then_inc(s_fev, 1)
                act.wait_ge(s_unit, U_ZB)
                act.copy(m_st[:, 0, 0:2 * P], bank[6][:, 0:2 * P]).then_inc(s_mev, 1)
                flat = "p d c h -> p (d c h)"
                part = 0
                for what in GATE_PHASE:
                    if what == "z":
                        zi = ZI_P + part // NG
                        if part % NG == 0:
                            split(zi + SHIFT_B + AHEAD, zi + SHIFT_B + AHEAD)
                        z_evac(zi, zi, SHIFT_B, part % NG)
                        part += 1
                    elif what[:2] == "Pa":
                        pool_a(int(what[2]))
                    elif what[:2] == "Pb":
                        pool_b(int(what[2]))
                    elif what == "G1":
                        act.wait_ge(s_gd, GD_ABS)
                        act.activation(lse[:].rearrange(flat), absf[:].rearrange(flat), ACT.Exp, scale=-1.0).then_inc(s_ga, 1)
                        act.wait_ge(s_ga, 1)
                        act.activation(lse[:].rearrange(flat), lse[:].rearrange(flat), ACT.Ln, bias=1.0).then_inc(s_ga, 1)
                    elif what == "G7":
                        act.wait_ge(s_gd, GD_LOGS)
                        for a in (em, sdec, wst, carry):
                            act.activation(a[:].rearrange(flat), a[:].rearrange(flat), ACT.Exp).then_inc(s_ga, 1)
                        act.wait_ge(s_ga, 6)

                def turn(t):
                    for s in range(2):
                        for d in range(2):
                            ml_step(t * 2 + s, d, t * 4 + (ZI_M + 2 * s + d), ZI_M + 2 * s + d)

                turn(0)
                with act.Fori(1, (NT - 1) // 2) as t:
                    turn(t)
                for d in range(2):
                    ml_step(NT - 1, d, ZI_C + d, ZI_C + d)
                for part in range(2 * NG):
                    zi = ZI_H + part // NG
                    if part % NG == 0:
                        split(zi + SHIFT_B + AHEAD, zi + SHIFT_B + AHEAD)
                    z_evac(zi, zi, SHIFT_B, part % NG)
                    for c in HM_TILES[part]:
                        act.wait_ge(s_ol[c % 3], 16 * (c // 3 + 1))
                        act.activation(o_sb[:, c % 3].rearrange("p h t -> p (h t)"),
                                       o_sb[:, c % 3].rearrange("p h t -> p (h t)"), ACT.Sigmoid).then_inc(s_so, 1)
                    for c in HM_TILES[part + 1] if part + 1 < len(HM_TILES) else ():
                        o_load(c)

            def o_load(c):
                if c == 0:
                    act.wait_ge(s_hst[0], 16 * NT)
                    act.wait_ge(s_hst[1], 16 * NT)
                if c >= 3:
                    act.wait_ge(s_ho, c - 2)
                act.dma_start(o_sb[:, c % 3],
                              z_dram[16:20, :, c * P:(c + 1) * P].rearrange("a p t -> p a t")).then_inc(s_ol[c % 3], 16)

            def ml_step(i, d, zi, zi0):
                x = i * 2 + d
                c = chunk(i, d)
                split(zi + (SHIFT_B + AHEAD), zi0 + SHIFT_B + AHEAD)
                act.wait_ge(s_t, x + 1)
                act.activation(ew[:, d].rearrange("p h t -> p (h t)"), ew[:, d].rearrange("p h t -> p (h t)"),
                               ACT.Exp).then_inc(s_e, 1)
                act.copy(sdec_now[:, d], grow(sdec, d, c)).then_inc(s_sn, 1)
                z_evac(zi, zi0, SHIFT_B, 0)
                act.wait_ge(s_sn, x + 1)
                act.wait_ge(s_int, x + 1)
                if zi0 >= ZI_M + 2:
                    act.wait_ge(s_num, x - 1)
                for h in range(H):
                    m = act.activation(inter[:, d, h, :], bank[5 + h // 2][:, C1 * (h % 2):C1 * (h % 2 + 1)],
                                       ACT.Copy, scale=sdec_now[:, d, h:h + 1])
                m.then_inc(s_iev, 1)
                z_evac(zi, zi0, SHIFT_B, 1)
                z_evac(zi, zi0, SHIFT_B, 2)

            def mx_piece(g, k):
                x = KT * g + k
                act.wait_ge(s_mx[x % MX], 16 * (x // MX + 1))
                if x == 0:
                    act.wait_ge(s_unit, U_E)
                if g and k == 0:
                    act.wait_ge(s_unit, e_unit(g - 1, KT))
                act.copy(mx_hi[:, k], mx_in[:, x % MX]).then_inc(s_mxh, 1)

            def mx(g):
                for k in range(KT):
                    mx_piece(g, k)

            def pieces(stage, i, n):
                for kind, w in WITH.get(stage, ()):
                    for j in piece_range(kind, i, n):
                        if kind in act_pieces:
                            act_pieces[kind](w, j)

            act_pieces = {"MX": mx_piece, "SQ": sq_piece, "HN": hn_piece}

            merge = z_dram[Z1_UNITS + 4:Z1_UNITS + Z2_UNITS].rearrange("(b c) p t -> c p b t", b=3)

            def mg_load(g, c):
                if KT * g + c >= MG:
                    before = KT * g + c - MG if c >= MG else KT * g - 1
                    act.wait_ge(s_ym, 3 * (before + 1))
                act.dma_start(mg[:, c % MG], merge[c, :, :, g * GW:(g + 1) * GW]).then_inc(s_mg[c % MG], 16)

            def e1(which):
                g, c_from, c_to = which
                if g and c_from == 0:
                    act.wait_ge(s_unit, e_unit(g, 0))
                if g == 0 and c_from == 0:
                    for u in range(3):
                        act.wait_ge(s_host[u], 16 * NT // 3)
                    act.wait_ge(s_new, 80)
                    for u in range(2):
                        act.wait_ge(s_zst[u], 8 * (Z_COUNT - 1))
                if c_from == 0:
                    for c in range(MG):
                        mg_load(g, c)
                for c in range(c_from, c_to):
                    n = U_E + g * E_UNITS + c
                    split(n + AHEAD, n + AHEAD)
                    act.wait_ge(s_mg[c % MG], 16 * (mg_uses(g, c) + 1))
                    act.activation(mg[:, c % MG], mg[:, c % MG], ACT.Sigmoid).then_inc(s_sg, 1)
                    if 1 <= c <= KT - MG:
                        mg_load(g, c - 1 + MG)
                    if g == 0:
                        act.dma_start(xT2[:, c], x_dram[c]).then_inc(s_back, 16)
                    if c:
                        yhigh(g, c - 1)
                    if c < KT - 1:
                        pieces(("E1", which), c - c_from, c_to - c_from)
                if c_to == KT:
                    yhigh(g, KT - 1)
                    pieces(("E1", which), c_to - c_from - 1, c_to - c_from)

            def yhigh(g, c):
                act.wait_ge(s_ya, 2 * (KT * g + c + 1))
                act.copy(yy_hi[:, c], ya[:, c % 2]).then_inc(s_yh, 1)

            def e2(which):
                g, c_from, c_to = which
                if g and c_from == 0:
                    wait_x(act, f"y{g - 1}")
                for c in range(c_from, c_to):
                    n = U_E + g * E_UNITS + KT + c
                    split(n + AHEAD, n + AHEAD)
                    act.wait_ge(s_unit, n + 1)
                    act.copy(y2[:, c], bank[6 + c % 2][:, 0:GW]).then_inc(s_e2e, 1)
                    pieces(("E2", which), c - c_from, c_to - c_from)

            def fi(which):
                g, t_from, t_to = which
                n0 = U_FF + g * FF_UNITS
                if g and t_from == 0:
                    act.wait_ge(s_unit, f_unit(g, 0))

                def high(j, slot):
                    act.wait_ge(s_ff, j + FT * g + 1)
                    act.copy(f_hi[:, bass.ds(j, 1), :].rearrange("p a n -> p (a n)"), ff[:, slot]).then_inc(s_fh, 1)

                def turn(i, first):
                    for u in range(4):
                        split(i * 4 + (n0 + u + AHEAD), n0 + u + AHEAD)
                        if u % 2 == 0:
                            continue
                        if ("FI", which) in WITH:
                            pieces(("FI", which), 2 * (i - t_from) + u // 2, 2 * (t_to - t_from))
                        p = u // 2
                        act.wait_ge(s_unit, i * 4 + (n0 + 2 * p + 1))
                        if not (first and g == 0):
                            act.wait_ge(s_ff, i * 2 + (FT * g + p - 1))
                        act.activation(sa[:, p], bank[2 * p][:, 0:GW], ACT.Silu).then_inc(s_sa, 1)
                        if not (first and p == 0):
                            high(i * 2 + (p - 1), (p - 1) % 2)

                if ("FI", which) in WITH:
                    for i in range(t_from, t_to):
                        turn(i, False)
                else:
                    if t_from == 0:
                        turn(0, True)
                    with act.Fori(max(t_from, 1), t_to) as i:
                        turn(i, False)
                if t_to == FT // 2:
                    high(FT - 1, 1)

            def fo(g):
                n0 = U_FF + g * FF_UNITS + 2 * FT
                if g == 0:
                    wait_x(act, "y2")
                else:
                    act.wait_ge(s_ot, 6 * g)

                def turn(i):
                    for c in range(4):
                        for part in range(3):
                            u = 3 * c + part
                            if n0 + 12 * i + u + AHEAD < U_END:
                                split(i * 12 + (n0 + u + AHEAD), n0 + u + AHEAD)
                        act.wait_ge(s_unit, n0 + 12 * i + 3 * (c + 1))
                        act.copy(y2[:, i * 4 + c], bank[4 + c % 2][:, 0:GW]).then_inc(s_foe, 1)
                        pieces(("FO", g), i * 4 + c, KT)

                turn(0)
                turn(1)

            def ot(g):
                for x in range(6):
                    xx = 6 * g + x
                    act.wait_ge(s_ot, xx + 1)
                    if xx >= 2:
                        act.wait_ge(s_ost[x % 2], 16 * (xx // 2))
                    act.copy(o_st[:, x % 2], bank[4 + x % 4][:, :]).then_inc(s_oe, 1)

            silu_vectors()
            for n in range(AHEAD):
                split(n, n)
            stages = {"ST": stat, "HN": hn, "MX": mx, "E1": e1, "E2": e2, "FI": fi, "FO": fo, "OT": ot}
            for stage, w in ORDER:
                if stage in ("XT", "ADA"):
                    for n in range(*w):
                        if stage == "ADA" or n < NT - 1:
                            ada(n, n + 1)
                        pieces((stage, w), n - w[0], w[1] - w[0])
                elif stage == "MIX":
                    project()
                    mixers()
                elif stage in stages:
                    stages[stage](w)

        @block.vector
        def _(dve):
            def split(n, n0):
                slot = n0 % RAW
                dve.wait_ge(s_whi, n + 1)
                dve.tensor_tensor(w_lo[:, slot], raw[:, slot], w_hi[:, slot].bitcast(F32),
                                  ALU.subtract).then_inc(s_wlo, 1)

            def x_evac(c):
                for half in range(2):
                    dve.wait_ge(s_xt, 2 * c + half + 1)
                    ps = bank[2 * (c % 2) + half][:, :].rearrange("p (k r w) -> p k r w", k=4, r=2)
                    out = xT[:, 4 * half:4 * half + 4, c * P:(c + 1) * P].rearrange("p k (r w) -> p k r w", r=2)
                    if half == 0:
                        pos = last(K["pos_r"].rearrange("p (k r) -> p k r", k=4)[:, :, 2 * c:2 * c + 2], GRID_W)
                    else:
                        pos = K["pos_c"].rearrange("p (k w) -> p k w", k=4).unsqueeze(2).broadcast_to(
                            (P, 4, 2, GRID_W))
                    dve.tensor_tensor(out, ps, pos, ALU.add).then_inc(s_xev, 1)

            def gain(i):
                return last(vec[:, V_NORM + 8 * i:V_NORM + 8 * (i + 1)], 2)

            def mod_columns(a, b, chain):
                dve.wait_ge(s_aturn, b // ADA_G)
                dve.tensor_tensor(mod[:, a:b], bank[4][:, 2 * a:2 * b].rearrange("p (j v) -> p j v", v=2),
                                  last(vec[:, V_BADA + a:V_BADA + b], 2), ALU.add).then_inc(s_modc, 1)
                dve.wait_ge(s_modc, chain)

            def modulation():
                mod_columns(0, ADA_FIRST, 1)
                dve.scalar_tensor_tensor(A1[:], mod[:, 8:16], 1.0, gain(0), ALU.add, ALU.mult).then_inc(s_mod, 1)

            def modulation_rest():
                mod_columns(ADA_FIRST, ADA_UNITS, 2)
                dve.tensor_tensor(G1[:], mod[:, 16:24], gain(1), ALU.mult).then_inc(s_modc, 1)
                dve.tensor_tensor(G2[:], mod[:, 40:48], gain(3), ALU.mult).then_inc(s_modc, 1)
                dve.scalar_tensor_tensor(A2[:], mod[:, 32:40], 1.0, gain(2), ALU.add, ALU.mult).then_inc(s_mod, 1)
                dve.wait_ge(s_modc, 4)
                dve.wait_ge(s_mod, 2)

            def sq_piece(which, j):
                if which not in POOL_SQ:
                    sum_square(dve, which, j)

            def stat(which):
                q = number["ST", which]
                dve.wait_ge(s_sd, q + 1)
                dve.reciprocal(rstd_of(which), rstd_of(which)).then_inc(s_rs, 1)
                dve.wait_ge(s_rs, q + 1)

            def hn_scale(which, j):
                n, t = hn_slot(which, j)
                slots = hn_slots(which)
                if n >= slots:
                    dve.wait_ge(s_nl, n - slots + 1)
                dve.tensor_tensor(t, source(which)[:, j], rstd_of(which), ALU.mult).then_inc(s_nx, 1)

            def hn_low(which, j):
                n, t = hn_slot(which, j)
                g = int(which[1])
                dve.wait_ge(s_nh, n + 1)
                if which[0] == "h":
                    r = slice(g * GW, (g + 1) * GW)
                    lo, hi = h_lo[:, j, r], h_hi[:, j, r]
                else:
                    lo, hi = h2_lo[:, j], h2_hi[:, j]
                dve.tensor_tensor(lo, t, hi.bitcast(F32), ALU.subtract).then_inc(s_nl, 1)

            def hn(which):
                for j in range(KT + 2):
                    if j < KT:
                        hn_scale(which, j)
                    if j >= 2:
                        hn_low(which, j - 2)

            def hn_piece(which, j):
                hn_scale(which, j)
                if j:
                    hn_low(which, j - 1)
                if j == KT - 1:
                    hn_low(which, j)

            def x_piece(which, j):
                g = int(which[1])
                if (which, j) == ("y0", 0):
                    dve.wait_ge(s_back, 16 * KT)
                dve.tensor_tensor(y2[:, j], y2[:, j], rstd[:, :], ALU.mult).then_inc(s_xs, 1)
                dve.wait_ge(s_xs, KT * number["X", which] + j + 1)
                G = G1 if which[0] == "y" else G2
                for a, b, col in halves(g):
                    x = xT2[:, j, g * GW + a:g * GW + b]
                    out = x if which[0] == "y" else y2[:, j, a:b]
                    m = dve.scalar_tensor_tensor(out, y2[:, j, a:b], G[:, j, col:col + 1], x, ALU.mult, ALU.add)
                m.then_inc(s_app, 1)

            def xstage(which):
                for j in range(KT):
                    x_piece(which, j)

            def project():
                with dve.Fori(0, Z1_UNITS // 4) as i:
                    for u in range(12):
                        split(i * 12 + (ADA_FIRST + u + AHEAD), ADA_FIRST + u + AHEAD)
                split(U_G + AHEAD, U_G + AHEAD)
                modulation_rest()

            def t_tile(c):
                if c < LAT // P:
                    dve.wait_ge(s_zt[0], 16 * (c + 1))
                    dve.tensor_reduce(red[:, c], zt[:, 0, 0:2, :].rearrange("p j (t e) -> p j e t", e=2), AX.X,
                                      ALU.add).then_inc(s_red, 1)
                dve.wait_ge(s_tact, 2 * c + 1)
                dve.tensor_tensor(ab_lo[:, c], bank[4][:, :], ab_hi[:, c].bitcast(F32), ALU.subtract).then_inc(s_tdve, 1)
                dve.wait_ge(s_tmm, 4 * c + 2)
                dve.tensor_copy(up[:, c], bank[5][:, 0:FW]).then_inc(s_tdve, 1)
                dve.wait_ge(s_tmm, 4 * c + 4)
                if c:
                    dve.wait_ge(s_kvst, 16 * c)
                dve.tensor_copy(kv_st[:, 1], bank[7][:, :]).then_inc(s_tdve, 1)

            n_gd = [0]

            def link(m):
                n_gd[0] += 1
                m.then_inc(s_gd, 1)
                dve.wait_ge(s_gd, n_gd[0])

            def gates(step):
                flat, half = "p d c h -> p (d c h)", "p c h -> p (c h)"

                def col(d, kind):
                    return gts[:, :, 8 * d + 4 * kind:8 * d + 4 * kind + 4]

                dve.wait_ge(s_gp, step)
                if step == 1:
                    dve.wait_ge(s_gl, 32)
                    link(dve.tensor_tensor(gts[:], bank[4][:, 0:NT * NGC].rearrange("p (c g) -> p c g", c=NT),
                                           b3(bg[:], NT), ALU.add))
                    for d in range(2):
                        link(dve.scalar_tensor_tensor(absf[:, d], col(d, 1), -1.0, col(d, 1), ALU.mult, ALU.max))
                    assert n_gd[0] == GD_ABS
                    dve.wait_ge(s_ga, 2)
                    for d in range(2):
                        link(dve.scalar_tensor_tensor(lf[:, d], col(d, 1), 0.0, lse[:, d], ALU.min, ALU.subtract))
                    assert n_gd[0] == GD_LF
                elif step == 2:
                    link(dve.tensor_copy(cum[:].rearrange(flat), bank[5][:, 0:2 * NJ]))
                    link(dve.tensor_copy(blast[:].rearrange(flat), bank[6][:, 0:2 * NJ]))
                    for d in range(2):
                        link(dve.tensor_tensor(al[:, d], col(d, 0), cum[:, d], ALU.subtract))
                    assert n_gd[0] == GD_AL
                elif step == 3:
                    for d in range(2):
                        link(dve.tensor_copy(rows_a[:, d], bank[4 + 3 * d][0:NJ, 0:P]))
                    for d in range(2):
                        link(dve.tensor_tensor_scan(rows_m[:, d], rows_a[:, d], rows_a[:, d], -3e38, ALU.max,
                                                    ALU.max))
                    assert n_gd[0] == GD_SCAN
                elif step == 4:
                    link(dve.tensor_copy(mtok[:, 0].rearrange(half), bank[5][:, 0:NJ]))
                    link(dve.tensor_copy(mrev[:, :], bank[6][:, 0:NJ]))
                    assert n_gd[0] == GD_MCOPY
                elif step == 5:
                    link(dve.tensor_copy(mtok[:, 1].rearrange(half), bank[4][:, 0:NJ]))
                    assert n_gd[0] == GD_MTOK
                elif step == 6:
                    stabilisers(flat)
                else:
                    link(dve.tensor_copy(g_rows[:, :], bank[5][0:2 * NJ, 0:P]))
                    assert n_gd[0] == GD_END

            def stabilisers(flat):
                link(dve.tensor_copy(mlast[:].rearrange(flat), bank[7][:, 0:2 * NJ]))
                NL = NT - 1
                link(dve.tensor_copy(mprev[:, 0, 0], sm[:, 0]))
                link(dve.tensor_copy(mprev[:, 1, NL - 1], sm[:, 1]))
                link(dve.memset(mprev[:, :, NL], 0.0))
                for s in range(NL):
                    for d in range(2):
                        c = s if d == 0 else NL - 1 - s
                        before = mprev[:, d, c] if s == 0 else mnew[:, d, c + (1 if d else -1)]
                        link(dve.tensor_tensor(mnew[:, d, c], before, mlast[:, d, c], ALU.max))
                        link(dve.tensor_tensor(mnew[:, d, c], mnew[:, d, c], blast[:, d, c], ALU.add))
                link(dve.tensor_tensor(mnew[:, :, NL], mprev[:, :, NL], mlast[:, :, NL], ALU.max))
                link(dve.tensor_tensor(mnew[:, :, NL], mnew[:, :, NL], blast[:, :, NL], ALU.add))
                link(dve.tensor_copy(mprev[:, 0, 1:NL], mnew[:, 0, 0:NL - 1]))
                link(dve.tensor_copy(mprev[:, 1, 0:NL - 1], mnew[:, 1, 1:NL]))
                link(dve.tensor_tensor(gneg[:], mprev[:], mtok[:], ALU.max))
                link(dve.tensor_scalar(gneg[:], gneg[:], -1.0, None, ALU.mult))
                assert n_gd[0] == GD_G
                link(dve.tensor_tensor(em[:], gneg[:], cum[:], ALU.subtract))
                link(dve.tensor_tensor(sdec[:], mprev[:], gneg[:], ALU.add))
                link(dve.tensor_tensor(wst[:], al[:], blast[:], ALU.add))
                link(dve.tensor_tensor(wst[:], wst[:], mnew[:], ALU.subtract))
                link(dve.tensor_tensor(carry[:], blast[:], mprev[:], ALU.add))
                link(dve.tensor_tensor(carry[:], carry[:], mnew[:], ALU.subtract))
                assert n_gd[0] == GD_LOGS

            def mixers():
                for part in range(NG * ZA_UNITS):
                    if part % NG == 0:
                        n = ZI_T + SHIFT_A + part // NG + AHEAD
                        split(n, n)
                    if part in TURNED:
                        t_tile(TURNED[part])
                dve.memset(wp[:], 0.0).then_inc(s_wp0, 1)
                dve.wait_ge(s_red, LAT // P)
                dve.tensor_reduce(red_sum[:], red[:].rearrange("p c j e -> p j e c"), AX.X, ALU.add).then_inc(s_redc, 1)
                dve.wait_ge(s_redc, 1)
                dve.tensor_tensor(alt[:], red_sum[:, :, 0], red_sum[:, :, 1], ALU.subtract).then_inc(s_alt, 1)
                for i in range(F_UNITS):
                    split(U_F + i + AHEAD, U_F + i + AHEAD)
                half = LAT // 2
                for j in range(2):
                    dve.wait_ge(s_fev, j + 1)
                    if j == 0:
                        dve.wait_ge(s_fmm, 2)
                    else:
                        dve.wait_ge(s_unit, U_ZB - 1)
                    dve.tensor_tensor(f_st[:, j, half + 1:LAT], f_st[:, j, half - 1:0:-1],
                                      bank[2 + j][:, half - 1:0:-1], ALU.subtract).then_inc(s_fd, 1)
                    dve.wait_ge(s_fd, j + 1)
                    dve.tensor_tensor(f_st[:, j, 0:half], f_st[:, j, 0:half], bank[2 + j][:, :],
                                      ALU.add).then_inc(s_fout, 1)
                part = 0
                for what in GATE_PHASE:
                    if what == "z":
                        if part % NG == 0:
                            n = ZI_P + SHIFT_B + part // NG + AHEAD
                            split(n, n)
                        part += 1
                    elif what[:2] == "Pa":
                        g = int(what[2])
                        dve.wait_ge(s_pmm, g + 1)
                        if g:
                            dve.wait_ge(s_cmm, 2 * g)
                        dve.tensor_copy(pT[:, 1], bank[5][:, 0:GW]).then_inc(s_pd, 1)
                    elif what[0] == "G":
                        gates(int(what[1]))
                        if what == "G1":
                            dve.wait_ge(s_mst[0], 64)
                            dve.wait_ge(s_mst[1], 48)
                            dve.wait_ge(s_fst, 32)
                            dve.memset(v_sb[:], 1.0).then_inc(s_set, 1)
                            dve.memset(st_ctx[:], 0.0).then_inc(s_set, 1)
                mlstm()

            def ml_step(i, d, st, first, n, n0):
                x = i * 2 + d
                c = chunk(i, d)
                mask = K["mask_b"] if d else K["mask_f"]
                dve.wait_ge(s_ld[d], i * 80 + 80)
                if not first:
                    dve.wait_ge(s_intra, x - 1)
                for h in range(H):
                    m = dve.scalar_tensor_tensor(ew[:, d, h], g_sb[:, d, h], gcol(al, d, c, h), mask, ALU.add,
                                                 ALU.min)
                m.then_inc(s_t, 1)
                if not first:
                    dve.wait_ge(s_kvm, x - 1)
                dve.tensor_tensor(wv[:, d], v_sb[:, d], last(grow(wst, d, c), C1), ALU.mult).then_inc(s_wv, 1)
                split(n, n0)
                dve.wait_ge(s_e, x + 1)
                dve.wait_ge(s_qk, x + 1)
                dve.tensor_tensor(ew[:, d].rearrange("p h t -> p (h t)"), ew[:, d].rearrange("p h t -> p (h t)"),
                                  bank[4][:, :], ALU.mult).then_inc(s_p, 1)
                dve.wait_ge(s_iev, x + 1)
                if not first:
                    dve.wait_ge(s_hst[d], i * 16)
                dve.wait_ge(s_intra, x + 1)
                for hh in range(2):
                    r = slice(2 * hh, 2 * hh + 2)
                    m = dve.tensor_tensor(num[:, d, r].rearrange("p h e -> p (h e)"),
                                          inter[:, d, r].rearrange("p h e -> p (h e)"),
                                          bank[7 if hh == 0 else 4][:, 0:2 * C1], ALU.add)
                m.then_inc(s_num, 1)
                dve.wait_ge(s_num, x + 1)
                dd = num[:, d, :, DH]
                dve.scalar_tensor_tensor(den[:, d], dd, -1.0, dd, ALU.mult, ALU.max).then_inc(s_den, 1)
                dve.wait_ge(s_den, x * 3 + 1)
                dve.tensor_tensor(den[:, d], den[:, d], grow(em, d, c), ALU.max).then_inc(s_den, 1)
                dve.wait_ge(s_den, x * 3 + 2)
                dve.reciprocal(den[:, d], den[:, d]).then_inc(s_den, 1)
                dve.wait_ge(s_den, x * 3 + 3)
                dve.tensor_tensor(num[:, d, :, 0:DH], num[:, d, :, 0:DH], last(den[:, d], DH),
                                  ALU.mult).then_inc(s_hd, 1)
                dve.wait_ge(s_kvm, x + 1)
                for h in range(H):
                    m = dve.scalar_tensor_tensor(st[:, d, h], st[:, d, h], gcol(carry, d, c, h),
                                                 bank[5 + h // 2][:, C1 * (h % 2):C1 * (h % 2 + 1)], ALU.mult,
                                                 ALU.add)
                m.then_inc(s_cup, 1)

            def mlstm():
                def turn(t, first):
                    for s in range(2):
                        for d in range(2):
                            n0 = ZI_M + SHIFT_B + AHEAD + 2 * s + d
                            ml_step(t * 2 + s, d, st_lat, first and s == 0, t * 4 + n0, n0)

                dve.wait_ge(s_ga, 6)
                dve.wait_ge(s_st0, 64)
                turn(0, True)
                with dve.Fori(1, (NT - 1) // 2) as t:
                    turn(t, False)
                for d in range(2):
                    n = ZI_C + SHIFT_B + AHEAD + d
                    ml_step(NT - 1, d, st_ctx, False, n, n)
                for part in range(2 * NG):
                    if part % NG == 0:
                        n = ZI_H + SHIFT_B + AHEAD + part // NG
                        split(n, n)
                    tiles = HM_TILES[part]
                    for c in tiles:
                        dve.wait_ge(s_hl[c % 3], 16 * (c // 3 + 1))
                        if c >= 3:
                            dve.wait_ge(s_ht, c - 2)
                        dve.tensor_tensor(hs[:, c % 3], hf_sb[:, c % 3, 0], hf_sb[:, c % 3, 1], ALU.add).then_inc(s_hs, 1)
                    for c in tiles:
                        dve.wait_ge(s_ht, c + 1)
                        dve.wait_ge(s_so, c + 1)
                        if c >= 3:
                            dve.wait_ge(s_host[c % 3], 16 * (c // 3))
                        dve.tensor_tensor(ho[:, c % 3].rearrange("p h t -> p (h t)"),
                                          o_sb[:, c % 3].rearrange("p h t -> p (h t)"), bank[5 + c % 3][:, :],
                                          ALU.mult).then_inc(s_ho, 1)

            def mx_piece(g, k):
                dve.wait_ge(s_mxh, KT * g + k + 1)
                dve.tensor_tensor(mx_lo[:, k], mx_in[:, (KT * g + k) % MX], mx_hi[:, k].bitcast(F32),
                                  ALU.subtract).then_inc(s_mxl, 1)

            def mx(g):
                for k in range(KT):
                    mx_piece(g, k)

            def pieces(stage, i, n):
                for kind, w in WITH.get(stage, ()):
                    for j in piece_range(kind, i, n):
                        dve_pieces[kind](w, j)

            dve_pieces = {"MX": mx_piece, "SQ": sq_piece, "HN": hn_piece, "X": x_piece}

            def ylow(g, c):
                dve.wait_ge(s_yh, KT * g + c + 1)
                dve.tensor_tensor(yy_lo[:, c], ya[:, c % 2], yy_hi[:, c].bitcast(F32),
                                  ALU.subtract).then_inc(s_yl, 1)

            def e1(which):
                g, c_from, c_to = which
                for c in range(c_from, c_to):
                    n = U_E + g * E_UNITS + c
                    split(n + AHEAD, n + AHEAD)
                    dve.wait_ge(s_unit, n + 1)
                    x = KT * g + c
                    dve.wait_ge(s_sg, x + 1)
                    if x >= 2:
                        dve.wait_ge(s_yl, x - 1)
                    for b in range(3):
                        if b and x:
                            dve.wait_ge(s_ya, 2 * (x - 1) + b)
                        dve.tensor_tensor(yb[:, b - 1] if b else ya[:, c % 2], mg[:, c % MG, b], bank[3 * (c % 2) + b][:, 0:GW],
                                          ALU.mult).then_inc(s_ym, 1)
                    if c:
                        ylow(g, c - 1)
                    if c < KT - 1:
                        pieces(("E1", which), c - c_from, c_to - c_from)
                if c_to == KT:
                    ylow(g, KT - 1)
                    pieces(("E1", which), c_to - c_from - 1, c_to - c_from)

            def e2(which):
                g, c_from, c_to = which
                for c in range(c_from, c_to):
                    n = U_E + g * E_UNITS + KT + c
                    split(n + AHEAD, n + AHEAD)
                    pieces(("E2", which), c - c_from, c_to - c_from)

            def fi(which):
                g, t_from, t_to = which
                n0 = U_FF + g * FF_UNITS

                def low(j, slot):
                    dve.wait_ge(s_fh, j + FT * g + 1)
                    sl = bass.ds(j, 1)
                    dve.tensor_tensor(f_lo[:, sl, :].rearrange("p a n -> p (a n)"), ff[:, slot],
                                      f_hi[:, sl, :].rearrange("p a n -> p (a n)").bitcast(F32),
                                      ALU.subtract).then_inc(s_fl, 1)

                def turn(i, first):
                    for u in range(4):
                        split(i * 4 + (n0 + u + AHEAD), n0 + u + AHEAD)
                        if u % 2 == 0:
                            continue
                        if ("FI", which) in WITH:
                            pieces(("FI", which), 2 * (i - t_from) + u // 2, 2 * (t_to - t_from))
                        p = u // 2
                        dve.wait_ge(s_unit, i * 4 + (n0 + 2 * p + 2))
                        dve.wait_ge(s_sa, i * 2 + (FT * g + p + 1))
                        if not (first and g == 0):
                            dve.wait_ge(s_fl, i * 2 + (FT * g + p - 1))
                        dve.tensor_tensor(ff[:, p], sa[:, p], bank[2 * p + 1][:, 0:GW], ALU.mult).then_inc(s_ff, 1)
                        if not (first and p == 0):
                            low(i * 2 + (p - 1), (p - 1) % 2)

                if ("FI", which) in WITH:
                    for i in range(t_from, t_to):
                        turn(i, False)
                else:
                    if t_from == 0:
                        turn(0, True)
                    with dve.Fori(max(t_from, 1), t_to) as i:
                        turn(i, False)
                if t_to == FT // 2:
                    low(FT - 1, 1)

            def fo(g):
                n0 = U_FF + g * FF_UNITS + 2 * FT
                for u in range(3 * KT):
                    if n0 + u + AHEAD < U_END:
                        split(n0 + u + AHEAD, n0 + u + AHEAD)
                    if u % 3 == 2:
                        pieces(("FO", g), u // 3, KT)

            dve.memset(eps[:], EPS).then_inc(s_set, 1)
            dve.memset(c_wide[:], 0.0).then_inc(s_cz0, 1)
            dve.wait_ge(s_cz0, 1)
            dve.tensor_copy(c_split[:], b3(c_wide[:], KT)).then_inc(s_cz, 1)
            dve.wait_ge(s_vec, 1)
            dve.tensor_copy(vec[:], bank[4][:, 0:V_ROWS]).then_inc(s_vecc, 1)
            dve.wait_ge(s_vecc, 1)
            dve.wait_ge(s_chi, 1)
            dve.tensor_tensor(c_split[:, :, 2:4], silu_c[:], c_split[:, :, 0:2].bitcast(F32),
                              ALU.subtract).then_inc(s_clo, 1)
            for n in range(AHEAD - 1):
                split(n, n)
            dve.wait_ge(s_early, 16)

            def x_tiles(which):
                for c in range(*which):
                    split(c + AHEAD - 1, c + AHEAD - 1)
                    if c < NT - 1:
                        x_evac(c)
                    else:
                        for half in range(2):
                            dve.wait_ge(s_xt, 2 * c + half + 1)
                            dve.tensor_copy(xT[:, 4 * half:4 * half + 4, LAT:T],
                                            bank[half][:, :].rearrange("p (k t) -> p k t", k=4)).then_inc(s_xev, 1)
                    pieces(("XT", which), c - which[0], which[1] - which[0])

            stages = {"ST": stat, "HN": hn, "X": xstage, "MX": mx, "E1": e1, "E2": e2, "FI": fi, "FO": fo}
            for stage, w in ORDER:
                if stage == "XT":
                    x_tiles(w)
                elif stage == "ADA":
                    for n in range(*w):
                        split(n + AHEAD, n + AHEAD)
                        pieces((stage, w), n - w[0], w[1] - w[0])
                elif stage == "MOD":
                    modulation()
                elif stage == "MIX":
                    project()
                    mixers()
                elif stage in stages:
                    stages[stage](w)

        @block.gpsimd
        def _(pool):
            def one(ap):
                return ap.rearrange("a p n -> (a p) n")

            def x_load(i, us, first):
                for u in us:
                    if not first:
                        pool.wait_ge(s_xt, i * 4 + 2 * u - 2)
                    pool.dma_start(x_in[:, u], x_sample[0, bass.ds(i * 2 * P + u * P, P), :]).then_inc(s_xin[u], 16)

            x_load(0, (0, 1), True)
            with pool.Fori(1, 4) as i:
                x_load(i, (0, 1), False)
            pool.wait_ge(s_xt, 14)
            pool.dma_start(x_in[:, 0], x_prompt[0]).then_inc(s_xin[0], 16)

            for j in range(KT):
                sum_square(pool, "h1", j)
            for j in range(KT):
                sum_square(pool, "h2", j)

            pool.wait_ge(s_xev, 2 * NT)
            pool.wait_ge(s_nl, KT * NG)
            for k in range(KT):
                pool.dma_start(x_dram[k], xT[:, k]).then_inc(s_spill, 16)

            def t_load(c):
                t = slice(c * P, (c + 1) * P)
                for piece, z0 in enumerate((0, 8, 12)):
                    if c:
                        pool.wait_ge(s_tmm, 4 * (c - 1) + piece + 2)
                        if piece == 0:
                            pool.wait_ge(s_red, c)
                    pool.dma_start(zt[:, piece], z_dram[z0:z0 + 4, :, t].rearrange("a p t -> p a t")).then_inc(s_zt[piece], 16)

            def kv_store(c):
                pool.wait_ge(s_tact, 2 * c + 2)
                pool.wait_ge(s_tdve, 3 * c + 3)
                pool.dma_start(kv_dram[c], kv_st[:].rearrange("p a c -> p (a c)")).then_inc(s_kvst, 16)

            pool.wait_ge(s_spill, 16 * KT)
            pool.wait_ge(s_unit, U_G)
            pool.wait_ge(s_aturn, ADA_UNITS // ADA_G)
            for u in range(2):
                pool.wait_ge(s_zst[u], 16 * Z1_UNITS // 2)
            t_load(0)
            for c in range(1, NT):
                t_load(c)
                kv_store(c - 1)
            kv_store(NT - 1)
            pool.wait_ge(s_wp0, 1)
            for w in range(4):
                r = slice(GD * (w % 2), GD * (w % 2) + GD)
                pool.dma_start(wp[r, w // 2, r], w_pool[0, w]).then_inc(s_wp, 16)
            for j in range(2):
                pool.wait_ge(s_fev, 3)
                pool.wait_ge(s_fout, j + 1)
                pool.dma_start(mix_dram[j, :, 0:LAT], f_st[:, j]).then_inc(s_fst, 16)
            pool.wait_ge(s_mev, 1)
            pool.dma_start(mix_dram[0:2, :, LAT:T].rearrange("a p t -> p a t"),
                           m_st[:, 0, 0:2 * P].rearrange("p (a t) -> p a t", a=2)).then_inc(s_mst[0], 16)
            pool.wait_ge(s_unit, U_ZB)
            pool.dma_start(bg[:], b_gate.rearrange("a d i h -> a (d i h)").broadcast_to((P, NGC))).then_inc(s_gl, 16)
            pool.dma_start(sm[:].rearrange("p d h -> p (d h)"),
                           state_m.rearrange("a e d h -> (a e) (d h)").broadcast_to((P, 2 * H))).then_inc(s_gl, 16)
            for x in range(1, 1 + 2 * NG):
                pool.wait_ge(s_mev, x + 1)
                g, j = divmod(x - 1, 2)
                pool.dma_start(mix_dram[2 + j, :, g * GW:(g + 1) * GW], m_st[:, x % 2, 0:GW]).then_inc(s_mst[x % 2], 16)
            for d in range(2):
                pool.dma_start(st_lat[:, d, :, 0:DH], state_C[0, 0, d].rearrange("h k v -> k h v")).then_inc(s_st0, 16)
                pool.dma_start(st_lat[:, d, :, DH], state_n[0, 0, d].rearrange("h k -> k h"), allow_slow_non_contiguous=True).then_inc(s_st0, 16)
            pool.wait_ge(s_mst[0], 64)
            pool.wait_ge(s_mst[1], 48)
            pool.wait_ge(s_fst, 32)
            pool.wait_ge(s_set, 2)

            def ml_load_g(i, d):
                pool.dma_start(g_sb[:, d].rearrange("p h t -> p (h t)"),
                               g_dram[bass.ds(chunk(i, d) + NT * d, 1), :].broadcast_to((P, H * P))).then_inc(s_ld[d], 16)

            def ml_load(i, d, first):
                c = chunk(i, d)
                if not first:
                    pool.wait_ge(s_kvm, i * 2 + d - 1)
                t = bass.ds(c * P, P)
                pool.dma_start(q_sb[:, d], z_dram[4:8, :, t].rearrange("a p t -> p a t")).then_inc(s_ld[d], 16)
                pool.dma_start(k_sb[:, d], z_dram[8:12, :, t].rearrange("a p t -> p a t")).then_inc(s_ld[d], 16)
                kv = one(kv_dram[bass.ds(c, 1)])
                pool.dma_start(kt_sb[:, d], kv[:, 0:MW]).then_inc(s_ld[d], 16)
                pool.dma_start(v_sb[:, d, :, 0:DH], kv[:, MW:2 * MW].rearrange("p (h e) -> p h e", h=H)).then_inc(s_ld[d], 16)
                if not first:
                    ml_load_g(i, d)

            def ml_store(i, d):
                pool.wait_ge(s_hd, i * 2 + d + 1)
                pool.dma_start(one(h_dram[bass.ds(chunk(i, d) + NT * d, 1)]).rearrange("p (h e) -> p h e", h=H),
                               num[:, d, :, 0:DH]).then_inc(s_hst[d], 16)

            for d in range(2):
                ml_load(0, d, True)
            pool.wait_ge(s_gd, GD_END)
            pool.dma_start(g_dram.rearrange("a (h t) -> (a h) t", h=H), g_rows[:, :]).then_inc(s_gst, 16)
            pool.wait_ge(s_gst, 16)
            for d in range(2):
                ml_load_g(0, d)
            with pool.Fori(1, NT - 1) as i:
                for d in range(2):
                    ml_store(i - 1, d)
                    ml_load(i, d, False)
            for d in range(2):
                ml_store(NT - 2, d)
                ml_load(NT - 1, d, False)
            for d in range(2):
                ml_store(NT - 1, d)
                pool.wait_ge(s_cup, 2 * NT - 1 + d)
                pool.dma_start(new_C[0, 0, d].rearrange("h k v -> k h v"), st_ctx[:, d, :, 0:DH]).then_inc(s_new, 16)
                pool.dma_start(new_n[0, 0, d].rearrange("h k -> k h"), st_ctx[:, d, :, DH], allow_slow_non_contiguous=True).then_inc(s_new, 16)
            pool.dma_start(new_m[0], mnew[0:1, :, NT - 1]).then_inc(s_new, 16)
            pool.wait_ge(s_hst[0], 16 * NT)
            pool.wait_ge(s_hst[1], 16 * NT)

            both = h_dram.rearrange("(d c) p n -> c p d n", d=2)

            def hm_load(c):
                if c >= 3:
                    pool.wait_ge(s_hs, c - 2)
                pool.dma_start(hf_sb[:, c % 3], both[c]).then_inc(s_hl[c % 3], 16)

            def hm_store(c):
                pool.wait_ge(s_ho, c + 1)
                pool.dma_start(mix_dram[4:8, :, c * P:(c + 1) * P].rearrange("a p t -> p a t"), ho[:, c % 3]).then_inc(s_host[c % 3], 16)

            def mx_load(x):
                g, k = divmod(x, KT)
                if x >= MX:
                    pool.wait_ge(s_mxl, x - MX + 1)
                pool.dma_start(mx_in[:, x % MX], mix_dram[k, :, g * GW:(g + 1) * GW]).then_inc(s_mx[x % MX], 16)

            for c in range(3):
                hm_load(c)
            for k in range(MX):
                mx_load(k)
            for c in range(NT):
                hm_store(c)
                if c + 3 < NT:
                    hm_load(c + 3)
            pool.wait_ge(s_new, 80)
            pool.wait_ge(s_unit, U_E)
            for u in range(3):
                pool.wait_ge(s_host[u], 16)
            for k in range(MX, KT):
                mx_load(k)
            for u in range(3):
                pool.wait_ge(s_host[u], 16 * NT // 3)

            def e1(which):
                g, c_from, c_to = which
                for c in range(c_from, c_to):
                    x = KT * g + c
                    for b in (1, 2):
                        pool.wait_ge(s_ym, 3 * x + b + 1)
                        if b == 2:
                            pool.wait_ge(s_ya, 2 * x + 1)
                        pool.tensor_tensor(ya[:, c % 2], ya[:, c % 2], yb[:, b - 1], ALU.add).then_inc(s_ya, 1)

            def ot(g):
                for x in range(6):
                    half, t = divmod(x, 3)
                    pool.wait_ge(s_oe, 6 * g + x + 1)
                    tok = (3 * g + t) * P
                    cols = slice(512 * half, 512 * half + 512)
                    dst = y_sample[0, tok:tok + P, cols] if tok < LAT else y_prompt[0, :, cols]
                    pool.dma_start(dst, o_st[:, x % 2]).then_inc(s_ost[x % 2], 16)

            def pieces(stage, n):
                for i in range(n):
                    for kind, w in WITH.get(stage, ()):
                        for j in piece_range(kind, i, n):
                            if kind == "MX":
                                mx_load(KT * w + j)
                            elif kind == "SQ" and w in POOL_SQ:
                                sum_square(pool, w, j)

            for stage, w in ORDER:
                if stage == "E1":
                    e1(w)
                elif stage == "E2":
                    pieces((stage, w), w[2] - w[1])
                elif stage == "OT":
                    ot(w)
            pool.wait_ge(s_ost[0], 16 * 3 * NG)
            pool.wait_ge(s_ost[1], 16 * 3 * NG)


def _tiles(w, cols=P):
    k, n = w.shape
    u = np.ascontiguousarray(w.reshape(k // P, P, n // cols, cols).transpose(2, 1, 0, 3)).reshape(n // cols, P, k // P * cols)
    return u


def kernel(**inputs):
    import concourse.bacc as _bacc
    from concourse.bass_utils import run_bass_kernel_spmd as _run

    a = {k: np.asarray(v) for k, v in inputs.items()}
    w_in = a["w_in"][0]
    w_proj = np.concatenate([a["w_proj_f"][0], a["w_proj_p"][0], a["w_proj_m"][0]])
    w_ada = a["w_ada"][0].reshape(ADA_G, D // ADA_W, P, 6 * D // ADA_W, ADA_W).transpose(3, 0, 2, 1, 4).reshape(-1, P, D)
    ffn_in = _tiles(a["w_ffn_in"][0])
    ffn_in = np.stack([ffn_in[:FT], ffn_in[FT:]], axis=1).reshape(2 * FT, P, D)
    ffn_out = np.concatenate([
        _tiles(a["w_ffn_out"][0][sum(FO_K[:i]) * P:sum(FO_K[:i + 1]) * P]) if n == 8 else
        np.concatenate([_tiles(a["w_ffn_out"][0][sum(FO_K[:i]) * P:sum(FO_K[:i + 1]) * P]),
                        np.zeros((KT, P, D - n * P), np.float32)], axis=2)
        for i, n in enumerate(FO_K)])
    ffn_out = ffn_out.reshape(3, KT, P, D).transpose(1, 0, 2, 3).reshape(3 * KT, P, D)
    w_stream = np.concatenate([
        _tiles(w_in[:, :O_COL]), _tiles(w_in[:, GATE_COL:GATE_COL + P]), _tiles(w_in[:, O_COL:GATE_COL]),
        _tiles(w_in[:, MERGE_COL:]), _tiles(w_proj), _tiles(a["w_out"][0]), ffn_in, ffn_out])
    vectors = np.concatenate([a["c"].reshape(-1, P), a["c_ctx"].reshape(-1, P), a["b_ada"].reshape(-1, P),
                              a["norm_g"].reshape(-1, P), a["pool_scale"].reshape(-1, P)])
    base, cst, dft = shape_constants()
    ins = {"x_prompt": a["x_prompt"], "x_sample": a["x_sample"], "state_C": a["state_C"], "state_n": a["state_n"],
           "state_m": a["state_m"], "vectors": vectors, "w_ada": w_ada, "w_stream": w_stream,
           "b_gate": a["b_gate"], "w_pool": a["w_pool"], "k_base": base, "k_cst": cst, "k_dft": dft}
    outs = [("y_prompt", (1, CTX, D)), ("y_sample", (1, LAT, D)), ("new_C", (1, 1, 2, H, DH, DH)),
            ("new_n", (1, 1, 2, H, DH)), ("new_m", (1, 1, 2, H))]
    nc = _bacc.Bacc("TRN2", target_bir_lowering=False, num_devices=1)
    arrays, args = {}, {}
    for name, v in ins.items():
        arrays[f"in_{name}"] = np.ascontiguousarray(v)
        args[name] = nc.dram_tensor(f"in_{name}", v.shape, F32, kind="ExternalInput").ap()
    for name, shape in outs:
        args[name] = nc.dram_tensor(f"out_{name}", shape, F32, kind="ExternalOutput").ap()
    build(nc, **args)
    r = _run(nc, [arrays], core_ids=[0])
    return tuple(r.results[0][f"out_{name}"] for name, _ in outs)
```
